# Optimizing a Trainium2 kernel written in Bass

```python
import functools
import jax, jax.numpy as jnp
from jax import lax
import numpy as np

D_MODEL = 1024
BATCH = 1
SEQ = 2048
DEPTH = 1
DEC_BATCH = 1
DEC_SEQ = 32
PAST_LEN = 4096

CHUNK = 64
Q_BLOCK = 2 * CHUNK
HEAD_DIM = 64
D_R = D_MODEL // 2
D_F = D_MODEL - D_R
D_MIX = D_R + D_F
RWKV_HEADS = D_R // HEAD_DIM
FOX_HEADS = D_F // HEAD_DIM
DECAY_LORA = 64
A_LORA = 64
G_LORA = 128
RWKV_COLS = 3 * D_R + DECAY_LORA + A_LORA + G_LORA
FOX_COLS = 3 * D_F + FOX_HEADS + D_F
IN_COLS = RWKV_COLS + FOX_COLS
SHIFT = 2
N_EXPERTS = 32
N_GROUPS = 4
EXPERTS_PER_GROUP = N_EXPERTS // N_GROUPS
TOP_K = 2
D_EXPERT = D_MODEL // 2
MOE_BLOCK = 128
ALPHA = (2 * DEPTH) ** 0.25
BETA = (8 * DEPTH) ** -0.25
FORGET_BIAS = 3.0
LN_EPS = 1e-5
GN_EPS = 64e-5
QK_EPS = 1e-6
SCALE = HEAD_DIM ** -0.5

kernel_name = 'hybrid_rwkv7_fox_grouped_moe_stream_step'

def layer_norm(x, g, b):
    xf = x.astype(jnp.float32)
    mu = xf.mean(-1, keepdims=True)
    var = jnp.square(xf - mu).mean(-1, keepdims=True)
    return ((xf - mu) * lax.rsqrt(var + LN_EPS) * g.astype(jnp.float32) + b.astype(jnp.float32)).astype(x.dtype)

def rms_norm(x, g):
    xf = x.astype(jnp.float32)
    return (xf * lax.rsqrt(jnp.mean(xf * xf, -1, keepdims=True) + QK_EPS) * g.astype(jnp.float32)).astype(x.dtype)

def rwkv_scan(S0, r, w, k, v, kk, a):
    def step(S, inp):
        r_t, w_t, k_t, v_t, kk_t, a_t = inp
        sa = jnp.einsum('bhvk,bhk->bhv', S, -kk_t)
        S = (S * w_t[:, :, None, :] + sa[..., None] * (kk_t * a_t)[:, :, None, :]
             + v_t[..., None] * k_t[:, :, None, :])
        return S, jnp.einsum('bhvk,bhk->bhv', S, r_t)
    xs = tuple(jnp.swapaxes(t, 0, 1) for t in (r, w, k, v, kk, a))
    S, y = lax.scan(step, S0.astype(jnp.float32), xs)
    return S, jnp.swapaxes(y, 0, 1)

def rwkv_mixer(pr, shift_prev, S0, mu, w0, w2, a0, a2, g2, k_k, k_a, r_k, lnx_w, lnx_b):
    B, T, _ = pr.shape
    f32 = jnp.float32
    prev = jnp.concatenate([shift_prev.astype(pr.dtype), pr[:, :-1]], axis=1)
    xs = pr + (prev - pr) * mu
    xr, xk, xv, xw, xa, xg = jnp.split(
        xs, [D_R, 2 * D_R, 3 * D_R, 3 * D_R + DECAY_LORA, 3 * D_R + DECAY_LORA + A_LORA], axis=-1)
    heads = lambda t: t.astype(f32).reshape(B, T, RWKV_HEADS, HEAD_DIM)
    w = -jax.nn.softplus(-(w0 + jnp.tanh(xw) @ w2).astype(f32)) - 0.5
    decay = jnp.exp(-jnp.exp(w))
    a = jax.nn.sigmoid((a0 + xa @ a2).astype(f32))
    g = jax.nn.sigmoid(xg) @ g2
    kk = heads(xk * k_k)
    kk = kk / jnp.maximum(jnp.linalg.norm(kk, axis=-1, keepdims=True), 1e-12)
    k = xk.astype(f32) * (1.0 + (a - 1.0) * k_a.astype(f32))
    r, k, v, decay, a = heads(xr), heads(k), heads(xv), heads(decay), heads(a)
    S, y = rwkv_scan(S0, r, decay, k, v, kk, a)
    mean = y.mean(-1, keepdims=True)
    var = jnp.square(y - mean).mean(-1, keepdims=True)
    y = ((y - mean) * lax.rsqrt(var + GN_EPS)).reshape(B, T, D_R) * lnx_w.astype(f32) + lnx_b.astype(f32)
    bonus = jnp.sum(r * k * r_k.astype(f32), -1, keepdims=True) * v
    y = (y + bonus.reshape(B, T, D_R)) * g.astype(f32)
    return y.astype(pr.dtype), S, pr[:, -1:]

def fox_project(pf, b_f, q_g, k_g):
    B, T, _ = pf.shape
    q, k, v, fl, og = jnp.split(pf, [D_F, 2 * D_F, 3 * D_F, 3 * D_F + FOX_HEADS], axis=-1)
    hd = lambda t: t.reshape(B, T, FOX_HEADS, HEAD_DIM)
    logf = jax.nn.log_sigmoid((fl + b_f).astype(jnp.float32))
    return rms_norm(hd(q), q_g), rms_norm(hd(k), k_g), hd(v), logf, og

def fox_prompt_attention(q, k, v, logf):
    B, T, H, Dh = q.shape
    nb = T // Q_BLOCK
    c = jnp.swapaxes(jnp.cumsum(logf, axis=1), 1, 2)
    qb = jnp.moveaxis(q.reshape(B, nb, Q_BLOCK, H, Dh), 1, 0)
    cb = jnp.moveaxis(c.reshape(B, H, nb, Q_BLOCK), 2, 0)
    key_pos = jnp.arange(T)

    def block(args):
        q_i, c_i, i = args
        s = (jnp.einsum('bqhd,bkhd->bhqk', q_i, k).astype(jnp.float32) * SCALE
             + c_i[..., :, None] - c[..., None, :])
        q_pos = i * Q_BLOCK + jnp.arange(Q_BLOCK)
        s = jnp.where(key_pos[None, :] <= q_pos[:, None], s, -jnp.inf)
        p = jax.nn.softmax(s, axis=-1).astype(v.dtype)
        return jnp.einsum('bhqk,bkhd->bqhd', p, v)

    o = lax.map(block, (qb, cb, jnp.arange(nb)))
    return jnp.moveaxis(o, 0, 1).reshape(B, T, H, Dh)

def fox_sample_attention(q, k, v, logf, k_past, v_past, logf_past):
    f32 = jnp.float32
    P = k_past.shape[1]
    n = q.shape[1]
    c_new = jnp.swapaxes(jnp.cumsum(logf, axis=1), 1, 2)
    lp = logf_past.astype(f32)
    tail = jnp.swapaxes(lax.cumsum(lp, axis=1, reverse=True) - lp, 1, 2)
    s_past = (jnp.einsum('bqhd,bkhd->bhqk', q, k_past.astype(q.dtype)).astype(f32) * SCALE
              + c_new[..., :, None] + tail[..., None, :])
    s_new = (jnp.einsum('bqhd,bkhd->bhqk', q, k).astype(f32) * SCALE
             + c_new[..., :, None] - c_new[..., None, :])
    s_new = jnp.where(jnp.tril(jnp.ones((n, n), bool)), s_new, -jnp.inf)
    p = jax.nn.softmax(jnp.concatenate([s_past, s_new], axis=-1), axis=-1).astype(v.dtype)
    return (jnp.einsum('bhqk,bkhd->bqhd', p[..., :P], v_past.astype(v.dtype))
            + jnp.einsum('bhqk,bkhd->bqhd', p[..., P:], v))

def grouped_moe(h, router_w, router_b, w1, w3, w2):
    B, T, D = h.shape
    n = B * T
    hf = h.reshape(n, D)
    scores = jax.nn.sigmoid((hf @ router_w).astype(jnp.float32))
    sel = (scores + router_b.astype(jnp.float32)).reshape(n, N_GROUPS, EXPERTS_PER_GROUP)
    g_idx = jnp.argmax(lax.top_k(sel, 2)[0].sum(-1), axis=-1)
    in_group = sel[jnp.arange(n), g_idx]
    eidx = g_idx[:, None] * EXPERTS_PER_GROUP + lax.top_k(in_group, TOP_K)[1]
    gate = jnp.take_along_axis(scores, eidx, axis=1)
    gate = (gate / gate.sum(-1, keepdims=True)).astype(h.dtype)
    A = n * TOP_K
    flat_e = eidx.reshape(A)
    flat_tok = jnp.repeat(jnp.arange(n, dtype=jnp.int32), TOP_K)
    order = jnp.argsort(flat_e)
    se = flat_e[order]
    counts = jnp.bincount(flat_e, length=N_EXPERTS)
    starts = jnp.cumsum(counts) - counts
    padded = (counts + MOE_BLOCK - 1) // MOE_BLOCK * MOE_BLOCK
    pends = jnp.cumsum(padded)
    dest = (pends - padded)[se] + jnp.arange(A) - starts[se]
    nb = -(-A // MOE_BLOCK) + N_EXPERTS
    rows = nb * MOE_BLOCK
    tok_pad = jnp.full((rows,), n, jnp.int32).at[dest].set(flat_tok[order])
    gate_pad = jnp.zeros((rows,), h.dtype).at[dest].set(gate.reshape(A)[order])
    block_expert = jnp.clip(jnp.searchsorted(pends, jnp.arange(nb) * MOE_BLOCK, side='right'), 0, N_EXPERTS - 1)
    h_pad = jnp.concatenate([hf, jnp.zeros((1, D), h.dtype)], axis=0)[tok_pad].reshape(nb, MOE_BLOCK, D)

    def expert_block(args):
        hb, e = args
        return (jax.nn.silu(hb @ w1[e]) * (hb @ w3[e])) @ w2[e]

    y_pad = lax.map(expert_block, (h_pad, block_expert)).reshape(rows, D) * gate_pad[:, None]
    out = jnp.zeros((n + 1, D), h.dtype).at[tok_pad].add(y_pad)[:n]
    return out.reshape(B, T, D)

def trunk_layer(x, shift_prev, rwkv_state, attend, lp, router_w, router_b):
    B, T, _ = x.shape
    p = x @ lp['w_in']
    ry, rwkv_state, shift = rwkv_mixer(p[..., :RWKV_COLS], shift_prev, rwkv_state, lp['mu'], lp['w0'],
                                       lp['w2'], lp['a0'], lp['a2'], lp['g2'], lp['k_k'], lp['k_a'],
                                       lp['r_k'], lp['lnx_w'], lp['lnx_b'])
    q, k, v, logf, og = fox_project(p[..., RWKV_COLS:], lp['b_f'], lp['q_g'], lp['k_g'])
    fy = attend(q, k, v, logf).reshape(B, T, D_F) * jax.nn.sigmoid(og)
    m = jnp.concatenate([ry, fy.astype(ry.dtype)], axis=-1) @ lp['w_out']
    x = layer_norm(ALPHA * x + m, lp['ln1_g'], lp['ln1_b'])
    x = layer_norm(ALPHA * x + grouped_moe(x, router_w, router_b, lp['e_w1'], lp['e_w3'], lp['e_w2']),
                   lp['ln2_g'], lp['ln2_b'])
    return x, k, v, logf, rwkv_state, shift

def setup_inputs(seed: int = 0) -> dict:
    key = jax.random.key(seed)
    ks = iter(jax.random.split(key, 40))
    nrm = lambda shape, s=1.0: s * jax.random.normal(next(ks), shape, jnp.float32)
    col_scale = (jnp.ones((IN_COLS,), jnp.float32).at[2 * D_R:3 * D_R].set(BETA)
                 .at[RWKV_COLS + 2 * D_F:RWKV_COLS + 3 * D_F].set(BETA))
    return {
        'x_prompt': nrm((BATCH, SEQ, D_MODEL)),
        'x_sample': nrm((DEC_BATCH, DEC_SEQ, D_MODEL)),
        'cache_fox_k': nrm((DEPTH, DEC_BATCH, PAST_LEN, FOX_HEADS, HEAD_DIM)),
        'cache_fox_v': nrm((DEPTH, DEC_BATCH, PAST_LEN, FOX_HEADS, HEAD_DIM), BETA),
        'cache_fox_logf': jax.nn.log_sigmoid(FORGET_BIAS + nrm((DEPTH, DEC_BATCH, PAST_LEN, FOX_HEADS))),
        'state_rwkv': nrm((DEPTH, DEC_BATCH, RWKV_HEADS, HEAD_DIM, HEAD_DIM), 0.5),
        'state_rwkv_shift': nrm((DEPTH, DEC_BATCH, SHIFT - 1, RWKV_COLS)),
        'w_in': nrm((DEPTH, D_MODEL, IN_COLS), D_MODEL ** -0.5) * col_scale,
        'rwkv_mu': jax.random.uniform(next(ks), (DEPTH, RWKV_COLS), jnp.float32),
        'rwkv_w0': jax.random.uniform(next(ks), (DEPTH, D_R), jnp.float32, minval=-6.0, maxval=-1.0),
        'rwkv_w2': nrm((DEPTH, DECAY_LORA, D_R), 0.1),
        'rwkv_a0': nrm((DEPTH, D_R), 0.1),
        'rwkv_a2': nrm((DEPTH, A_LORA, D_R), 0.5 * A_LORA ** -0.5),
        'rwkv_g2': nrm((DEPTH, G_LORA, D_R), G_LORA ** -0.5),
        'rwkv_k_k': 0.85 + nrm((DEPTH, D_R), 0.05),
        'rwkv_k_a': 1.0 + nrm((DEPTH, D_R), 0.05),
        'rwkv_r_k': nrm((DEPTH, RWKV_HEADS, HEAD_DIM), 0.1),
        'rwkv_lnx_w': 1.0 + nrm((DEPTH, D_R), 0.05),
        'rwkv_lnx_b': nrm((DEPTH, D_R), 0.02),
        'fox_b_f': FORGET_BIAS + nrm((DEPTH, FOX_HEADS), 0.5),
        'fox_q_g': 1.0 + nrm((DEPTH, HEAD_DIM), 0.05),
        'fox_k_g': 1.0 + nrm((DEPTH, HEAD_DIM), 0.05),
        'w_out': nrm((DEPTH, D_MIX, D_MODEL), BETA * D_MIX ** -0.5),
        'ln1_g': 1.0 + nrm((DEPTH, D_MODEL), 0.05),
        'ln1_b': nrm((DEPTH, D_MODEL), 0.02),
        'ln2_g': 1.0 + nrm((DEPTH, D_MODEL), 0.05),
        'ln2_b': nrm((DEPTH, D_MODEL), 0.02),
        'router_w': nrm((D_MODEL, N_EXPERTS), D_MODEL ** -0.5),
        'router_b': nrm((N_EXPERTS,), 0.01),
        'moe_w1': nrm((DEPTH, N_EXPERTS, D_MODEL, D_EXPERT), BETA * D_MODEL ** -0.5),
        'moe_w3': nrm((DEPTH, N_EXPERTS, D_MODEL, D_EXPERT), BETA * D_MODEL ** -0.5),
        'moe_w2': nrm((DEPTH, N_EXPERTS, D_EXPERT, D_MODEL), BETA * D_EXPERT ** -0.5),
    }

def reference(x_prompt, x_sample, cache_fox_k, cache_fox_v, cache_fox_logf, state_rwkv, state_rwkv_shift,
              w_in, rwkv_mu, rwkv_w0, rwkv_w2, rwkv_a0, rwkv_a2, rwkv_g2, rwkv_k_k, rwkv_k_a, rwkv_r_k,
              rwkv_lnx_w, rwkv_lnx_b, fox_b_f, fox_q_g, fox_k_g, w_out, ln1_g, ln1_b, ln2_g, ln2_b,
              router_w, router_b, moe_w1, moe_w3, moe_w2):
    xp, xs = x_prompt, x_sample
    nb_p = xp.shape[0]
    outs_p, outs_s = [], []
    for l in range(DEPTH):
        lp = dict(w_in=w_in[l], mu=rwkv_mu[l], w0=rwkv_w0[l], w2=rwkv_w2[l], a0=rwkv_a0[l], a2=rwkv_a2[l],
                  g2=rwkv_g2[l], k_k=rwkv_k_k[l], k_a=rwkv_k_a[l], r_k=rwkv_r_k[l], lnx_w=rwkv_lnx_w[l],
                  lnx_b=rwkv_lnx_b[l], b_f=fox_b_f[l], q_g=fox_q_g[l], k_g=fox_k_g[l], w_out=w_out[l],
                  ln1_g=ln1_g[l], ln1_b=ln1_b[l], ln2_g=ln2_g[l], ln2_b=ln2_b[l],
                  e_w1=moe_w1[l], e_w3=moe_w3[l], e_w2=moe_w2[l])
        xp, *st_p = trunk_layer(xp, jnp.zeros((nb_p, SHIFT - 1, RWKV_COLS), xp.dtype),
                                jnp.zeros((nb_p, RWKV_HEADS, HEAD_DIM, HEAD_DIM), jnp.float32),
                                fox_prompt_attention, lp, router_w, router_b)
        attend_s = functools.partial(fox_sample_attention, k_past=cache_fox_k[l], v_past=cache_fox_v[l],
                                     logf_past=cache_fox_logf[l])
        xs, *st_s = trunk_layer(xs, state_rwkv_shift[l], state_rwkv[l], attend_s, lp, router_w, router_b)
        outs_p.append(st_p)
        outs_s.append(st_s)
    stk = lambda outs, i: jnp.stack([o[i] for o in outs], axis=0)
    p_fox_k, p_fox_v, p_fox_logf = stk(outs_p, 0), stk(outs_p, 1), stk(outs_p, 2)
    p_rwkv, p_shift = stk(outs_p, 3), stk(outs_p, 4)
    s_fox_k, s_fox_v, s_fox_logf = stk(outs_s, 0), stk(outs_s, 1), stk(outs_s, 2)
    s_rwkv, s_shift = stk(outs_s, 3), stk(outs_s, 4)
    return (xp, xs, p_fox_k, p_fox_v, p_fox_logf, p_rwkv, p_shift, s_fox_k, s_fox_v, s_fox_logf, s_rwkv, s_shift)


_drawn_inputs = setup_inputs


def setup_inputs(seed=0):
    import zlib

    import numpy as np

    out = dict(_drawn_inputs(seed))
    spreads = {}
    factors = {'cache_fox_k': 4.044,
     'cache_fox_v': 3.86,
     'cache_fox_logf': 8.0,
     'rwkv_lnx_w': 4.129,
     'rwkv_lnx_b': 16.846,
     'fox_q_g': 8.0,
     'ln2_b': 2.805,
     'router_b': 2.74}
    for name, (base, spread) in spreads.items():
        noise = np.random.default_rng([zlib.crc32(name.encode()), seed]).standard_normal(out[name].shape)
        drawn = base * np.exp(spread * noise) if base else spread * noise
        out[name] = __import__('jax').numpy.asarray(drawn.astype(out[name].dtype))
    for name, factor in factors.items():
        out[name] = (out[name] * factor).astype(out[name].dtype)
    return out
```

```python
from contextlib import ExitStack

import concourse.bass as bass
from concourse import mybir

F32 = mybir.dt.float32
I32 = mybir.dt.int32
U32 = mybir.dt.uint32
ALU = mybir.AluOpType
ACT = mybir.ActivationFunctionType
AX_X = mybir.AxisListType.X

P = 128
D = 1024
KD = D // P
SEQ = 2048
NEW = 32
PAST = 4096
NT = SEQ // P
TILES = NT + 1
ROWS = TILES * P
HEADS = 8
DH = 64
DG = HEADS * DH
PAIRS = HEADS // 2
LORA = 64
RCOLS = 3 * DG + 2 * LORA + P
FCOLS = 3 * DG + HEADS + DG
RCH = RCOLS // P
EXPERTS = 32
GROUPS = 4
PER_GROUP = EXPERTS // GROUPS
DE = D // 2
TOKENS = SEQ + NEW
BLOCKS = -(-2 * TOKENS // P) + EXPERTS
ALPHA = 2.0 ** 0.25
LN_EPS = 1e-5
GN_EPS = 64e-5
QK_EPS = 1e-6
SCALE = DH ** -0.5
DECAY = 0.6065306597126334
FAR = -1e30


class Steps:

    def __init__(self, sem, names):
        self.sem, self.names, self.at = sem, names, 0
        assert len(set(names)) == len(names)

    def begin(self, eng):
        eng.nop().then_inc(self.sem, len(self.names))

    def done(self, name):
        assert self.names[self.at % len(self.names)] == name, (self.names[self.at % len(self.names)], name)
        self.at += 1
        return self.sem, 1

    def after(self, name, t):
        return self.sem, (t + 1) * len(self.names) + self.names.index(name) + 1


def hold(eng, sem):
    eng.sem_inc(sem, 1)


def over_tiles(eng, tile):
    with eng.Fori(0, NT // 2) as j:
        for slot in (0, 1):
            tile(2 * j + slot, slot, j)
    tile(NT, 0, NT // 2)
def constants(nc, ctx):
    keep = {}

    def sb(name, shape, dt=F32):
        keep[name] = ctx.enter_context(nc.sbuf_tensor(name, shape, dt))
        return keep[name]

    ready = ctx.enter_context(nc.semaphore("constants_ready"))
    keep["constants_ready"] = ready
    ident, ones, upto, before, after = (sb(n, [P, P]) for n in ("ident", "ones", "upto", "before", "after"))
    halves, causal = sb("halves", [P, P]), sb("causal", [P, P])
    sb("expert_id", [P, EXPERTS])
    sb("group_of", [P, EXPERTS])
    sb("expert", [P, TILES, 2])
    sb("gate", [P, TILES, 2])
    sb("rank", [P, TILES, 2])
    sb("counts", [P, EXPERTS])
    sb("row", [P, TILES, 2], I32)
    sb("block_expert", [1, BLOCKS], I32)
    ids = sb("ids", [P, 2, EXPERTS], I32)
    shapes = [
        (ident, 0.0, ALU.not_equal, -1, 1, 0, 1.0),
        (ones, 1.0, None, 0, 0, 0, 0.0),
        (upto, 1.0, ALU.is_ge, 1, -1, 0, 0.0),
        (before, 1.0, ALU.is_gt, 1, -1, 0, 0.0),
        (after, 1.0, ALU.is_gt, -1, 1, 0, 0.0),
        (causal, 0.0, ALU.is_ge, -1, 1, 0, FAR),
    ]
    n = [0]
    with nc.Block() as block:
        @block.gpsimd
        def _(pool):
            def step(ins):
                n[0] += 1
                ins.then_inc(ready, 1)
                return n[0]

            for out, back, op, col, row, base, fill in shapes:
                count = step(pool.memset(out[:, :], back))
                if op is not None:
                    pool.wait_ge(ready, count)
                    step(pool.affine_select(out=out[:, :], in_=out[:, :], compare_op=op, fill=fill, base=base,
                                            pattern=[[col, P]], channel_multiplier=row))
            step(pool.iota(ids[:, 0, :], pattern=[[1, EXPERTS]], base=0, channel_multiplier=0))
            count = step(pool.iota(ids[:, 1, :], pattern=[[1, GROUPS], [0, PER_GROUP]], base=0, channel_multiplier=0))
            pool.wait_ge(ready, count)
            step(pool.tensor_copy(keep["expert_id"][:, :], ids[:, 0, :]))
            step(pool.tensor_copy(keep["group_of"][:, :], ids[:, 1, :]))
            count = step(pool.memset(halves[:, :], 0.0))
            pool.wait_ge(ready, count)
            step(pool.memset(halves[0:DH, 0:DH], 1.0))
            step(pool.memset(halves[DH:P, DH:P], 1.0))
            pool.wait_ge(ready, n[0])
    keep["constants"] = n[0]
    return keep
def fox_projection(nc, io, keep):
    with ExitStack() as ctx:
        def sb(name, shape, dt=F32):
            return ctx.enter_context(nc.sbuf_tensor(name, shape, dt))

        def sem(name):
            return ctx.enter_context(nc.semaphore(name))

        psum = [ctx.enter_context(nc.psum_tensor(f"fp{b}", [P, 512], F32)) for b in range(8)]
        X, Q, K, V, G, S, T = psum[0:2], psum[2], psum[3], psum[4], psum[5], psum[6], psum[7]
        w = sb("f_w", [P, KD, FCOLS])
        x = sb("f_x", [P, 2, D])
        xT = sb("f_xT", [P, KD, P])
        bf = sb("f_bf", [P, HEADS])
        qg = sb("f_qg", [P, DH])
        kg = sb("f_kg", [P, DH])
        carry = sb("f_carry", [P, HEADS])
        fb = sb("f_fb", [P, 4, HEADS])
        qk = sb("f_qk", [P, 2, DG])
        sq = sb("f_sq", [P, 2, DG])
        ss = sb("f_ss", [P, 3, 2 * HEADS])
        qn = sb("f_qn", [P, DG])
        kn = sb("f_kn", [P, 2, DG])
        vn = sb("f_vn", [P, 2, DG])
        og = sb("f_og", [P, 2, DG])
        lf = sb("f_lf", [P, 2, HEADS])
        negc = sb("f_negc", [P, HEADS])
        qT = sb("f_qT", [P, 2, DG])
        kT = sb("f_kT", [P, 2, DG])
        cT = sb("f_cT", [HEADS, 2, P])

        weights_loaded = sem("f_weights_loaded")
        x_loaded = [sem(f"f_x_loaded{s}") for s in (0, 1)]
        stored = [sem(f"f_stored{s}") for s in (0, 1)]
        pool_ready = sem("f_pool_ready")
        carry_zeroed = sem("f_carry_zeroed")
        pe = Steps(sem("f_pe_steps"), ["xT0", "xT1", "f", "q", "k", "v", "g", "cum", "qT", "kT", "cT"])
        act = Steps(sem("f_act_steps"), ["xT0", "xT1", "e", "l", "q", "k", "v", "g", "rms", "qT"])
        dve = Steps(sem("f_dve_steps"), [
            "fb", "negabs", "logf", "negc", "carry", "sq0", "ss0", "sq1", "ss1", "mean", "rs",
            "q1", "q2", "k1", "k2", "kT", "cT"])
        STORES = 7

        block = ctx.enter_context(nc.Block())
        w_rows = io["w_in"][0].rearrange("(p k) n -> p k n", k=KD)

        @block.sync
        def _(sp):
            sp.dma_start(w[:, :, :], w_rows[:, :, RCOLS:]).then_inc(weights_loaded, 16)
            with nc.allow_non_contiguous_dma(reason="small rows for all partitions"):
                sp.dma_start(bf[:, :], io["fox_b_f"].broadcast_to([P, HEADS])).then_inc(weights_loaded, 16)
                sp.dma_start(qg[:, :], io["fox_q_g"].broadcast_to([P, DH])).then_inc(weights_loaded, 16)
                sp.dma_start(kg[:, :], io["fox_k_g"].broadcast_to([P, DH])).then_inc(weights_loaded, 16)

            def stores(t, slot, rows, dst_row, k_out, v_out, lf_out):
                sp.wait_ge(*act.after("qT", t))
                sp.wait_ge(*dve.after("cT", t))
                with nc.allow_non_contiguous_dma(reason="rows of 8 gates"):
                    sp.dma_start(lf_out, lf[0:rows, slot, :]).then_inc(stored[slot], 16)
                sp.dma_start(k_out, kn[0:rows, slot, :]).then_inc(stored[slot], 16)
                sp.dma_start(v_out, vn[0:rows, slot, :]).then_inc(stored[slot], 16)
                sp.dma_start(io["og"][bass.ds(dst_row, P), :], og[:, slot, :]).then_inc(stored[slot], 16)
                for kind, src in (("qT", qT), ("kT", kT)):
                    sp.dma_start(io[kind][:, :, bass.ds(dst_row, P)].rearrange("a p t -> p a t"),
                                 src[:, slot, :].rearrange("p (a t) -> p a t", a=PAIRS)).then_inc(stored[slot], 16)
                sp.dma_start(io["cT"][:, bass.ds(dst_row, P)], cT[:, slot, :]).then_inc(stored[slot], 16)

            def stores_of(t, slot):
                at = t * P
                stores(t, slot, P, at, io["p_k"][bass.ds(at, P), :], io["p_v"][bass.ds(at, P), :],
                       io["p_lf"][bass.ds(at, P), :])

            sp.dma_start(x[:, 0, :], io["x_prompt"][0, 0:P, :]).then_inc(x_loaded[0], 16)
            with sp.Fori(0, NT // 2 - 1) as j:
                for slot in (0, 1):
                    t = 2 * j + slot
                    sp.wait_ge(*pe.after("xT1", t - 1))
                    sp.dma_start(x[:, 1 - slot, :], io["x_prompt"][0, bass.ds((t + 1) * P, P), :]).then_inc(
                        x_loaded[1 - slot], 16)
                    stores_of(t, slot)
            t = NT - 2
            sp.wait_ge(*pe.after("xT1", t - 1))
            sp.dma_start(x[:, 1, :], io["x_prompt"][0, (t + 1) * P:(t + 2) * P, :]).then_inc(x_loaded[1], 16)
            stores_of(t, 0)
            sp.wait_ge(pool_ready, 1)
            sp.dma_start(x[0:NEW, 0, :], io["x_sample"][0]).then_inc(x_loaded[0], 16)
            stores_of(NT - 1, 1)
            stores(NT, 0, NEW, NT * P, io["s_k"], io["s_v"], io["s_lf"])
            sp.wait_ge(stored[0], 16 * STORES * (NT // 2 + 1))
            sp.wait_ge(stored[1], 16 * STORES * (NT // 2))

        @block.gpsimd
        def _(pool):
            pool.wait_ge(*pe.after("xT1", NT - 2))
            pool.memset(x[:, 0, :], 0.0).then_inc(pool_ready, 1)

        @block.tensor
        def _(eng):
            pe.begin(eng)
            eng.wait_ge(keep["constants_ready"], keep["constants"])
            eng.wait_ge(weights_loaded, 64)

            def tile(t, slot, j):
                eng.wait_ge(x_loaded[slot], 16 * (j + 1))
                for half in (0, 1):
                    eng.wait_ge(*act.after(f"xT{half}", t - 1))
                    for k in range(4):
                        c = half * 4 + k
                        mm = eng.transpose(X[half][:, k * P:(k + 1) * P], x[:, slot, c:D:KD], keep["ident"][:, :])
                    mm.then_inc(*pe.done(f"xT{half}"))
                eng.wait_ge(*act.after("xT1", t))
                for name, a, n, out, owner in (("f", 3 * DG, HEADS, S[:, 0:HEADS], (dve, "fb")),
                                               ("q", 0, DG, Q[:, :], (act, "q")),
                                               ("k", DG, DG, K[:, :], (act, "k")),
                                               ("v", 2 * DG, DG, V[:, :], (act, "v")),
                                               ("g", 3 * DG + HEADS, DG, G[:, :], (act, "g"))):
                    if name == "f":
                        eng.wait_ge(*dve.after("cT", t - 1))
                    else:
                        eng.wait_ge(*owner[0].after(owner[1], t - 1))
                    for k in range(KD):
                        mm = eng.matmul(out, xT[:, k, :], w[:, k, a:a + n], start=(k == 0), stop=(k == KD - 1))
                    mm.then_inc(*pe.done(name))
                eng.wait_ge(*dve.after("logf", t))
                eng.matmul(S[:, 8:16], keep["upto"][:, :], lf[:, slot, :], start=True, stop=True)
                eng.matmul(S[:, 16:24], keep["ones"][:, :], lf[:, slot, :], start=True, stop=True)\
                   .then_inc(*pe.done("cum"))
                eng.wait_ge(*dve.after("q2", t))
                eng.wait_ge(*dve.after("kT", t - 1))
                for a in range(PAIRS):
                    mm = eng.transpose(T[:, a * P:(a + 1) * P], qn[:, a * P:(a + 1) * P], keep["ident"][:, :])
                mm.then_inc(*pe.done("qT"))
                eng.wait_ge(*dve.after("k2", t))
                eng.wait_ge(*act.after("qT", t))
                for a in range(PAIRS):
                    mm = eng.transpose(T[:, a * P:(a + 1) * P], kn[:, slot, a * P:(a + 1) * P], keep["ident"][:, :])
                mm.then_inc(*pe.done("kT"))
                eng.wait_ge(*dve.after("negc", t))
                eng.transpose(S[0:HEADS, 128:128 + P], negc[:, :], keep["ident"][:, :]).then_inc(*pe.done("cT"))

            over_tiles(eng, tile)

        @block.scalar
        def _(eng):
            act.begin(eng)

            def tile(t, slot, j):
                for half in (0, 1):
                    eng.wait_ge(*pe.after(f"xT{half}", t))
                    eng.wait_ge(*pe.after("g", t - 1))
                    eng.copy(xT[:, half * 4:half * 4 + 4, :], X[half][:, :].rearrange("p (k t) -> p k t", k=4))\
                       .then_inc(*act.done(f"xT{half}"))
                eng.wait_ge(*dve.after("negabs", t))
                eng.activation(fb[:, 2, :], fb[:, 1, :], ACT.Exp).then_inc(*act.done("e"))
                eng.wait_ge(*act.after("e", t))
                eng.activation(fb[:, 3, :], fb[:, 2, :], ACT.Ln, bias=1.0).then_inc(*act.done("l"))
                for n, (name, bank) in enumerate((("q", Q), ("k", K))):
                    eng.wait_ge(*pe.after(name, t))
                    eng.wait_ge(*dve.after(f"{name}1", t - 1))
                    eng.copy(qk[:, n, :], bank[:, :]).then_inc(*act.done(name))
                eng.wait_ge(stored[slot], 16 * STORES * j)
                eng.wait_ge(*pe.after("v", t))
                eng.copy(vn[:, slot, :], V[:, :]).then_inc(*act.done("v"))
                eng.wait_ge(*pe.after("g", t))
                eng.activation(og[:, slot, :], G[:, :], ACT.Sigmoid).then_inc(*act.done("g"))
                eng.wait_ge(*dve.after("mean", t))
                eng.activation(ss[:, 1, :], ss[:, 0, :], ACT.Sqrt).then_inc(*act.done("rms"))
                eng.wait_ge(*pe.after("qT", t))
                eng.copy(qT[:, slot, :], T[:, :]).then_inc(*act.done("qT"))

            over_tiles(eng, tile)

        @block.vector
        def _(eng):
            dve.begin(eng)
            eng.memset(carry[:, :], 0.0).then_inc(carry_zeroed, 1)
            eng.wait_ge(carry_zeroed, 1)
            eng.wait_ge(weights_loaded, 64)
            eng.tensor_scalar(qg[:, :], qg[:, :], SCALE, None, ALU.mult).then_inc(carry_zeroed, 1)
            eng.wait_ge(carry_zeroed, 2)

            def tile(t, slot, j):
                eng.wait_ge(*pe.after("f", t))
                eng.tensor_tensor(fb[:, 0, :], S[:, 0:HEADS], bf[:, :], ALU.add).then_inc(*dve.done("fb"))
                eng.wait_ge(*dve.after("fb", t))
                eng.scalar_tensor_tensor(out=fb[:, 1, :], in0=fb[:, 0, :], scalar=-1.0, in1=fb[:, 0, :],
                                         op0=ALU.mult, op1=ALU.min)\
                   .then_inc(*dve.done("negabs"))
                eng.wait_ge(*act.after("l", t))
                eng.wait_ge(stored[slot], 16 * STORES * j)
                eng.scalar_tensor_tensor(out=lf[:, slot, :], in0=fb[:, 0, :], scalar=0.0, in1=fb[:, 3, :],
                                         op0=ALU.min, op1=ALU.subtract).then_inc(*dve.done("logf"))
                eng.wait_ge(*pe.after("cum", t))
                eng.wait_ge(*pe.after("cT", t - 1))
                eng.wait_ge(*dve.after("carry", t - 1))
                eng.scalar_tensor_tensor(out=negc[:, :], in0=S[:, 8:16], scalar=-1.0, in1=carry[:, :],
                                         op0=ALU.mult, op1=ALU.subtract).then_inc(*dve.done("negc"))
                eng.wait_ge(*dve.after("negc", t))
                eng.tensor_tensor(carry[:, :], S[:, 16:24], carry[:, :], ALU.add).then_inc(*dve.done("carry"))
                for n, name in enumerate("qk"):
                    eng.wait_ge(*act.after(name, t))
                    eng.tensor_tensor(sq[:, n, :], qk[:, n, :], qk[:, n, :], ALU.mult).then_inc(*dve.done(f"sq{n}"))
                    eng.wait_ge(*dve.after(f"sq{n}", t))
                    eng.tensor_reduce(ss[:, 0, n * HEADS:(n + 1) * HEADS],
                                      sq[:, n, :].rearrange("p (h d) -> p h d", d=DH), AX_X, ALU.add)\
                       .then_inc(*dve.done(f"ss{n}"))
                eng.wait_ge(*dve.after("ss1", t))
                eng.tensor_scalar(ss[:, 0, :], ss[:, 0, :], 1.0 / DH, QK_EPS, ALU.mult, ALU.add)\
                   .then_inc(*dve.done("mean"))
                eng.wait_ge(*act.after("rms", t))
                eng.reciprocal(ss[:, 2, :], ss[:, 1, :]).then_inc(*dve.done("rs"))
                eng.wait_ge(*dve.after("rs", t))
                eng.wait_ge(*pe.after("qT", t - 1))
                for n, (name, out, g) in enumerate((("q", qn[:, :], qg), ("k", kn[:, slot, :], kg))):
                    heads = out.rearrange("p (h d) -> p h d", d=DH)
                    rs = ss[:, 2, n * HEADS:(n + 1) * HEADS].unsqueeze(2).broadcast_to([P, HEADS, DH])
                    eng.tensor_tensor(heads, qk[:, n, :].rearrange("p (h d) -> p h d", d=DH), rs, ALU.mult)\
                       .then_inc(*dve.done(f"{name}1"))
                    eng.wait_ge(*dve.after(f"{name}1", t))
                    eng.tensor_tensor(heads, heads, g[:, :].unsqueeze(1).broadcast_to([P, HEADS, DH]), ALU.mult)\
                       .then_inc(*dve.done(f"{name}2"))
                eng.wait_ge(*pe.after("kT", t))
                eng.tensor_copy(kT[:, slot, :], T[:, :]).then_inc(*dve.done("kT"))
                eng.wait_ge(*pe.after("cT", t))
                eng.tensor_copy(cT[:, slot, :], S[0:HEADS, 128:128 + P]).then_inc(*dve.done("cT"))

            with eng.Fori(0, NT // 2) as j:
                for slot in (0, 1):
                    tile(2 * j + slot, slot, j)
            eng.wait_ge(*dve.after("carry", NT - 1))
            eng.memset(carry[:, :], 0.0).then_inc(carry_zeroed, 1)
            eng.wait_ge(carry_zeroed, 3)
            tile(NT, 0, NT // 2)
LEVELS = 7


def rwkv(nc, io, keep):
    with ExitStack() as ctx:
        def sb(name, shape, dt=F32):
            return ctx.enter_context(nc.sbuf_tensor(name, shape, dt))

        def sem(name):
            return ctx.enter_context(nc.semaphore(name))

        bank = [ctx.enter_context(nc.psum_tensor(f"rp{b}", [P, 512], F32)) for b in range(8)]
        w = sb("r_w", [P, KD, RCOLS])
        w2 = sb("r_w2", [P, DG])
        g2 = sb("r_g2", [P, DG])
        mu = sb("r_mu", [P, RCH])
        par = sb("r_par", [P, 7, PAIRS])
        one_ka = sb("r_one_ka", [P, PAIRS])
        x = sb("r_x", [P, 2, D])
        xT = sb("r_xT", [P, KD, P])
        pr = sb("r_pr", [P, RCH, P + 1])
        last = sb("r_last", [P, RCH])
        xs = sb("r_xs", [P, RCH, P])
        th = sb("r_th", [LORA, P])
        sg = sb("r_sg", [P, P])

        def quad(name, n=1):
            return sb(name, [P, PAIRS, n * P]) if n == 1 else sb(name, [P, PAIRS, n, P])

        ld, a, g, kk, sq, nrm, kf, beta = (quad("r_" + n) for n in ("ld", "a", "g", "kk", "sq", "nrm", "kf", "beta"))
        cum = sb("r_cum", [P, PAIRS, P + 1])
        e1 = sb("r_e1", [P, PAIRS, P + 1])
        e2, bt, kt, bv = (quad("r_" + n) for n in ("e2", "bt", "kt", "bv"))
        ar = quad("r_ar", 2)
        cm = sb("r_cm", [P, 3, PAIRS])
        vtok, btok, ktok = (quad("r_" + n) for n in ("vtok", "btok", "ktok"))
        mab = sb("r_mab", [P, 2, PAIRS, P])
        mrb = sb("r_mrb", [P, 2, PAIRS, P])
        mk = sb("r_mk", [P, 2, PAIRS, 2, P])
        X = sb("r_X", [P, 2, PAIRS, P])
        XT = sb("r_XT", [P, 2, PAIRS, P])
        t1 = sb("r_t1", [P, 2, PAIRS, P])
        rhs = sb("r_rhs", [P, 2, PAIRS, DH])
        sa = sb("r_sa", [P, 2, PAIRS, DH])
        st = sb("r_st", [P, PAIRS, DH])
        sbar = sb("r_sbar", [P, PAIRS, DH])
        y = quad("r_y")
        ysq = quad("r_ysq")
        ys = quad("r_ys")
        out = sb("r_out", [P, 2, PAIRS, P])
        io_st = sb("r_io_st", [DH, HEADS, DH])
        masks_f = sb("r_masks_f", [P, P])
        mask = sb("r_mask", [P, 2, LEVELS, P], I32)
        mask2 = sb("r_mask2", [P, 2, P])

        weights_loaded = sem("r_weights_loaded")
        x_loaded = [sem(f"r_x_loaded{s}") for s in (0, 1)]
        out_stored = [sem(f"r_out_stored{s}") for s in (0, 1)]
        masks_ready = sem("r_masks_ready")
        pad_zeroed = sem("r_pad_zeroed")
        prepared = sem("r_prepared")
        MASKS = 2 * LEVELS + 2
        cleared = sem("r_cleared")
        held = sem("r_held")
        state_pe, state_dve, state_dma = sem("r_state_pe"), sem("r_state_dve"), sem("r_state_dma")
        shift_dma = sem("r_shift_dma")

        uses = [("zw", 2, "act", "ld"), ("za", 3, "act", "a"), ("zg", 4, "act", "g"), ("ss", 5, "act", "nrm"),
                ("vT", 6, "act", "vT"), ("bs", 7, "dve", "bv"), ("bT", 6, "act", "bT"), ("kT", 7, "act", "kT"),
                ("mab0", 2, "dve", "x0_1"), ("mab1", 3, "dve", "x1_1"),
                ("mrb0", 4, "dve", "mrb0"), ("mrb1", 5, "dve", "mrb1"),
                ("mk00", 6, "dve", "mk00"), ("mk01", 7, "dve", "mk01"),
                ("t0_1", 2, "dve", "xT0_1"), ("t1_1", 3, "dve", "xT1_1"),
                ("mk10", 6, "dve", "mk10"), ("mk11", 7, "dve", "mk11")]
        for n in range(2, LEVELS + 1):
            uses += [(f"t0_{n}", 2, "act", f"t0_{n}"), (f"t1_{n}", 3, "act", f"t1_{n}")]
            for e in (0, 1):
                uses += [(f"ut{e}_{n}", 4 + e, "dve", f"xT{e}_{n}")]
                if n < LEVELS:
                    uses += [(f"u{e}_{n}", 6 + e, "dve", f"x{e}_{n}")]
        uses += [("rhs0", 2, "act", "rhs0"), ("rhs1", 3, "dve", "rhs1"), ("sa0", 4, "act", "sa0"),
                 ("sa1", 5, "dve", "sa1"), ("y0", 6, "act", "y0"), ("y1", 7, "act", "y1"), ("st", 2, "dve", "st1"),
                 ("mean", 3, "dve", "yc"), ("var", 4, "dve", "var")]
        pe = Steps(sem("r_pe_steps"), [u[0] for u in uses])
        act = Steps(sem("r_act_steps"), ["th", "sg", "ld", "a", "g", "nrm", "e1", "e2", "emid", "vT", "bT", "kT"]
                    + [f"t{e}_{n}" for n in range(2, LEVELS + 1) for e in (0, 1)]
                    + ["rhs0", "sa0", "y0", "y1", "std"])
        dve = Steps(sem("r_dve_steps"), [
            "head", "last", "diff", "mix", "xs", "kkr", "sq", "scan", "mid", "nmid", "nmax", "rn", "kk", "beta",
            "ka1", "ka2", "kf", "A", "R", "B", "K", "rk1", "rk2", "sbar", "bv"]
            + ["mab0", "x0_1", "mab1", "x1_1", "mrb0", "mrb1", "mk00", "mk01", "xT0_1", "xT1_1", "mk10", "mk11"]
            + [f"{k}{e}_{n}" for n in range(2, LEVELS + 1) for e in (0, 1) for k in ("xT", "x")
               if not (k == "x" and n == LEVELS)]
            + ["rhs1", "sa1", "st1", "st2", "yc", "ysq", "var", "rstd", "y1", "y2", "y3", "y4", "out"])
        pool = Steps(sem("r_pool_steps"), ["X", "XT"])
        ppe = Steps(sem("r_proj_pe_steps"), ["xT0", "xT1", "r", "k", "v", "l"])
        pact = Steps(sem("r_proj_act_steps"), ["xT0", "xT1", "r", "k", "v", "l"])
        engines = {"act": act, "dve": dve}

        def emptied(step, t):
            i = [u[0] for u in uses].index(step)
            b = uses[i][1]
            before = [u for u in uses[:i] if u[1] == b]
            u = before[-1] if before else [u for u in uses if u[1] == b][-1]
            return engines[u[2]].after(u[3], t if before else t - 1)

        def bank_of(step):
            return bank[[u[1] for u in uses if u[0] == step][0]]

        def four(b, n=P):
            return b[:, 0:PAIRS * n].rearrange("p (a t) -> p a t", a=PAIRS)

        def by_channel(ap):
            return ap.rearrange("o (c p) -> p (o c)", p=P)

        def over(ap, n=P):
            return ap.unsqueeze(2).broadcast_to([P, ap.shape[1], n])

        block = ctx.enter_context(nc.Block())

        @block.sync
        def _(sp):
            sp.dma_start(x[:, 0, :], io["x_prompt"][0, 0:P, :]).then_inc(x_loaded[0], 16)
            sp.dma_start(x[:, 1, :], io["x_prompt"][0, P:2 * P, :]).then_inc(x_loaded[1], 16)
            with nc.allow_non_contiguous_dma(reason="vectors of parameters, channels in rows"):
                loads = [(w[:, :, :], io["w_in"][0].rearrange("(p k) n -> p k n", k=KD)[:, :, 0:RCOLS]),
                         (w2[0:LORA, :], io["rwkv_w2"][0]), (w2[LORA:P, :], io["rwkv_a2"][0]),
                         (g2[:, :], io["rwkv_g2"][0]), (mu[:, :], by_channel(io["rwkv_mu"]))]
                for n, name in enumerate(("w0", "a0", "k_k", "k_a", "r_k", "lnx_w", "lnx_b")):
                    v = io["rwkv_" + name]
                    v = v.rearrange("o h d -> o (h d)") if name == "r_k" else v
                    loads.append((par[:, n, :], by_channel(v)))
                for dst, src in loads:
                    sp.dma_start(dst, src).then_inc(weights_loaded, 16)

            def store(t, slot):
                sp.wait_ge(*dve.after("out", t))
                sp.dma_start(io["ryT"][:, :, bass.ds(t * P, P)].rearrange("a p t -> p a t"), out[:, slot, :, :])\
                  .then_inc(out_stored[slot], 16)

            with sp.Fori(0, NT // 2 - 1) as j:
                for slot in (0, 1):
                    t = 2 * j + slot
                    sp.wait_ge(*ppe.after("xT1", t))
                    sp.dma_start(x[:, slot, :], io["x_prompt"][0, bass.ds((t + 2) * P, P), :])\
                      .then_inc(x_loaded[slot], 16)
                    store(t, slot)
            sp.wait_ge(pad_zeroed, 1)
            sp.dma_start(x[0:NEW, 0, :], io["x_sample"][0]).then_inc(x_loaded[0], 16)
            store(NT - 2, 0)
            with nc.allow_non_contiguous_dma(reason="one frame, channels in rows"):
                sp.wait_ge(*dve.after("last", NT - 1))
                sp.dma_start(by_channel(io["p_shift"]), last[:, :]).then_inc(shift_dma, 16)
                sp.wait_ge(shift_dma, 16)
                sp.dma_start(last[:, :], by_channel(io["state_rwkv_shift"][0, 0])).then_inc(shift_dma, 16)
                store(NT - 1, 1)
                sp.wait_ge(state_dve, 1)
                sp.dma_start(io["p_rwkv"].rearrange("h v k -> v h k"), io_st[:, :, :]).then_inc(state_dma, 16)
                sp.wait_ge(state_dma, 16)
                sp.dma_start(io_st[:, :, :], io["state_rwkv"][0, 0].rearrange("h v k -> v h k"))\
                  .then_inc(state_dma, 16)
                sp.wait_ge(*pact.after("l", NT))
                sp.dma_start(by_channel(io["s_shift"]), pr[:, :, NEW]).then_inc(shift_dma, 16)
                store(NT, 0)
                sp.wait_ge(state_dve, 3)
                sp.dma_start(io["s_rwkv"].rearrange("h v k -> v h k"), io_st[:, :, :]).then_inc(state_dma, 16)
            sp.wait_ge(shift_dma, 48)
            sp.wait_ge(state_dma, 48)
            sp.wait_ge(out_stored[0], 16 * (NT // 2 + 1))
            sp.wait_ge(out_stored[1], 16 * (NT // 2))

        @block.gpsimd
        def _(eng):
            pool.begin(eng)
            n = 0
            for turned in (0, 1):
                for level in range(LEVELS):
                    s = 1 << level
                    if n:
                        eng.wait_ge(prepared, n)
                    eng.memset(masks_f[:, :], 0.0).then_inc(masks_ready, 1)
                    eng.wait_ge(masks_ready, 5 * n + 1)
                    cols = masks_f[:, :].rearrange("p (b h i) -> p b h i", h=2, i=s)[:, :, turned, :]
                    nb = P // (2 * s)
                    eng.memset(cols, 1.0).then_inc(masks_ready, 1)
                    eng.wait_ge(masks_ready, 5 * n + 2)
                    low = 0 if turned else s
                    eng.affine_select(out=cols, in_=cols, compare_op=ALU.is_ge, fill=0.0, base=-low,
                                      pattern=[[-2 * s, nb], [0, s]], channel_multiplier=1).then_inc(masks_ready, 1)
                    eng.wait_ge(masks_ready, 5 * n + 3)
                    eng.affine_select(out=cols, in_=cols, compare_op=ALU.is_ge, fill=0.0, base=low + s - 1,
                                      pattern=[[2 * s, nb], [0, s]], channel_multiplier=-1).then_inc(masks_ready, 2)
                    n += 1

            def tile(t, slot, j):
                eng.wait_ge(*pe.after(f"ut1_{LEVELS}", t - 1))
                hold(eng, held)
                eng.tensor_copy(X[:, :, :, :].rearrange("p e a t -> p (e a) t"),
                                keep["ident"][:, :].unsqueeze(1).broadcast_to([P, HEADS, P]))\
                   .then_inc(*pool.done("X"))
                eng.wait_ge(*pe.after("sa1", t - 1))
                hold(eng, held)
                eng.tensor_copy(XT[:, :, :, :].rearrange("p e a t -> p (e a) t"),
                                keep["ident"][:, :].unsqueeze(1).broadcast_to([P, HEADS, P]))\
                   .then_inc(*pool.done("XT"))

            with eng.Fori(0, NT // 2 - 1) as j:
                for slot in (0, 1):
                    tile(2 * j + slot, slot, j)
            eng.wait_ge(*ppe.after("xT1", NT - 2))
            eng.memset(x[:, 0, :], 0.0).then_inc(pad_zeroed, 1)
            for t in (NT - 2, NT - 1, NT):
                tile(t, t % 2, t // 2)

        @block.tensor
        def _(eng):
            pe.begin(eng)
            ppe.begin(eng)
            eng.wait_ge(keep["constants_ready"], keep["constants"])
            eng.wait_ge(weights_loaded, 16 * 12)
            eng.wait_ge(prepared, MASKS)
            ident = keep["ident"][:, :]

            def project_x(u, slot, turn):
                eng.wait_ge(x_loaded[slot], 16 * (turn + 1))
                for half in (0, 1):
                    eng.wait_ge(*pact.after("vl"[half], u - 1))
                    for k in range(4):
                        mm = eng.transpose(bank[half][:, k * P:(k + 1) * P], x[:, slot, half * 4 + k:D:KD], ident)
                    mm.then_inc(*ppe.done(f"xT{half}"))

            def project(u, name):
                n = "rkvl".index(name)
                eng.wait_ge(*pact.after(("xT1", "xT1", "r", "k")[n], u))
                b = four(bank[n % 2])
                for f in range(4 if n < 3 else 2):
                    c = (4 * n + f) * P
                    for k in range(KD):
                        mm = eng.matmul(b[:, f, :], w[:, k, c:c + P], xT[:, k, :], start=(k == 0), stop=(k == KD - 1))
                mm.then_inc(*ppe.done(name))

            def half_of(e):
                return slice(e * DH, (e + 1) * DH)

            def tile(t, slot, j, following=True):
                def start(step):
                    eng.wait_ge(*emptied(step, t))
                    return bank_of(step)

                if following:
                    project_x(t + 1, 1 - slot, j + slot)
                    project(t + 1, "r")
                b = four(start("zw"))
                eng.wait_ge(*act.after("th", t))
                for p in range(PAIRS):
                    mm = eng.matmul(b[:, p, :], w2[0:LORA, p * P:(p + 1) * P], th[:, :], start=True, stop=True)
                mm.then_inc(*pe.done("zw"))
                b = four(start("za"))
                for p in range(PAIRS):
                    mm = eng.matmul(b[:, p, :], w2[LORA:P, p * P:(p + 1) * P], xs[LORA:P, 12, :], start=True, stop=True)
                mm.then_inc(*pe.done("za"))
                b = four(start("zg"))
                eng.wait_ge(*act.after("sg", t))
                for p in range(PAIRS):
                    mm = eng.matmul(b[:, p, :], g2[:, p * P:(p + 1) * P], sg[:, :], start=True, stop=True)
                mm.then_inc(*pe.done("zg"))
                if following:
                    project(t + 1, "k")
                b = start("ss")
                eng.wait_ge(*dve.after("sq", t))
                eng.matmul(b[:, :], keep["halves"][:, :], sq[:, :, :].rearrange("p a t -> p (a t)"), start=True, stop=True)\
                   .then_inc(*pe.done("ss"))
                if following:
                    project(t + 1, "v")
                b = start("vT")
                for p in range(PAIRS):
                    mm = eng.transpose(b[:, p * P:(p + 1) * P], xs[:, 8 + p, :], ident)
                mm.then_inc(*pe.done("vT"))
                if following:
                    project(t + 1, "l")
                b = start("bs")
                eng.wait_ge(*dve.after("rk2", t))
                eng.matmul(b[:, :], keep["halves"][:, :], sq[:, :, :].rearrange("p a t -> p (a t)"), start=True, stop=True)\
                   .then_inc(*pe.done("bs"))
                for name, src in (("bT", bt), ("kT", kt)):
                    b = start(name)
                    for p in range(PAIRS):
                        mm = eng.transpose(b[:, p * P:(p + 1) * P], src[:, p, :], ident)
                    mm.then_inc(*pe.done(name))
                for e in (0, 1):
                    h = half_of(e)
                    b = four(start(f"mab{e}"))
                    for p in range(PAIRS):
                        mm = eng.matmul(b[:, p, :], ar[h, p, 0, :], bt[h, p, :], start=True, stop=True)
                    mm.then_inc(*pe.done(f"mab{e}"))
                for e in (0, 1):
                    h = half_of(e)
                    b = four(start(f"mrb{e}"))
                    for p in range(PAIRS):
                        mm = eng.matmul(b[:, p, :], bt[h, p, :], ar[h, p, 1, :], start=True, stop=True)
                    mm.then_inc(*pe.done(f"mrb{e}"))

                def mk_products(e):
                    h = half_of(e)
                    for n in (0, 1):
                        b = start(f"mk{e}{n}")
                        for i in (0, 1):
                            p = 2 * n + i
                            mm = eng.matmul(b[:, i * 2 * P:(i + 1) * 2 * P], kt[h, p, :],
                                            ar[h, p, :, :].rearrange("p a t -> p (a t)"), start=True, stop=True)
                        mm.then_inc(*pe.done(f"mk{e}{n}"))

                mk_products(0)
                for e in (0, 1):
                    b = four(start(f"t{e}_1"))
                    eng.wait_ge(*dve.after(f"mab{e}", t))
                    for p in range(PAIRS):
                        mm = eng.matmul(b[:, p, :], mab[:, e, p, :], ident, start=True, stop=True)
                    mm.then_inc(*pe.done(f"t{e}_1"))
                mk_products(1)
                for n in range(2, LEVELS + 1):
                    for e in (0, 1):
                        b = four(start(f"t{e}_{n}"))
                        eng.wait_ge(*dve.after(f"xT{e}_{n - 1}", t))
                        for p in range(PAIRS):
                            mm = eng.matmul(b[:, p, :], mab[:, e, p, :], XT[:, e, p, :], start=True, stop=True)
                        mm.then_inc(*pe.done(f"t{e}_{n}"))
                    for e in (0, 1):
                        b = four(start(f"ut{e}_{n}"))
                        eng.wait_ge(*dve.after(f"x{e}_{n - 1}", t))
                        eng.wait_ge(*act.after(f"t{e}_{n}", t))
                        for p in range(PAIRS):
                            mm = eng.matmul(b[:, p, :], X[:, e, p, :], t1[:, e, p, :], start=True, stop=True)
                        mm.then_inc(*pe.done(f"ut{e}_{n}"))
                        if n < LEVELS:
                            b = four(start(f"u{e}_{n}"))
                            for p in range(PAIRS):
                                mm = eng.matmul(b[:, p, :], t1[:, e, p, :], X[:, e, p, :], start=True, stop=True)
                            mm.then_inc(*pe.done(f"u{e}_{n}"))
                for e in (0, 1):
                    h = half_of(e)
                    b = four(start(f"rhs{e}"), DH)
                    eng.wait_ge(*dve.after("sbar", t))
                    for p in range(PAIRS):
                        eng.matmul(b[:, p, :], ar[h, p, 0, :], sbar[h, p, :], start=True, stop=False)
                        mm = eng.matmul(b[:, p, :], mk[:, e, p, 0, :], vtok[:, p, h], start=False, stop=True)
                    mm.then_inc(*pe.done(f"rhs{e}"))
                for e in (0, 1):
                    b = four(start(f"sa{e}"), DH)
                    eng.wait_ge(*(act, dve)[e].after(f"rhs{e}", t))
                    eng.wait_ge(*dve.after(f"xT{e}_{LEVELS}", t))
                    for p in range(PAIRS):
                        mm = eng.matmul(b[:, p, :], XT[:, e, p, :], rhs[:, e, p, :], start=True, stop=True)
                    mm.then_inc(*pe.done(f"sa{e}"))
                for e in (0, 1):
                    h = half_of(e)
                    b = four(start(f"y{e}"))
                    eng.wait_ge(*(act, dve)[e].after(f"sa{e}", t))
                    for p in range(PAIRS):
                        eng.matmul(b[h, p, :], sa[:, e, p, :], mrb[:, e, p, :], start=True, stop=False)
                        eng.matmul(b[h, p, :], sbar[h, p, :], ar[h, p, 1, :], start=False, stop=False)
                        mm = eng.matmul(b[h, p, :], vtok[:, p, h], mk[:, e, p, 1, :], start=False, stop=True)
                    mm.then_inc(*pe.done(f"y{e}"))
                b = four(start("st"), DH)
                for e in (0, 1):
                    h = half_of(e)
                    for p in range(PAIRS):
                        eng.matmul(b[h, p, :], btok[:, p, h], sa[:, e, p, :], start=True, stop=False)
                        mm = eng.matmul(b[h, p, :], ktok[:, p, h], vtok[:, p, h], start=False, stop=True)
                mm.then_inc(*pe.done("st"))
                b = start("mean")
                eng.wait_ge(*act.after("y1", t))
                eng.matmul(b[:, :], keep["halves"][:, :], y[:, :, :].rearrange("p a t -> p (a t)"), start=True, stop=True)\
                   .then_inc(*pe.done("mean"))
                b = start("var")
                eng.wait_ge(*dve.after("ysq", t))
                eng.matmul(b[:, :], keep["halves"][:, :], ysq[:, :, :].rearrange("p a t -> p (a t)"), start=True, stop=True)\
                   .then_inc(*pe.done("var"))

            project_x(0, 0, 0)
            for name in "rkvl":
                project(0, name)
            with eng.Fori(0, NT // 2) as j:
                for slot in (0, 1):
                    tile(2 * j + slot, slot, j)

            def state_out():
                for p in range(PAIRS):
                    mm = eng.transpose(bank[5][0:DH, p * P:(p + 1) * P], st[:, p, :], ident)
                mm.then_inc(state_pe, 1)

            eng.wait_ge(*dve.after("st2", NT - 1))
            state_out()
            eng.wait_ge(state_dma, 32)
            for p in range(PAIRS):
                mm = eng.transpose(bank[6][:, p * DH:(p + 1) * DH],
                                   io_st[:, 2 * p:2 * p + 2, :].rearrange("v h k -> v (h k)"), ident[0:DH, 0:DH])
            mm.then_inc(state_pe, 1)
            eng.wait_ge(state_dve, 2)
            tile(NT, 0, NT // 2, following=False)
            eng.wait_ge(*dve.after("st2", NT))
            state_out()

        @block.scalar
        def _(eng):
            act.begin(eng)
            pact.begin(eng)

            def project_x(u):
                for half in (0, 1):
                    eng.wait_ge(*ppe.after(f"xT{half}", u))
                    eng.copy(xT[:, half * 4:half * 4 + 4, :], four(bank[half])).then_inc(*pact.done(f"xT{half}"))

            def project(u, name):
                n = "rkvl".index(name)
                eng.wait_ge(*ppe.after(name, u))
                eng.wait_ge(*dve.after("xs", u - 1))
                m = 4 if n < 3 else 2
                eng.copy(pr[:, 4 * n:4 * n + m, 1:P + 1], four(bank[n % 2])[:, 0:m, :]).then_inc(*pact.done(name))

            def tile(t, slot, j, following=True):
                if following:
                    project_x(t + 1)
                eng.wait_ge(*dve.after("xs", t))
                eng.wait_ge(*pe.after("zw", t - 1))
                eng.activation(th[:, :], xs[0:LORA, 12, :], ACT.Tanh).then_inc(*act.done("th"))
                eng.wait_ge(*pe.after("zg", t - 1))
                eng.activation(sg[:, :], xs[:, 13, :], ACT.Sigmoid).then_inc(*act.done("sg"))
                for name, dst, n, readers in (("ld", ld, 0, "scan"), ("a", a, 1, "ka1")):
                    eng.wait_ge(*pe.after({"ld": "zw", "a": "za"}[name], t))
                    eng.wait_ge(*dve.after(readers, t - 1))
                    for p in range(PAIRS):
                        ins = eng.activation(dst[:, p, :], four(bank_of({"ld": "zw", "a": "za"}[name]))[:, p, :],
                                             ACT.Sigmoid, bias=par[:, n, p:p + 1])
                    ins.then_inc(*act.done(name))
                eng.wait_ge(*pe.after("zg", t))
                eng.wait_ge(*dve.after("out", t - 1))
                eng.copy(g[:, :, :], four(bank_of("zg"))).then_inc(*act.done("g"))
                if following:
                    project(t + 1, "r")
                eng.wait_ge(*pe.after("ss", t))
                eng.wait_ge(*dve.after("rn", t - 1))
                eng.activation(nrm[:, :, :], four(bank_of("ss")), ACT.Sqrt).then_inc(*act.done("nrm"))
                if following:
                    project(t + 1, "k")
                eng.wait_ge(*dve.after("nmid", t))
                eng.wait_ge(*dve.after("st2", t - 1))
                for p in range(PAIRS):
                    ins = eng.activation(e1[:, p, :], cum[:, p, :], ACT.Exp, scale=-DECAY, bias=cm[:, 0, p:p + 1])
                ins.then_inc(*act.done("e1"))
                for p in range(PAIRS):
                    ins = eng.activation(e2[:, p, :], cum[:, p, 1:P + 1], ACT.Exp, scale=DECAY, bias=cm[:, 1, p:p + 1])
                ins.then_inc(*act.done("e2"))
                eng.activation(cm[:, 2, :], cm[:, 1, :], ACT.Exp).then_inc(*act.done("emid"))
                if following:
                    project(t + 1, "v")
                eng.wait_ge(*pe.after("vT", t))
                eng.wait_ge(*pe.after("st", t - 1))
                eng.copy(vtok[:, :, :], four(bank_of("vT"))).then_inc(*act.done("vT"))
                if following:
                    project(t + 1, "l")
                for name, dst in (("bT", btok), ("kT", ktok)):
                    eng.wait_ge(*pe.after(name, t))
                    eng.copy(dst[:, :, :], four(bank_of(name))).then_inc(*act.done(name))
                for n in range(2, LEVELS + 1):
                    for e in (0, 1):
                        eng.wait_ge(*pe.after(f"t{e}_{n}", t))
                        eng.wait_ge(*pe.after(f"u{e}_{n - 1}", t) if n > 2 else pe.after(f"ut{e}_{LEVELS}", t - 1))
                        eng.copy(t1[:, e, :, :], four(bank_of(f"t{e}_{n}"))).then_inc(*act.done(f"t{e}_{n}"))
                eng.wait_ge(*pe.after("rhs0", t))
                eng.copy(rhs[:, 0, :, :], four(bank_of("rhs0"), DH)).then_inc(*act.done("rhs0"))
                eng.wait_ge(*pe.after("sa0", t))
                eng.copy(sa[:, 0, :, :], four(bank_of("sa0"), DH)).then_inc(*act.done("sa0"))
                for e in (0, 1):
                    h = slice(e * DH, (e + 1) * DH)
                    eng.wait_ge(*pe.after(f"y{e}", t))
                    eng.wait_ge(*dve.after("yc", t - 1))
                    eng.copy(y[h, :, :], four(bank_of(f"y{e}"))[h, :, :]).then_inc(*act.done(f"y{e}"))
                eng.wait_ge(*dve.after("var", t))
                eng.activation(ysq[:, :, :], ys[:, :, :], ACT.Sqrt).then_inc(*act.done("std"))

            project_x(0)
            for name in "rkvl":
                project(0, name)
            with eng.Fori(0, NT // 2) as j:
                for slot in (0, 1):
                    tile(2 * j + slot, slot, j)
            tile(NT, 0, NT // 2, following=False)

        @block.vector
        def _(eng):
            n = 0
            for turned in (0, 1):
                for level in range(LEVELS):
                    eng.wait_ge(masks_ready, 5 * (n + 1))
                    eng.tensor_copy(mask[:, turned, level, :], masks_f[:, :]).then_inc(prepared, 1)
                    n += 1
            eng.wait_ge(keep["constants_ready"], keep["constants"])
            eng.tensor_copy(mask2[:, 0, :], keep["before"][:, :])
            eng.tensor_copy(mask2[:, 1, :], keep["upto"][:, :])
            eng.memset(cum[:, :, 0:1], 0.0)
            eng.memset(last[:, :], 0.0)
            eng.memset(st[:, :, :], 0.0)
            eng.wait_ge(weights_loaded, 16 * 12)
            eng.tensor_scalar(one_ka[:, :], par[:, 3, :], -1.0, 1.0, ALU.mult, ALU.add).then_inc(prepared, 2)
            eng.wait_ge(prepared, MASKS)
            dve.begin(eng)

            def chained(*step_t):
                eng.wait_ge(*dve.after(*step_t))

            def tt(name, out_, a_, b_, op, t):
                eng.tensor_tensor(out_, a_, b_, op).then_inc(*dve.done(name))

            def heads4(ap):
                return ap.unsqueeze(1).broadcast_to([P, PAIRS, P])

            def tile(t, slot, j, final=False):
                chained("last", t - 1)
                chained("xs", t - 1)
                if final:
                    eng.wait_ge(shift_dma, 32)
                eng.tensor_copy(pr[:, :, 0:1], last[:, :].unsqueeze(2)).then_inc(*dve.done("head"))
                chained("head", t)
                eng.wait_ge(*pact.after("l", t))
                eng.tensor_copy(last[:, :].unsqueeze(2), pr[:, :, P:P + 1]).then_inc(*dve.done("last"))
                eng.wait_ge(*pe.after("vT", t - 1))
                chained("bv", t - 1)
                tt("diff", xs[:, :, :], pr[:, :, 0:P], pr[:, :, 1:P + 1], ALU.subtract, t)
                chained("diff", t)
                tt("mix", xs[:, :, :], xs[:, :, :], over(mu[:, :]), ALU.mult, t)
                chained("mix", t)
                tt("xs", xs[:, :, :], xs[:, :, :], pr[:, :, 1:P + 1], ALU.add, t)
                chained("xs", t)
                xr, xk, xv = xs[:, 0:4, :], xs[:, 4:8, :], xs[:, 8:12, :]
                eng.wait_ge(*pe.after("bs", t - 1))
                tt("kkr", kk[:, :, :], xk, over(par[:, 2, :]), ALU.mult, t)
                chained("kkr", t)
                tt("sq", sq[:, :, :], kk[:, :, :], kk[:, :, :], ALU.mult, t)
                eng.wait_ge(*act.after("ld", t))
                if final:
                    eng.memset(ld[:, :, NEW:P], 0.0).then_inc(cleared, 1)
                    eng.wait_ge(cleared, 1)
                for p in range(PAIRS):
                    ins = eng.tensor_tensor_scan(out=cum[:, p, 1:P + 1], data0=keep["ones"][:, :], data1=ld[:, p, :],
                                                 initial=0.0, op0=ALU.mult, op1=ALU.add)
                ins.then_inc(*dve.done("scan"))
                chained("scan", t)
                eng.tensor_scalar(cm[:, 0, :], cum[:, :, DH], DECAY, None, ALU.mult).then_inc(*dve.done("mid"))
                eng.tensor_scalar(cm[:, 1, :], cum[:, :, DH], -DECAY, None, ALU.mult).then_inc(*dve.done("nmid"))
                eng.wait_ge(*act.after("nrm", t))
                eng.tensor_scalar(nrm[:, :, :], nrm[:, :, :], 1e-12, None, ALU.max).then_inc(*dve.done("nmax"))
                chained("nmax", t)
                eng.reciprocal(nrm[:, :, :], nrm[:, :, :]).then_inc(*dve.done("rn"))
                chained("rn", t)
                tt("kk", kk[:, :, :], kk[:, :, :], nrm[:, :, :], ALU.mult, t)
                chained("kk", t)
                eng.wait_ge(*act.after("a", t))
                tt("beta", beta[:, :, :], kk[:, :, :], a[:, :, :], ALU.mult, t)
                chained("beta", t)
                tt("ka1", kf[:, :, :], a[:, :, :], over(par[:, 3, :]), ALU.mult, t)
                chained("ka1", t)
                tt("ka2", kf[:, :, :], kf[:, :, :], over(one_ka[:, :]), ALU.add, t)
                chained("ka2", t)
                tt("kf", kf[:, :, :], kf[:, :, :], xk, ALU.mult, t)
                chained("kf", t)
                if final:
                    eng.memset(kf[:, :, NEW:P], 0.0).then_inc(cleared, 1)
                    eng.memset(beta[:, :, NEW:P], 0.0).then_inc(cleared, 1)
                    eng.wait_ge(cleared, 3)
                eng.wait_ge(*act.after("emid", t))
                eng.wait_ge(*pe.after("y1", t - 1))
                eng.scalar_tensor_tensor(out=ar[:, :, 0, :], in0=kk[:, :, :], scalar=-1.0, in1=e1[:, :, 0:P],
                                         op0=ALU.mult, op1=ALU.mult).then_inc(*dve.done("A"))
                tt("R", ar[:, :, 1, :], xr, e1[:, :, 1:P + 1], ALU.mult, t)
                tt("B", bt[:, :, :], beta[:, :, :], e2[:, :, :], ALU.mult, t)
                tt("K", kt[:, :, :], kf[:, :, :], e2[:, :, :], ALU.mult, t)
                eng.wait_ge(*pe.after("ss", t))
                tt("rk1", sq[:, :, :], xr, kf[:, :, :], ALU.mult, t)
                chained("rk1", t)
                tt("rk2", sq[:, :, :], sq[:, :, :], over(par[:, 4, :]), ALU.mult, t)
                if final:
                    eng.wait_ge(state_dve, 2)
                chained("st2", t - 1)
                tt("sbar", sbar[:, :, :], st[:, :, :], over(cm[:, 2, :], DH), ALU.mult, t)
                chained("out", t - 1)
                eng.wait_ge(*pe.after("bs", t))
                tt("bv", bv[:, :, :], four(bank_of("bs")), xv, ALU.mult, t)
                for e in (0, 1):
                    eng.wait_ge(*pe.after(f"mab{e}", t))
                    b = four(bank_of(f"mab{e}"))
                    eng.wait_ge(*pe.after(f"t{e}_{LEVELS}", t - 1))
                    tt(f"mab{e}", mab[:, e, :, :], b, heads4(keep["after"][:, :]), ALU.mult, t)
                    eng.wait_ge(*pool.after("X", t))
                    hold(eng, held)
                    eng.copy_predicated(X[:, e, :, :], heads4(mask[:, 0, 0, :]), b).then_inc(*dve.done(f"x{e}_1"))
                for e in (0, 1):
                    eng.wait_ge(*pe.after(f"mrb{e}", t))
                    tt(f"mrb{e}", mrb[:, e, :, :], four(bank_of(f"mrb{e}")), heads4(keep["upto"][:, :]), ALU.mult, t)

                def mk_masked(e):
                    for n in (0, 1):
                        eng.wait_ge(*pe.after(f"mk{e}{n}", t))
                        tt(f"mk{e}{n}", mk[:, e, 2 * n:2 * n + 2, :, :].rearrange("p a b t -> p a (b t)"),
                           bank_of(f"mk{e}{n}")[:, :].rearrange("p (a x) -> p a x", a=2),
                           mask2[:, :, :].rearrange("p b t -> p (b t)").unsqueeze(1).broadcast_to([P, 2, 2 * P]),
                           ALU.mult, t)

                mk_masked(0)
                eng.wait_ge(*pool.after("XT", t))
                for e in (0, 1):
                    eng.wait_ge(*pe.after(f"t{e}_1", t))
                    hold(eng, held)
                    eng.copy_predicated(XT[:, e, :, :], heads4(mask[:, 1, 0, :]), four(bank_of(f"t{e}_1")))\
                       .then_inc(*dve.done(f"xT{e}_1"))
                mk_masked(1)
                for n in range(2, LEVELS + 1):
                    for e in (0, 1):
                        eng.wait_ge(*pe.after(f"ut{e}_{n}", t))
                        hold(eng, held)
                        eng.copy_predicated(XT[:, e, :, :], heads4(mask[:, 1, n - 1, :]), four(bank_of(f"ut{e}_{n}")))\
                           .then_inc(*dve.done(f"xT{e}_{n}"))
                        if n < LEVELS:
                            eng.wait_ge(*pe.after(f"u{e}_{n}", t))
                            hold(eng, held)
                            eng.copy_predicated(X[:, e, :, :], heads4(mask[:, 0, n - 1, :]),
                                                four(bank_of(f"u{e}_{n}"))).then_inc(*dve.done(f"x{e}_{n}"))
                eng.wait_ge(*pe.after("rhs1", t))
                eng.tensor_copy(rhs[:, 1, :, :], four(bank_of("rhs1"), DH)).then_inc(*dve.done("rhs1"))
                eng.wait_ge(*pe.after("sa1", t))
                eng.tensor_copy(sa[:, 1, :, :], four(bank_of("sa1"), DH)).then_inc(*dve.done("sa1"))
                eng.wait_ge(*pe.after("st", t))
                tt("st1", st[:, :, :], four(bank_of("st"), DH), sbar[:, :, :], ALU.add, t)
                chained("st1", t)
                tt("st2", st[:, :, :], st[:, :, :], e1[:, :, P:P + 1].broadcast_to([P, PAIRS, DH]), ALU.mult, t)
                eng.wait_ge(*pe.after("mean", t))
                eng.scalar_tensor_tensor(out=y[:, :, :], in0=four(bank_of("mean")), scalar=-1.0 / DH, in1=y[:, :, :],
                                         op0=ALU.mult, op1=ALU.add).then_inc(*dve.done("yc"))
                chained("yc", t)
                tt("ysq", ysq[:, :, :], y[:, :, :], y[:, :, :], ALU.mult, t)
                eng.wait_ge(*pe.after("var", t))
                eng.tensor_scalar(ys[:, :, :], four(bank_of("var")), 1.0 / DH, GN_EPS, ALU.mult, ALU.add)\
                   .then_inc(*dve.done("var"))
                eng.wait_ge(*act.after("std", t))
                eng.reciprocal(ys[:, :, :], ysq[:, :, :]).then_inc(*dve.done("rstd"))
                chained("rstd", t)
                tt("y1", ys[:, :, :], ys[:, :, :], y[:, :, :], ALU.mult, t)
                chained("y1", t)
                tt("y2", ys[:, :, :], ys[:, :, :], over(par[:, 5, :]), ALU.mult, t)
                chained("y2", t)
                tt("y3", ys[:, :, :], ys[:, :, :], over(par[:, 6, :]), ALU.add, t)
                chained("y3", t)
                tt("y4", ys[:, :, :], ys[:, :, :], bv[:, :, :], ALU.add, t)
                chained("y4", t)
                eng.wait_ge(*act.after("g", t))
                eng.wait_ge(out_stored[slot], 16 * j)
                tt("out", out[:, slot, :, :], ys[:, :, :], g[:, :, :], ALU.mult, t)

            with eng.Fori(0, NT // 2) as j:
                for slot in (0, 1):
                    tile(2 * j + slot, slot, j)
            eng.wait_ge(state_pe, 1)
            eng.tensor_copy(io_st[:, :, :], bank[5][0:DH, :].rearrange("v (h k) -> v h k", h=HEADS))\
               .then_inc(state_dve, 1)
            eng.wait_ge(state_pe, 2)
            eng.tensor_copy(st[:, :, :], bank[6][:, 0:PAIRS * DH].rearrange("p (a v) -> p a v", a=PAIRS))\
               .then_inc(state_dve, 1)
            tile(NT, 0, NT // 2, final=True)
            eng.wait_ge(state_pe, 3)
            eng.tensor_copy(io_st[:, :, :], bank[5][0:DH, :].rearrange("v (h k) -> v h k", h=HEADS))\
               .then_inc(state_dve, 1)
def fox_prompt(nc, io, keep):
    with ExitStack() as ctx:
        def sb(name, shape, dt=F32):
            return ctx.enter_context(nc.sbuf_tensor(name, shape, dt))

        def sem(name):
            return ctx.enter_context(nc.semaphore(name))

        logits = ctx.enter_context(nc.psum_tensor("a_logits", [P, SEQ], F32))
        turned = [ctx.enter_context(nc.psum_tensor(f"a_turned{b}", [P, 512], F32)) for b in range(2)]
        o = [ctx.enter_context(nc.psum_tensor(f"a_o{b}", [P, 512], F32)) for b in range(2)]
        q = sb("a_q", [DH + 1, 2, SEQ])
        k = sb("a_k", [DH + 1, 2, SEQ])
        v = sb("a_v", [P, NT, DG])
        pr = sb("a_p", [P, 2, SEQ])
        pT = sb("a_pT", [P, 2, SEQ])
        nmax = sb("a_nmax", [P, 2])
        total = sb("a_total", [P, 2])
        inv = sb("a_inv", [P, 2])
        fy = keep["fy"]

        v_loaded = sem("a_v_loaded")
        qk_loaded = [sem(f"a_qk_loaded{s}") for s in (0, 1)]
        ones_set = sem("a_ones_set")
        quads = [-(-(t + 1) // 4) for t in range(NT)]
        all_quads = [(t, c) for t in range(NT) for c in range(quads[t])]
        owner = {tc: n % 2 for n, tc in enumerate(all_quads)}
        pe_names, dve_names, act_names = [], [], []
        for t in range(NT + 1):
            if t < NT:
                pe_names.append(f"s{t}")
                dve_names.append(f"max{t}")
                act_names.append(f"exp{t}")
            if t > 0:
                for c in range(quads[t - 1]):
                    pe_names.append(f"T{t - 1}_{c}")
                    (act_names if owner[t - 1, c] else dve_names).append(f"T{t - 1}_{c}")
                pe_names.append(f"o{t - 1}")
                dve_names += [f"inv{t - 1}", f"o{t - 1}"]
        pe = Steps(sem("a_pe_steps"), pe_names)
        act = Steps(sem("a_act_steps"), act_names)
        dve = Steps(sem("a_dve_steps"), dve_names)

        def emptied(n, h):
            if n >= 2:
                t, c = all_quads[n - 2]
                return (act if owner[t, c] else dve).after(f"T{t}_{c}", h)
            t, c = all_quads[n - 2]
            return (act if owner[t, c] else dve).after(f"T{t}_{c}", h - 1)

        block = ctx.enter_context(nc.Block())

        @block.sync
        def _(sp):
            sp.dma_start(v[:, :, :], io["p_v"].rearrange("(n p) c -> p n c", p=P)).then_inc(v_loaded, 16)
            with sp.Fori(0, PAIRS) as j:
                for e in (0, 1):
                    sp.wait_ge(*pe.after(f"s{NT - 1}", 2 * j + e - 1) if e else pe.after(f"s{NT - 1}", 2 * j - 1))
                    rows = slice(e * DH, (e + 1) * DH)
                    sp.dma_start(q[0:DH, e, :], io["qT"][bass.ds(j, 1), rows, 0:SEQ].rearrange("a p t -> p (a t)"))\
                      .then_inc(qk_loaded[e], 16)
                    sp.dma_start(k[0:DH, e, :], io["kT"][bass.ds(j, 1), rows, 0:SEQ].rearrange("a p t -> p (a t)"))\
                      .then_inc(qk_loaded[e], 16)
                    sp.dma_start(k[DH:DH + 1, e, :], io["cT"][bass.ds(2 * j + e, 1), 0:SEQ]).then_inc(qk_loaded[e], 16)

        @block.gpsimd
        def _(eng):
            eng.memset(q[DH:DH + 1, :, :], 1.0).then_inc(ones_set, 1)

        @block.tensor
        def _(eng):
            pe.begin(eng)
            eng.wait_ge(v_loaded, 16)
            eng.wait_ge(ones_set, 1)

            def head(h, e, j):
                eng.wait_ge(qk_loaded[e], 48 * (j + 1))

                def scores(t):
                    eng.wait_ge(*(act.after(f"exp{t - 1}", h) if t else act.after(f"exp{NT - 1}", h - 1)))
                    n = (t + 1) * P
                    for a in range(0, n, 512):
                        m = min(512, n - a)
                        last = a + m == n
                        mm = eng.matmul(logits[:, a:a + m], q[:, e, t * P:(t + 1) * P], k[:, e, a:a + m],
                                        start=True, stop=not last)
                    eng.matmul(logits[:, n - P:n], keep["ident"][:, :], keep["causal"][:, :], start=False, stop=True)\
                       .then_inc(*pe.done(f"s{t}"))

                def attend(t):
                    eng.wait_ge(*act.after(f"exp{t}", h))
                    for c in range(quads[t]):
                        n = all_quads.index((t, c))
                        eng.wait_ge(*emptied(n, h))
                        for i in range(min(4, t + 1 - 4 * c)):
                            mm = eng.transpose(turned[n % 2][:, i * P:(i + 1) * P],
                                               pr[:, t % 2, (4 * c + i) * P:(4 * c + i + 1) * P], keep["ident"][:, :])
                        mm.then_inc(*pe.done(f"T{t}_{c}"))
                    eng.wait_ge(*(dve.after(f"o{t - 2}", h) if t > 1 else dve.after(f"o{NT - 2 + t}", h - 1)))
                    for c in range(quads[t]):
                        eng.wait_ge(*(act if owner[t, c] else dve).after(f"T{t}_{c}", h))
                        for i in range(4 * c, min(4 * c + 4, t + 1)):
                            mm = eng.matmul(o[t % 2][:, 0:DH], pT[:, t % 2, i * P:(i + 1) * P],
                                            v[:, i, bass.ds(h * DH, DH)], start=(i == 0), stop=(i == t))
                    mm.then_inc(*pe.done(f"o{t}"))

                for t in range(NT + 1):
                    if t < NT:
                        scores(t)
                    if t > 0:
                        attend(t - 1)

            with eng.Fori(0, PAIRS) as j:
                for e in (0, 1):
                    head(2 * j + e, e, j)

        def empty_quad(eng, copy, t, c, h):
            n = min(4, t + 1 - 4 * c) * P
            eng.wait_ge(*pe.after(f"T{t}_{c}", h))
            eng.wait_ge(*(pe.after(f"o{t - 2}", h) if t > 1 else pe.after(f"o{NT - 2 + t}", h - 1)))
            return copy(pT[:, t % 2, 4 * c * P:4 * c * P + n], turned[all_quads.index((t, c)) % 2][:, 0:n])

        @block.scalar
        def _(eng):
            act.begin(eng)

            def head(h, e, j):
                for t in range(NT + 1):
                    if t < NT:
                        n = (t + 1) * P
                        eng.wait_ge(*dve.after(f"max{t}", h))
                        prev = (t - 2, h) if t > 1 else (NT - 2 + t, h - 1)
                        eng.wait_ge(*pe.after(f"o{prev[0]}", prev[1]))
                        eng.wait_ge(*dve.after(f"inv{prev[0]}", prev[1]))
                        eng.activation(pr[:, t % 2, 0:n], logits[:, 0:n], ACT.Exp, bias=nmax[:, t % 2:t % 2 + 1],
                                       accum_out=total[:, t % 2:t % 2 + 1]).then_inc(*act.done(f"exp{t}"))
                    if t > 0:
                        for c in range(quads[t - 1]):
                            if owner[t - 1, c]:
                                empty_quad(eng, eng.copy, t - 1, c, h).then_inc(*act.done(f"T{t - 1}_{c}"))

            with eng.Fori(0, PAIRS) as j:
                for e in (0, 1):
                    head(2 * j + e, e, j)

        @block.vector
        def _(eng):
            dve.begin(eng)

            def head(h, e, j):
                for t in range(NT + 1):
                    if t < NT:
                        n = (t + 1) * P
                        eng.wait_ge(*pe.after(f"s{t}", h))
                        prev = (t - 2, h) if t > 1 else (NT - 2 + t, h - 1)
                        eng.wait_ge(*act.after(f"exp{prev[0]}", prev[1]))
                        eng.tensor_reduce(nmax[:, t % 2:t % 2 + 1], logits[:, 0:n], AX_X, ALU.max, negate=True)\
                           .then_inc(*dve.done(f"max{t}"))
                    if t > 0:
                        u = t - 1
                        for c in range(quads[u]):
                            if not owner[u, c]:
                                empty_quad(eng, eng.tensor_copy, u, c, h).then_inc(*dve.done(f"T{u}_{c}"))
                        eng.wait_ge(*act.after(f"exp{u}", h))
                        eng.reciprocal(inv[:, u % 2:u % 2 + 1], total[:, u % 2:u % 2 + 1])\
                           .then_inc(*dve.done(f"inv{u}"))
                        eng.wait_ge(*pe.after(f"o{u}", h))
                        eng.wait_ge(*dve.after(f"inv{u}", h))
                        eng.tensor_scalar(fy[:, u, bass.ds(h * DH, DH)], o[u % 2][:, 0:DH], inv[:, u % 2:u % 2 + 1],
                                          None, ALU.mult).then_inc(*dve.done(f"o{u}"))

            with eng.Fori(0, PAIRS) as j:
                for e in (0, 1):
                    head(2 * j + e, e, j)


def fox_sample(nc, io, keep):
    CT = PAST // P
    KEYS = PAST + NEW
    HG = HEADS // 2
    with ExitStack() as ctx:
        def sb(name, shape, dt=F32):
            return ctx.enter_context(nc.sbuf_tensor(name, shape, dt))

        def sem(name):
            return ctx.enter_context(nc.semaphore(name))

        bank = [ctx.enter_context(nc.psum_tensor(f"sp{b}", [P, 512], F32)) for b in range(8)]
        q = sb("c_q", [P, PAIRS, NEW])
        qbd = sb("c_qbd", [P, PAIRS, P])
        knew = sb("c_knew", [P, PAIRS, NEW])
        negc = sb("c_negc", [HEADS, NEW])
        lf = sb("c_lf", [P, CT, HEADS])
        suffix = sb("c_suffix", [HEADS, CT, P])
        totals = sb("c_totals", [HEADS, CT])
        cum = sb("c_cum", [HEADS, CT + 1])
        pick = sb("c_pick", [HEADS, 2, P])
        spread = sb("c_spread", [NEW, P])
        kc = sb("c_kc", [P, 2, DG])
        kT = sb("c_kT", [P, 2, DG])
        v = sb("c_v", [P, CT + 1, DG])
        logit = sb("c_logit", [P, 2, KEYS])
        nmax = sb("c_nmax", [P, 2])
        total = sb("c_total", [P, 2])
        inv = sb("c_inv", [P, 2])
        pn = sb("c_pn", [P, 2, 2, P])
        pT = sb("c_pT", [P, 2, 2, P])
        zeros = sb("c_zeros", [P, NEW])

        small_loaded = sem("c_small_loaded")
        k_loaded = [sem(f"c_k_loaded{s}") for s in (0, 1)]
        v_loaded = sem("c_v_loaded")
        made = sem("c_made")
        ready = sem("c_ready")
        tails = sem("c_tails")
        kpe = Steps(sem("c_key_pe_steps"), ["T", "s"])
        kact = Steps(sem("c_key_act_steps"), ["T", "s"])
        final_pe = sem("c_final_pe")
        soft = sem("c_soft")
        exped = sem("c_exped")
        vpe = Steps(sem("c_val_pe_steps"), ["T", "o"])
        vdve = Steps(sem("c_val_dve_steps"), ["p0", "p1"])
        vact = Steps(sem("c_val_act_steps"), ["T"])

        block = ctx.enter_context(nc.Block())
        k_dram = io["cache_fox_k"][0, 0].rearrange("t h d -> t (h d)")
        v_dram = io["cache_fox_v"][0, 0].rearrange("t h d -> t (h d)")

        @block.sync
        def _(sp):
            at = NT * P
            with nc.allow_non_contiguous_dma(reason="32 queries, 8 gates"):
                sp.dma_start(q[:, :, :], io["qT"][:, :, at:at + NEW].rearrange("a p t -> p a t")).then_inc(small_loaded, 16)
                sp.dma_start(knew[:, :, :], io["kT"][:, :, at:at + NEW].rearrange("a p t -> p a t"))\
                  .then_inc(small_loaded, 16)
                sp.dma_start(negc[:, :], io["cT"][:, at:at + NEW]).then_inc(small_loaded, 16)
                sp.dma_start(lf[:, :, :], io["cache_fox_logf"][0, 0].rearrange("(n p) h -> p n h", p=P))\
                  .then_inc(small_loaded, 16)
            sp.dma_start(v[0:NEW, CT, :], io["s_v"]).then_inc(small_loaded, 16)
            with sp.Fori(0, CT // 2) as j:
                for s in (0, 1):
                    row = sp.snap(j * (-2 * P) + (CT - 1 - s) * P)
                    sp.wait_ge(*kpe.after("T", 2 * j + s - 1) if s else kpe.after("T", 2 * j - 1))
                    sp.dma_start(kc[:, s, :], k_dram[bass.ds(row, P), :]).then_inc(k_loaded[s], 16)
            sp.dma_start(v[:, 0:CT, :], v_dram.rearrange("(n p) c -> p n c", p=P)).then_inc(v_loaded, 16)

        @block.gpsimd
        def _(eng):
            eng.memset(qbd[:, :, :], 0.0).then_inc(made, 1)
            eng.memset(zeros[:, :], 0.0)
            eng.memset(cum[:, 0:1], 0.0)
            eng.memset(pick[:, :, :], 1.0)
            eng.memset(spread[:, :], 0.0).then_inc(made, 1)
            eng.wait_ge(made, 2)
            eng.affine_select(out=pick[:, :, :].rearrange("h g (a i) -> h g a i", i=NEW),
                              in_=pick[:, :, :].rearrange("h g (a i) -> h g a i", i=NEW),
                              compare_op=ALU.is_equal, fill=0.0, base=0,
                              pattern=[[-HG, 2], [-1, HG], [0, NEW]], channel_multiplier=1).then_inc(made, 1)
            eng.affine_select(out=spread[:, :].rearrange("t (a i) -> t a i", i=NEW),
                              in_=spread[:, :].rearrange("t (a i) -> t a i", i=NEW),
                              compare_op=ALU.not_equal, fill=1.0, base=0,
                              pattern=[[0, HG], [-1, NEW]], channel_multiplier=1).then_inc(made, 1)

        @block.tensor
        def _(eng):
            kpe.begin(eng)
            vpe.begin(eng)
            ident = keep["ident"][:, :]
            eng.wait_ge(small_loaded, 80)
            eng.wait_ge(made, 4)
            for n in range(CT):
                b = bank[n // 4 % 2]
                if n >= 8 and n % 4 == 0:
                    eng.wait_ge(tails, n // 4 - 1)
                mm = eng.matmul(b[0:HEADS, (n % 4) * P:(n % 4 + 1) * P], lf[:, CT - 1 - n, :], keep["after"][:, :],
                                start=True, stop=True)
                mm = eng.matmul(bank[2][0:HEADS, n:n + 1], lf[:, CT - 1 - n, :], keep["ones"][:, 0:1],
                                start=True, stop=True)
                if n % 4 == 3:
                    mm.then_inc(final_pe, 1)
            eng.wait_ge(ready, 1)

            def keys(n, s, j, past=True):
                slot_kT = kT[:, s, :] if past else None
                if past:
                    eng.wait_ge(k_loaded[s], 16 * (j + 1))
                    eng.wait_ge(*kact.after("T", n - 1))
                    for a in range(PAIRS):
                        mm = eng.transpose(bank[3][:, a * P:(a + 1) * P], kc[:, s, a * P:(a + 1) * P], ident)
                    mm.then_inc(*kpe.done("T"))
                    eng.wait_ge(*kact.after("T", n))
                    eng.wait_ge(*kact.after("s", n - 1))
                w = P if past else NEW
                for g in (0, 1):
                    out = bank[4][:, g * P:g * P + w]
                    for i in (0, 1):
                        a = 2 * g + i
                        rhs = kT[:, s, a * P:(a + 1) * P] if past else knew[:, a, :]
                        eng.matmul(out, qbd[:, a, :], rhs, start=(i == 0), stop=False)
                    if past:
                        mm = eng.matmul(out, pick[:, g, :], suffix[:, bass.ds(n, 1), :].rearrange("h o t -> h (o t)"),
                                        start=False, stop=True)
                    else:
                        eng.matmul(out, pick[:, g, :], negc[:, :], start=False, stop=False)
                        mm = eng.matmul(out, spread[:, :], keep["causal"][0:NEW, 0:NEW], start=False, stop=True)
                if past:
                    mm.then_inc(*kpe.done("s"))
                else:
                    mm.then_inc(final_pe, 1)

            with eng.Fori(0, CT // 2) as j:
                for s in (0, 1):
                    keys(2 * j + s, s, j)
            eng.wait_ge(*kact.after("s", CT - 1))
            keys(CT, 0, 0, past=False)

            eng.matmul(bank[5][0:NEW, :], zeros[0:NEW, :], v[0:NEW, CT, :], start=True, stop=False)
            eng.wait_ge(v_loaded, 16)

            def values(n, s, stop, w=P):
                tile = eng.snap(n * -1 + (CT - 1)) if w == P else None
                eng.wait_ge(*vact.after("T", n - 1))
                eng.wait_ge(*vdve.after("p1", n))
                for g in (0, 1):
                    mm = eng.transpose(bank[6][0:w, g * P:(g + 1) * P], pn[:, s, g, 0:w], ident)
                mm.then_inc(*vpe.done("T"))
                eng.wait_ge(*vact.after("T", n))
                for h in range(HEADS):
                    g, i = divmod(h, HG)
                    r = v[0:w, CT, h * DH:(h + 1) * DH] if w < P else v[:, bass.ds(tile, 1), h * DH:(h + 1) * DH]\
                        .rearrange("p o c -> p (o c)")
                    mm = eng.matmul(bank[5][0:NEW, h * DH:(h + 1) * DH], pT[0:w, s, g, i * NEW:(i + 1) * NEW], r,
                                    start=False, stop=stop and h == HEADS - 1)
                mm.then_inc(*vpe.done("o"))

            with eng.Fori(0, CT // 2) as j:
                for s in (0, 1):
                    values(2 * j + s, s, False)
            values(CT, 0, True, NEW)

        @block.scalar
        def _(eng):
            kact.begin(eng)
            vact.begin(eng)

            def keys(n, s, j):
                eng.wait_ge(*kpe.after("T", n))
                eng.wait_ge(*kpe.after("s", n - 1))
                eng.copy(kT[:, s, :], bank[3][:, :]).then_inc(*kact.done("T"))
                eng.wait_ge(*kpe.after("s", n))
                eng.copy(logit[:, :, bass.ds(n * P, P)], bank[4][:, 0:2 * P].rearrange("p (g t) -> p g t", g=2))\
                   .then_inc(*kact.done("s"))

            with eng.Fori(0, CT // 2) as j:
                for s in (0, 1):
                    keys(2 * j + s, s, j)
            eng.wait_ge(final_pe, CT // 4 + 1)
            eng.copy(logit[:, :, PAST:KEYS], bank[4][:, 0:2 * P].rearrange("p (g t) -> p g t", g=2)[:, :, 0:NEW])\
               .then_inc(exped, 1)
            for g in (0, 1):
                eng.wait_ge(soft, g + 1)
                eng.activation(logit[:, g, :], logit[:, g, :], ACT.Exp, bias=nmax[:, g:g + 1],
                               accum_out=total[:, g:g + 1]).then_inc(exped, 1)

            def values(n, s, w=P):
                eng.wait_ge(*vpe.after("T", n))
                eng.wait_ge(*vpe.after("o", n - 1))
                eng.copy(pT[0:w, s, :, :], bank[6][0:w, 0:2 * P].rearrange("p (g t) -> p g t", g=2))\
                   .then_inc(*vact.done("T"))

            with eng.Fori(0, CT // 2) as j:
                for s in (0, 1):
                    values(2 * j + s, s)
            values(CT, 0, NEW)

        @block.vector
        def _(eng):
            vdve.begin(eng)
            for c in range(CT // 4):
                eng.wait_ge(final_pe, c + 1)
                eng.tensor_copy(suffix[:, 4 * c:4 * c + 4, :],
                                bank[c % 2][0:HEADS, :].rearrange("h (n t) -> h n t", n=4)).then_inc(tails, 1)
            eng.tensor_copy(totals[:, :], bank[2][0:HEADS, 0:CT]).then_inc(tails, 1)
            eng.wait_ge(tails, CT // 4 + 1)
            eng.wait_ge(made, 4)
            eng.tensor_tensor_scan(out=cum[:, 1:CT + 1], data0=keep["ones"][0:HEADS, 0:CT], data1=totals[:, :],
                                   initial=0.0, op0=ALU.mult, op1=ALU.add).then_inc(tails, 1)
            eng.wait_ge(tails, CT // 4 + 2)
            eng.tensor_tensor(suffix[:, :, :], suffix[:, :, :], cum[:, 0:CT].unsqueeze(2).broadcast_to([HEADS, CT, P]),
                              ALU.add)
            eng.wait_ge(small_loaded, 80)
            for h in range(HEADS):
                a, e = divmod(h, 2)
                rows, i = slice(e * DH, (e + 1) * DH), h % HG
                ins = eng.tensor_copy(qbd[rows, a, i * NEW:(i + 1) * NEW], q[rows, a, :])
            ins.then_inc(ready, 1)
            eng.wait_ge(exped, 1)
            for g in (0, 1):
                eng.tensor_reduce(nmax[:, g:g + 1], logit[:, g, :], AX_X, ALU.max, negate=True).then_inc(soft, 1)
            eng.wait_ge(exped, 3)
            eng.reciprocal(inv[:, :], total[:, :]).then_inc(soft, 1)
            eng.wait_ge(soft, 3)

            def values(n, s, w=P):
                eng.wait_ge(*vpe.after("T", n - 1))
                for g in (0, 1):
                    eng.tensor_scalar(pn[:, s, g, 0:w], logit[:, g, bass.ds(n * P, w)], inv[:, g:g + 1], None, ALU.mult)\
                       .then_inc(*vdve.done(f"p{g}"))

            with eng.Fori(0, CT // 2) as j:
                for s in (0, 1):
                    values(2 * j + s, s)
            values(CT, 0, NEW)
            eng.wait_ge(*vpe.after("o", CT))
            eng.tensor_copy(keep["fy"][0:NEW, NT, :], bank[5][0:NEW, :])
def layer_norm_steps(eng, dve, held, act_after, z, stats, mv, std, out, gain, offset, pre, t):
    for half in (0, 1):
        ins = eng.bn_stats(stats[:, half, :], z[:, half * 512:(half + 1) * 512])
    ins.then_inc(*dve.done(pre + "stats"))
    eng.wait_ge(*dve.after(pre + "stats", t))
    hold(eng, held)
    eng.bn_aggr(mv[:, 0:2], stats[:, :, :].rearrange("p a b -> p (a b)")).then_inc(*dve.done(pre + "mv"))
    eng.wait_ge(*dve.after(pre + "mv", t))
    eng.tensor_scalar(mv[:, 2:3], mv[:, 1:2], 1.0, LN_EPS, ALU.mult, ALU.add).then_inc(*dve.done(pre + "eps"))
    eng.wait_ge(*act_after)
    eng.reciprocal(mv[:, 3:4], std).then_inc(*dve.done(pre + "rstd"))
    eng.wait_ge(*dve.after(pre + "rstd", t))
    eng.tensor_scalar(z, z, mv[:, 0:1], mv[:, 3:4], ALU.subtract, ALU.mult).then_inc(*dve.done(pre + "norm"))
    eng.wait_ge(*dve.after(pre + "norm", t))
    eng.tensor_tensor(z, z, gain, ALU.mult).then_inc(*dve.done(pre + "gain"))
    eng.wait_ge(*dve.after(pre + "gain", t))
    eng.tensor_tensor(out, z, offset, ALU.add).then_inc(*dve.done(pre + "out"))


def mix_and_route(nc, io, keep):
    with ExitStack() as ctx:
        def sb(name, shape, dt=F32):
            return ctx.enter_context(nc.sbuf_tensor(name, shape, dt))

        def sem(name):
            return ctx.enter_context(nc.semaphore(name))

        FT = ctx.enter_context(nc.psum_tensor("m_FT", [P, 512], F32))
        M = [ctx.enter_context(nc.psum_tensor(f"m_M{b}", [P, 512], F32)) for b in range(2)]
        HT = [ctx.enter_context(nc.psum_tensor(f"m_HT{b}", [P, 512], F32)) for b in range(2)]
        SC = ctx.enter_context(nc.psum_tensor("m_SC", [P, 512], F32))
        RK = ctx.enter_context(nc.psum_tensor("m_RK", [P, 512], F32))
        w = sb("m_w", [P, KD, D])
        rw = sb("m_rw", [P, KD, EXPERTS])
        rb = sb("m_rb", [P, EXPERTS])
        gain, offset = sb("m_gain", [P, D]), sb("m_offset", [P, D])
        x = sb("m_x", [P, 2, D])
        ry = sb("m_ry", [P, 2, PAIRS, P])
        og = sb("m_og", [P, 2, DG])
        f = sb("m_f", [P, DG])
        fT = sb("m_fT", [P, PAIRS, P])
        z = sb("m_z", [P, D])
        stats, mv, std = sb("m_stats", [P, 2, 6]), sb("m_mv", [P, 4]), sb("m_std", [P, 1])
        h = sb("m_h", [P, 2, D])
        hT = sb("m_hT", [P, KD, P])
        score, sel, selm, gm = (sb("m_" + n, [P, EXPERTS]) for n in ("score", "sel", "selm", "gm"))
        top = sb("m_top", [P, GROUPS, 8])
        gs, gbest, ebest = sb("m_gs", [P, 8]), sb("m_gbest", [P, 8]), sb("m_ebest", [P, 8])
        gidx, eidx = sb("m_gidx", [P, 8], U32), sb("m_eidx", [P, 8], U32)
        gid = sb("m_gid", [P, 1])
        pick = sb("m_pick", [P, 2, EXPERTS])
        prod = sb("m_prod", [P, 2, EXPERTS])
        both = sb("m_both", [P, EXPERTS])
        gsum = sb("m_gsum", [P, 2])
        graw = sb("m_graw", [P, 2])
        rank = sb("m_rank", [P, EXPERTS])

        weights_loaded = sem("m_weights_loaded")
        loaded = [sem(f"m_loaded{s}") for s in (0, 1)]
        stored = [sem(f"m_stored{s}") for s in (0, 1)]
        counts_zeroed, mixers_padded, rows_padded = sem("m_counts_zeroed"), sem("m_mixers_padded"), sem("m_rows_padded")
        held = sem("m_held")
        pe = Steps(sem("m_pe_steps"), ["fT", "m", "hT0", "hT1", "score", "rank"])
        act = Steps(sem("m_act_steps"), ["fT", "std", "hT0", "hT1", "score"])
        dve = Steps(sem("m_dve_steps"), ["f", "z0", "z1", "stats", "mv", "eps", "rstd", "norm", "gain", "out", "sel",
                                         "top", "gs", "gbest", "gidx", "gid", "gm", "pen", "selm1", "selm2", "ebest",
                                         "eidx", "eid", "pick0", "pick1", "both", "prod", "graw", "gsum", "ginv", "gate",
                                         "rank", "carry", "rprod", "rout"])
        block = ctx.enter_context(nc.Block())
        every = lambda ap, n: ap.unsqueeze(1).broadcast_to([P, n, ap.shape[1]])

        @block.sync
        def _(sp):
            sp.dma_start(w[:, :, :], io["w_out"][0].rearrange("(c p) n -> p c n", p=P)).then_inc(weights_loaded, 16)
            with nc.allow_non_contiguous_dma(reason="small rows for all partitions"):
                sp.dma_start(rw[:, :, :], io["router_w"].rearrange("(c p) n -> p c n", p=P)).then_inc(weights_loaded, 16)
                sp.dma_start(rb[:, :], io["router_b"].unsqueeze(0).broadcast_to([P, EXPERTS])).then_inc(weights_loaded, 16)
                sp.dma_start(gain[:, :], io["ln1_g"].broadcast_to([P, D])).then_inc(weights_loaded, 16)
                sp.dma_start(offset[:, :], io["ln1_b"].broadcast_to([P, D])).then_inc(weights_loaded, 16)

            def loads(t, slot, x_src, rows=P):
                sp.dma_start(ry[:, slot, :, :], io["ryT"][:, :, bass.ds(t * P, P)].rearrange("a p t -> p a t"))\
                  .then_inc(loaded[slot], 16)
                sp.dma_start(og[:, slot, :], io["og"][bass.ds(t * P, P), :]).then_inc(loaded[slot], 16)
                sp.dma_start(x[0:rows, slot, :], x_src).then_inc(loaded[slot], 16)

            def store(t, slot):
                sp.wait_ge(*dve.after("out", t))
                sp.dma_start(io["h"][bass.ds(t * P, P), :], h[:, slot, :]).then_inc(stored[slot], 16)

            for t in (0, 1):
                loads(t, t, io["x_prompt"][0, t * P:(t + 1) * P, :])
            with sp.Fori(0, NT // 2 - 1) as j:
                for slot in (0, 1):
                    t = 2 * j + slot
                    store(t, slot)
                    sp.wait_ge(*pe.after("m", t))
                    loads(t + 2, slot, io["x_prompt"][0, bass.ds((t + 2) * P, P), :])
            store(NT - 2, 0)
            sp.wait_ge(rows_padded, 1)
            loads(NT, 0, io["x_sample"][0], NEW)
            store(NT - 1, 1)
            store(NT, 0)
            sp.wait_ge(stored[0], 16 * (NT // 2 + 1))
            sp.wait_ge(stored[1], 16 * (NT // 2))

        @block.gpsimd
        def _(eng):
            eng.memset(keep["fy"][NEW:2 * NEW, NT, :], 0.0).then_inc(mixers_padded, 1)
            eng.memset(keep["fy"][DH:P, NT, :], 0.0).then_inc(mixers_padded, 1)
            eng.wait_ge(mixers_padded, 2)
            eng.memset(gs[:, :], FAR).then_inc(mixers_padded, 1)
            eng.wait_ge(mixers_padded, 3)
            eng.wait_ge(*dve.after("z1", NT - 2))
            eng.memset(x[:, 0, :], 0.0).then_inc(rows_padded, 1)

        @block.tensor
        def _(eng):
            pe.begin(eng)
            ident = keep["ident"][:, :]
            eng.wait_ge(weights_loaded, 80)

            def tile(t, slot, j):
                eng.wait_ge(*dve.after("f", t))
                eng.wait_ge(*act.after("fT", t - 1))
                for a in range(PAIRS):
                    mm = eng.transpose(FT[:, a * P:(a + 1) * P], f[:, a * P:(a + 1) * P], ident)
                mm.then_inc(*pe.done("fT"))
                eng.wait_ge(*dve.after("z1", t - 1))
                for c in range(PAIRS):
                    for half in (0, 1):
                        eng.matmul(M[half][:, :], ry[:, slot, c, :], w[:, c, half * 512:(half + 1) * 512],
                                   start=(c == 0), stop=False)
                eng.wait_ge(*act.after("fT", t))
                for c in range(PAIRS):
                    for half in (0, 1):
                        mm = eng.matmul(M[half][:, :], fT[:, c, :], w[:, PAIRS + c, half * 512:(half + 1) * 512],
                                        start=False, stop=(c == PAIRS - 1))
                mm.then_inc(*pe.done("m"))
                eng.wait_ge(*dve.after("out", t))
                for half in (0, 1):
                    eng.wait_ge(*act.after(f"hT{half}", t - 1))
                    for k in range(4):
                        c = 4 * half + k
                        mm = eng.transpose(HT[half][:, k * P:(k + 1) * P], h[:, slot, c * P:(c + 1) * P], ident)
                    mm.then_inc(*pe.done(f"hT{half}"))
                eng.wait_ge(*act.after("hT1", t))
                eng.wait_ge(*act.after("score", t - 1))
                for c in range(KD):
                    mm = eng.matmul(SC[:, 0:EXPERTS], hT[:, c, :], rw[:, c, :], start=(c == 0), stop=(c == KD - 1))
                mm.then_inc(*pe.done("score"))
                rows = P if slot is not None and not (isinstance(t, int) and t == NT) else NEW
                eng.wait_ge(*dve.after("both", t))
                eng.wait_ge(*dve.after("carry", t - 1))
                eng.matmul(RK[:, 0:EXPERTS], keep["before"][0:rows, :], both[0:rows, :], start=True, stop=True)
                eng.matmul(RK[:, EXPERTS:2 * EXPERTS], keep["ones"][0:rows, :], both[0:rows, :], start=True, stop=True)\
                   .then_inc(*pe.done("rank"))

            over_tiles(eng, tile)

        @block.scalar
        def _(eng):
            act.begin(eng)

            def tile(t, slot, j):
                eng.wait_ge(*pe.after("fT", t))
                eng.wait_ge(*pe.after("m", t - 1))
                eng.copy(fT[:, :, :], FT[:, :].rearrange("p (a t) -> p a t", a=PAIRS)).then_inc(*act.done("fT"))
                eng.wait_ge(*dve.after("eps", t))
                eng.activation(std[:, :], mv[:, 2:3], ACT.Sqrt).then_inc(*act.done("std"))
                for half in (0, 1):
                    eng.wait_ge(*pe.after(f"hT{half}", t))
                    eng.wait_ge(*pe.after("score", t - 1))
                    eng.copy(hT[:, 4 * half:4 * half + 4, :], HT[half][:, :].rearrange("p (a t) -> p a t", a=4))\
                       .then_inc(*act.done(f"hT{half}"))
                eng.wait_ge(*pe.after("score", t))
                eng.wait_ge(*dve.after("prod", t - 1))
                eng.activation(score[:, :], SC[:, 0:EXPERTS], ACT.Sigmoid).then_inc(*act.done("score"))

            over_tiles(eng, tile)

        @block.vector
        def _(eng):
            eng.memset(keep["counts"][:, :], 0.0).then_inc(counts_zeroed, 1)
            eng.wait_ge(counts_zeroed, 1)
            eng.wait_ge(mixers_padded, 3)
            dve.begin(eng)
            eng.wait_ge(weights_loaded, 80)

            def at(name, ins, t):
                ins.then_inc(*dve.done(name))
                eng.wait_ge(*dve.after(name, t))

            def tile(t, slot, j):
                eng.wait_ge(loaded[slot], 48 * (j + 1))
                eng.wait_ge(*pe.after("fT", t - 1))
                if isinstance(t, int):
                    here = keep["fy"][:, t, :]
                else:
                    here = keep["fy"][:, bass.ds(t, 1), :].rearrange("p o c -> p (o c)")
                eng.tensor_tensor(f[:, :], here, og[:, slot, :], ALU.mult).then_inc(*dve.done("f"))
                eng.wait_ge(*pe.after("m", t))
                for half in (0, 1):
                    c = slice(half * 512, (half + 1) * 512)
                    at(f"z{half}", eng.scalar_tensor_tensor(out=z[:, c], in0=x[:, slot, c], scalar=ALPHA, in1=M[half][:, :],
                                                           op0=ALU.mult, op1=ALU.add), t)
                eng.wait_ge(stored[slot], 16 * j)
                layer_norm_steps(eng, dve, held, act.after("std", t), z[:, :], stats, mv, std[:, :], h[:, slot, :],
                                 gain[:, :], offset[:, :], "", t)
                eng.wait_ge(*act.after("score", t))
                at("sel", eng.tensor_tensor(sel[:, :], score[:, :], rb[:, :], ALU.add), t)
                hold(eng, held)
                for g in range(GROUPS):
                    ins = eng.max(out=top[:, g, :], in_=sel[:, g * PER_GROUP:(g + 1) * PER_GROUP])
                at("top", ins, t)
                at("gs", eng.tensor_tensor(gs[:, 0:GROUPS].unsqueeze(2), top[:, :, 0:1], top[:, :, 1:2], ALU.add), t)
                hold(eng, held)
                at("gbest", eng.max(out=gbest[:, :], in_=gs[:, :]), t)
                hold(eng, held)
                at("gidx", eng.max_index(out=gidx[:, :], in_max=gbest[:, :], in_values=gs[:, :]), t)
                at("gid", eng.tensor_copy(gid[:, :], gidx[:, 0:1]), t)
                at("gm", eng.tensor_scalar(gm[:, :], keep["group_of"][:, :], gid[:, :], None, ALU.is_equal), t)
                at("pen", eng.tensor_scalar(selm[:, :], gm[:, :], -FAR, FAR, ALU.mult, ALU.add), t)
                at("selm1", eng.tensor_tensor(gm[:, :], gm[:, :], sel[:, :], ALU.mult), t)
                at("selm2", eng.tensor_tensor(selm[:, :], selm[:, :], gm[:, :], ALU.add), t)
                hold(eng, held)
                at("ebest", eng.max(out=ebest[:, :], in_=selm[:, :]), t)
                hold(eng, held)
                at("eidx", eng.max_index(out=eidx[:, :], in_max=ebest[:, :], in_values=selm[:, :]), t)
                one = bass.ds(t, 1)
                at("eid", eng.tensor_copy(keep["expert"][:, one, :], eidx[:, 0:2].unsqueeze(1)), t)
                for i in (0, 1):
                    at(f"pick{i}", eng.tensor_tensor(pick[:, i, :], keep["expert_id"][:, :],
                                                     keep["expert"][:, one, i].broadcast_to([P, EXPERTS]), ALU.is_equal), t)
                eng.wait_ge(*pe.after("rank", t - 1))
                at("both", eng.tensor_tensor(both[:, :], pick[:, 0, :], pick[:, 1, :], ALU.add), t)
                at("prod", eng.tensor_tensor(prod[:, :, :], pick[:, :, :], every(score[:, :], 2), ALU.mult), t)
                at("graw", eng.tensor_reduce(graw[:, :], prod[:, :, :], AX_X, ALU.add), t)
                at("gsum", eng.tensor_tensor(gsum[:, 0:1], graw[:, 0:1], graw[:, 1:2], ALU.add), t)
                at("ginv", eng.reciprocal(gsum[:, 1:2], gsum[:, 0:1]), t)
                at("gate", eng.tensor_scalar(keep["gate"][:, one, :], graw[:, :].unsqueeze(1), gsum[:, 1:2], None,
                                             ALU.mult), t)
                eng.wait_ge(*pe.after("rank", t))
                at("rank", eng.tensor_tensor(rank[:, :], RK[:, 0:EXPERTS], keep["counts"][:, :], ALU.add), t)
                at("carry", eng.tensor_tensor(keep["counts"][:, :], RK[:, EXPERTS:2 * EXPERTS], keep["counts"][:, :],
                                              ALU.add), t)
                at("rprod", eng.tensor_tensor(prod[:, :, :], pick[:, :, :], every(rank[:, :], 2), ALU.mult), t)
                at("rout", eng.tensor_reduce(keep["rank"][:, one, :].rearrange("p o i -> p (o i)"), prod[:, :, :],
                                             AX_X, ALU.add), t)

            over_tiles(eng, tile)


def dispatch(nc, io, keep):
    with ExitStack() as ctx:
        def sb(name, shape, dt=F32):
            return ctx.enter_context(nc.sbuf_tensor(name, shape, dt))

        def sem(name):
            return ctx.enter_context(nc.semaphore(name))

        ci = sb("d_ci", [P, EXPERTS], I32)
        nb = sb("d_nb", [P, EXPERTS])
        end, first = sb("d_end", [P, EXPERTS]), sb("d_first", [P, EXPERTS])
        N2 = 2 * TILES
        eq = sb("d_eq", [P, N2, EXPERTS])
        base = sb("d_base", [P, N2])
        bi, bf = sb("d_bi", [1, BLOCKS], I32), sb("d_bf", [1, BLOCKS])
        cmp = sb("d_cmp", [1, BLOCKS, EXPERTS])
        be = sb("d_be", [1, BLOCKS])
        zero = sb("d_zero", [P, BLOCKS], I32)
        frame = sb("d_frame", [P, TILES], I32)
        made = sem("d_made")
        steps = sem("d_steps")
        cleared = sem("d_cleared")
        scattered = sem("d_scattered")
        block = ctx.enter_context(nc.Block())

        @block.vector
        def _(eng):
            n = [0]

            def at(ins):
                n[0] += 1
                ins.then_inc(steps, 1)
                eng.wait_ge(steps, n[0])

            at(eng.tensor_scalar(ci[:, :], keep["counts"][:, :], float(P - 1), None, ALU.add))
            at(eng.tensor_scalar(ci[:, :], ci[:, :], 7, None, ALU.arith_shift_right))
            at(eng.tensor_copy(nb[:, :], ci[:, :]))
            at(eng.tensor_tensor_scan(out=end[:, :], data0=keep["ones"][:, 0:EXPERTS], data1=nb[:, :], initial=0.0,
                                      op0=ALU.mult, op1=ALU.add))
            at(eng.tensor_tensor(first[:, :], end[:, :], nb[:, :], ALU.subtract))
            at(eng.tensor_tensor(eq[:, :, :], keep["expert_id"][:, :].unsqueeze(1).broadcast_to([P, N2, EXPERTS]),
                                 keep["expert"][:, :, :].rearrange("p n i -> p (n i)").unsqueeze(2)
                                 .broadcast_to([P, N2, EXPERTS]), ALU.is_equal))
            at(eng.tensor_tensor(eq[:, :, :], eq[:, :, :], first[:, :].unsqueeze(1).broadcast_to([P, N2, EXPERTS]),
                                 ALU.mult))
            at(eng.tensor_reduce(base[:, :], eq[:, :, :], AX_X, ALU.add))
            at(eng.scalar_tensor_tensor(out=keep["row"][:, :, :].rearrange("p n i -> p (n i)"), in0=base[:, :],
                                        scalar=float(P), in1=keep["rank"][:, :, :].rearrange("p n i -> p (n i)"),
                                        op0=ALU.mult, op1=ALU.add))
            eng.wait_ge(made, 2)
            at(eng.tensor_copy(bf[:, :], bi[:, :]))
            at(eng.tensor_tensor(cmp[:, :, :], end[0:1, :].unsqueeze(1).broadcast_to([1, BLOCKS, EXPERTS]),
                                 bf[:, :].unsqueeze(2).broadcast_to([1, BLOCKS, EXPERTS]), ALU.is_le))
            at(eng.tensor_reduce(be[:, :], cmp[:, :, :], AX_X, ALU.add))
            at(eng.tensor_scalar(keep["block_expert"][:, :], be[:, :], float(EXPERTS - 1), None, ALU.min))

        STEPS = 13

        @block.sync
        def _(sp):
            sp.wait_ge(made, 3)
            sp.dma_start(io["frame_of"].rearrange("(p n) o -> p (n o)", p=P), zero[:, :]).then_inc(cleared, 16)

        @block.gpsimd
        def _(eng):
            eng.iota(bi[:, :], pattern=[[1, BLOCKS]], base=0, channel_multiplier=0).then_inc(made, 1)
            eng.iota(frame[:, :], pattern=[[P, TILES]], base=0, channel_multiplier=1).then_inc(made, 1)
            eng.memset(zero[:, :], 0).then_inc(made, 1)
            eng.wait_ge(made, 3)
            eng.wait_ge(steps, STEPS)
            eng.wait_ge(cleared, 16)
            for t in range(TILES):
                rows = P if t < NT else NEW
                for i in (0, 1):
                    eng.indirect_dma_start(out=io["frame_of"][:, :],
                                           out_offset=bass.IndirectOffsetOnAxis(ap=keep["row"][0:rows, t, i:i + 1], axis=0),
                                           in_=frame[0:rows, t:t + 1], in_offset=None,
                                           bounds_check=BLOCKS * P - 1, oob_is_err=False).then_inc(scattered, 16)
            eng.wait_ge(scattered, 16 * 2 * TILES)


def experts(nc, io, keep):
    with ExitStack() as ctx:
        def sb(name, shape, dt=F32):
            return ctx.enter_context(nc.sbuf_tensor(name, shape, dt))

        def sem(name):
            return ctx.enter_context(nc.semaphore(name))

        KE = DE // P
        XT = [ctx.enter_context(nc.psum_tensor(f"e_XT{b}", [P, 512], F32)) for b in range(2)]
        H1 = ctx.enter_context(nc.psum_tensor("e_H1", [P, 512], F32))
        H3 = ctx.enter_context(nc.psum_tensor("e_H3", [P, 512], F32))
        GT = ctx.enter_context(nc.psum_tensor("e_GT", [P, 512], F32))
        Y = [ctx.enter_context(nc.psum_tensor(f"e_Y{b}", [P, 512], F32)) for b in range(2)]
        w1, w3 = sb("e_w1", [P, 2, KD, DE]), sb("e_w3", [P, 2, KD, DE])
        w2 = sb("e_w2", [P, 2, KE, D])
        idx = sb("e_idx", [P, 2], I32)
        x = sb("e_x", [P, 2, D])
        xT = sb("e_xT", [P, 2, KD, P])
        a = sb("e_a", [P, DE])
        g = sb("e_g", [P, DE])
        gT = sb("e_gT", [P, KE, P])
        y = sb("e_y", [P, 2, D])

        w13_loaded = [sem(f"e_w13_loaded{s}") for s in (0, 1)]
        w2_loaded = [sem(f"e_w2_loaded{s}") for s in (0, 1)]
        idx_loaded = [sem(f"e_idx_loaded{s}") for s in (0, 1)]
        x_loaded = [sem(f"e_x_loaded{s}") for s in (0, 1)]
        stored = [sem(f"e_stored{s}") for s in (0, 1)]
        held = sem("e_pool_held")
        xpe = Steps(sem("e_x_pe_steps"), ["xT0", "xT1"])
        xact = Steps(sem("e_x_act_steps"), ["xT0"])
        xdve = Steps(sem("e_x_dve_steps"), ["xT1"])
        pe = Steps(sem("e_pe_steps"), ["h1", "h3", "gT", "y0", "y1"])
        act = Steps(sem("e_act_steps"), ["a", "y0"])
        dve = Steps(sem("e_dve_steps"), ["g", "gT", "y1"])
        block = ctx.enter_context(nc.Block())
        PAIRED = BLOCKS // 2
        assert BLOCKS % 2 == 1

        def over_blocks(eng, body):
            with eng.Fori(0, PAIRED) as j:
                for s in (0, 1):
                    body(2 * j + s, s, j)
            body(BLOCKS - 1, 0, PAIRED)

        @block.sync
        def _(sp):
            def body(b, s, j):
                e = sp.value_load(keep["block_expert"][0:1, bass.ds(b, 1)], min_val=0, max_val=EXPERTS - 1)
                sp.wait_ge(*pe.after("h3", b - 1))
                for w, name in ((w1, "moe_w1"), (w3, "moe_w3")):
                    sp.dma_start(w[:, s, :, :], io[name][0, bass.ds(e, 1)].rearrange("o (p k) n -> p (o k) n", k=KD))\
                      .then_inc(w13_loaded[s], 16)
                sp.wait_ge(*pe.after("y1", b - 1))
                sp.dma_start(w2[:, s, :, :], io["moe_w2"][0, bass.ds(e, 1)].rearrange("o (p k) n -> p (o k) n", k=KE))\
                  .then_inc(w2_loaded[s], 16)

            over_blocks(sp, body)

        @block.gpsimd
        def _(eng):
            def body(b, s, j):
                row = b * P if isinstance(b, int) else eng.snap(b * P)
                eng.wait_ge(*xpe.after("xT1", b - 1))
                eng.dma_start(idx[:, s:s + 1], io["frame_of"][bass.ds(row, P), :]).then_inc(idx_loaded[s], 16)
                eng.wait_ge(idx_loaded[s], 16 * (j + 1))
                hold(eng, held)
                eng.indirect_dma_start(out=x[:, s, :], out_offset=None, in_=io["h"][:, :],
                                       in_offset=bass.IndirectOffsetOnAxis(ap=idx[:, s:s + 1], axis=0),
                                       bounds_check=ROWS - 1, oob_is_err=False).then_inc(x_loaded[s], 16)

            over_blocks(eng, body)

        @block.tensor
        def _(eng):
            xpe.begin(eng)
            pe.begin(eng)
            ident = keep["ident"][:, :]

            def turn_x(b, s, j):
                eng.wait_ge(x_loaded[s], 16 * (j + 1))
                for half in (0, 1):
                    eng.wait_ge(*(xdve.after("xT1", b - 1) if half else xact.after("xT0", b - 1)))
                    for k in range(4):
                        mm = eng.transpose(XT[half][:, k * P:(k + 1) * P], x[:, s, 4 * half + k:D:KD], ident)
                    mm.then_inc(*xpe.done(f"xT{half}"))

            def body(b, s, j, following=True):
                eng.wait_ge(*xact.after("xT0", b))
                eng.wait_ge(*xdve.after("xT1", b))
                eng.wait_ge(w13_loaded[s], 32 * (j + 1))
                for name, w, out, free in (("h1", w1, H1, act.after("a", b - 1)), ("h3", w3, H3, dve.after("g", b - 1))):
                    eng.wait_ge(*free)
                    for k in range(KD):
                        mm = eng.matmul(out[:, :], xT[:, s, k, :], w[:, s, k, :], start=(k == 0), stop=(k == KD - 1))
                    mm.then_inc(*pe.done(name))
                if following:
                    turn_x(b + 1, 1 - s, j + s)
                eng.wait_ge(*dve.after("g", b))
                eng.wait_ge(*dve.after("gT", b - 1))
                for k in range(KE):
                    mm = eng.transpose(GT[:, k * P:(k + 1) * P], g[:, k:DE:KE], ident)
                mm.then_inc(*pe.done("gT"))
                eng.wait_ge(w2_loaded[s], 16 * (j + 1))
                eng.wait_ge(*dve.after("gT", b))
                for half in (0, 1):
                    eng.wait_ge(*(dve.after("y1", b - 1) if half else act.after("y0", b - 1)))
                    for k in range(KE):
                        mm = eng.matmul(Y[half][:, :], gT[:, k, :], w2[:, s, k, half * 512:(half + 1) * 512],
                                        start=(k == 0), stop=(k == KE - 1))
                    mm.then_inc(*pe.done(f"y{half}"))

            turn_x(0, 0, 0)
            with eng.Fori(0, PAIRED) as j:
                for s in (0, 1):
                    body(2 * j + s, s, j)
            body(BLOCKS - 1, 0, PAIRED, following=False)

        @block.scalar
        def _(eng):
            act.begin(eng)
            xact.begin(eng)

            def copy_x(b, s):
                eng.wait_ge(*xpe.after("xT0", b))
                eng.wait_ge(*pe.after("h3", b - 1))
                eng.copy(xT[:, s, 0:4, :], XT[0][:, :].rearrange("p (k t) -> p k t", k=4)).then_inc(*xact.done("xT0"))

            def body(b, s, j, following=True):
                eng.wait_ge(*pe.after("h1", b))
                eng.wait_ge(*dve.after("g", b - 1))
                eng.activation(a[:, :], H1[:, :], ACT.Silu).then_inc(*act.done("a"))
                if following:
                    copy_x(b + 1, 1 - s)
                eng.wait_ge(*pe.after("y0", b))
                eng.wait_ge(stored[s], 16 * j)
                eng.copy(y[:, s, 0:512], Y[0][:, :]).then_inc(*act.done("y0"))
                eng.wait_ge(*act.after("y0", b))
                eng.wait_ge(*dve.after("y1", b))
                eng.dma_start(io["ypad"][bass.ds(b * P, P), :], y[:, s, :]).then_inc(stored[s], 16)

            copy_x(0, 0)
            with eng.Fori(0, PAIRED) as j:
                for s in (0, 1):
                    body(2 * j + s, s, j)
            body(BLOCKS - 1, 0, PAIRED, following=False)
            eng.wait_ge(stored[0], 16 * (PAIRED + 1))
            eng.wait_ge(stored[1], 16 * PAIRED)

        @block.vector
        def _(eng):
            dve.begin(eng)
            xdve.begin(eng)

            def copy_x(b, s):
                eng.wait_ge(*xpe.after("xT1", b))
                eng.wait_ge(*pe.after("h3", b - 1))
                eng.tensor_copy(xT[:, s, 4:8, :], XT[1][:, :].rearrange("p (k t) -> p k t", k=4))\
                   .then_inc(*xdve.done("xT1"))

            def body(b, s, j, following=True):
                eng.wait_ge(*act.after("a", b))
                eng.wait_ge(*pe.after("h3", b))
                eng.wait_ge(*pe.after("gT", b - 1))
                eng.tensor_tensor(g[:, :], a[:, :], H3[:, :], ALU.mult).then_inc(*dve.done("g"))
                if following:
                    copy_x(b + 1, 1 - s)
                eng.wait_ge(*pe.after("gT", b))
                eng.wait_ge(*pe.after("y1", b - 1))
                eng.tensor_copy(gT[:, :, :], GT[:, :].rearrange("p (k t) -> p k t", k=KE)).then_inc(*dve.done("gT"))
                eng.wait_ge(*pe.after("y1", b))
                eng.wait_ge(stored[s], 16 * j)
                eng.tensor_copy(y[:, s, 512:D], Y[1][:, :]).then_inc(*dve.done("y1"))

            copy_x(0, 0)
            with eng.Fori(0, PAIRED) as j:
                for s in (0, 1):
                    body(2 * j + s, s, j)
            body(BLOCKS - 1, 0, PAIRED, following=False)


def combine(nc, io, keep):
    with ExitStack() as ctx:
        def sb(name, shape, dt=F32):
            return ctx.enter_context(nc.sbuf_tensor(name, shape, dt))

        def sem(name):
            return ctx.enter_context(nc.semaphore(name))

        gain, offset = sb("z_gain", [P, D]), sb("z_offset", [P, D])
        h = sb("z_h", [P, 2, D])
        idx = sb("z_idx", [P, 2, 2], I32)
        y = sb("z_y", [P, 2, 2, D])
        z = sb("z_z", [P, D])
        stats, mv, std = sb("z_stats", [P, 2, 6]), sb("z_mv", [P, 4]), sb("z_std", [P, 1])
        out = sb("z_out", [P, 2, D])
        weights_loaded = sem("z_weights_loaded")
        h_loaded = [sem(f"z_h_loaded{s}") for s in (0, 1)]
        y_loaded = [sem(f"z_y_loaded{s}") for s in (0, 1)]
        stored = [sem(f"z_stored{s}") for s in (0, 1)]
        held, pool_held = sem("z_held"), sem("z_pool_held")
        pool = Steps(sem("z_pool_steps"), ["idx"])
        act = Steps(sem("z_act_steps"), ["std"])
        dve = Steps(sem("z_dve_steps"), ["y0", "y1", "z", "stats", "mv", "eps", "rstd", "norm", "gain", "out"])
        block = ctx.enter_context(nc.Block())

        @block.sync
        def _(sp):
            sp.dma_start(gain[:, :], io["ln2_g"].broadcast_to([P, D])).then_inc(weights_loaded, 16)
            sp.dma_start(offset[:, :], io["ln2_b"].broadcast_to([P, D])).then_inc(weights_loaded, 16)

            def load(t, s):
                sp.dma_start(h[:, s, :], io["h"][bass.ds(t * P, P), :]).then_inc(h_loaded[s], 16)

            def store(t, s, dst, rows=P):
                sp.wait_ge(*dve.after("out", t))
                sp.dma_start(dst, out[0:rows, s, :]).then_inc(stored[s], 16)

            load(0, 0)
            load(1, 1)
            with sp.Fori(0, NT // 2 - 1) as j:
                for s in (0, 1):
                    t = 2 * j + s
                    store(t, s, io["y_prompt"][0, bass.ds(t * P, P), :])
                    load(t + 2, s)
            store(NT - 2, 0, io["y_prompt"][0, (NT - 2) * P:(NT - 1) * P, :])
            load(NT, 0)
            store(NT - 1, 1, io["y_prompt"][0, (NT - 1) * P:NT * P, :])
            store(NT, 0, io["y_sample"][0], NEW)
            sp.wait_ge(stored[0], 16 * (NT // 2 + 1))
            sp.wait_ge(stored[1], 16 * (NT // 2))

        @block.gpsimd
        def _(eng):
            pool.begin(eng)

            def tile(t, s, j):
                rows = NEW if isinstance(t, int) and t == NT else P
                eng.wait_ge(*dve.after("y1", t - 1))
                hold(eng, pool_held)
                eng.tensor_copy(idx[:, s, :].unsqueeze(1), keep["row"][:, bass.ds(t, 1), :]).then_inc(*pool.done("idx"))
                eng.wait_ge(*pool.after("idx", t))
                hold(eng, pool_held)
                for i in (0, 1):
                    eng.indirect_dma_start(out=y[0:rows, s, i, :], out_offset=None, in_=io["ypad"][:, :],
                                           in_offset=bass.IndirectOffsetOnAxis(ap=idx[0:rows, s, i:i + 1], axis=0),
                                           bounds_check=BLOCKS * P - 1, oob_is_err=False).then_inc(y_loaded[s], 16)

            over_tiles(eng, tile)

        @block.scalar
        def _(eng):
            act.begin(eng)

            def tile(t, s, j):
                eng.wait_ge(*dve.after("eps", t))
                eng.activation(std[:, :], mv[:, 2:3], ACT.Sqrt).then_inc(*act.done("std"))

            over_tiles(eng, tile)

        @block.vector
        def _(eng):
            dve.begin(eng)
            eng.wait_ge(weights_loaded, 32)

            def tile(t, s, j):
                g = keep["gate"][:, bass.ds(t, 1), :]
                eng.wait_ge(y_loaded[s], 32 * (j + 1))
                eng.wait_ge(*dve.after("out", t - 1))
                g0, g1 = (g[:, :, i:i + 1].rearrange("p o i -> p (o i)") for i in (0, 1))
                eng.tensor_scalar(z[:, :], y[:, s, 0, :], g0, None, ALU.mult).then_inc(*dve.done("y0"))
                eng.wait_ge(*dve.after("y0", t))
                eng.scalar_tensor_tensor(out=z[:, :], in0=y[:, s, 1, :], scalar=g1, in1=z[:, :], op0=ALU.mult,
                                         op1=ALU.add).then_inc(*dve.done("y1"))
                eng.wait_ge(h_loaded[s], 16 * (j + 1))
                eng.wait_ge(*dve.after("y1", t))
                eng.scalar_tensor_tensor(out=z[:, :], in0=h[:, s, :], scalar=ALPHA, in1=z[:, :], op0=ALU.mult,
                                         op1=ALU.add).then_inc(*dve.done("z"))
                eng.wait_ge(*dve.after("z", t))
                eng.wait_ge(stored[s], 16 * j)
                layer_norm_steps(eng, dve, held, act.after("std", t), z[:, :], stats, mv, std[:, :], out[:, s, :],
                                 gain[:, :], offset[:, :], "", t)

            over_tiles(eng, tile)


def build(nc, io):
    with ExitStack() as ctx:
        keep = constants(nc, ctx)
        fox_projection(nc, io, keep)
        rwkv(nc, io, keep)
        with ExitStack() as inner:
            keep["fy"] = inner.enter_context(nc.sbuf_tensor("fy", [P, TILES, DG], F32))
            fox_prompt(nc, io, keep)
            fox_sample(nc, io, keep)
            mix_and_route(nc, io, keep)
        dispatch(nc, io, keep)
        experts(nc, io, keep)
        combine(nc, io, keep)


_INS = ['x_prompt', 'x_sample', 'cache_fox_k', 'cache_fox_v', 'cache_fox_logf', 'state_rwkv', 'state_rwkv_shift',
        'w_in', 'rwkv_mu', 'rwkv_w0', 'rwkv_w2', 'rwkv_a0', 'rwkv_a2', 'rwkv_g2', 'rwkv_k_k', 'rwkv_k_a', 'rwkv_r_k',
        'rwkv_lnx_w', 'rwkv_lnx_b', 'fox_b_f', 'fox_q_g', 'fox_k_g', 'w_out', 'ln1_g', 'ln1_b', 'ln2_g', 'ln2_b',
        'router_w', 'router_b', 'moe_w1', 'moe_w3', 'moe_w2']
_OUTS = [('y_prompt', (1, SEQ, D), (1, SEQ, D)), ('y_sample', (1, NEW, D), (1, NEW, D)),
         ('p_k', (SEQ, DG), (1, 1, SEQ, HEADS, DH)), ('p_v', (SEQ, DG), (1, 1, SEQ, HEADS, DH)),
         ('p_lf', (SEQ, HEADS), (1, 1, SEQ, HEADS)), ('p_rwkv', (HEADS, DH, DH), (1, 1, HEADS, DH, DH)),
         ('p_shift', (1, RCOLS), (1, 1, 1, RCOLS)),
         ('s_k', (NEW, DG), (1, 1, NEW, HEADS, DH)), ('s_v', (NEW, DG), (1, 1, NEW, HEADS, DH)),
         ('s_lf', (NEW, HEADS), (1, 1, NEW, HEADS)), ('s_rwkv', (HEADS, DH, DH), (1, 1, HEADS, DH, DH)),
         ('s_shift', (1, RCOLS), (1, 1, 1, RCOLS))]
_SCRATCH = [('qT', (PAIRS, P, ROWS), F32), ('kT', (PAIRS, P, ROWS), F32), ('cT', (HEADS, ROWS), F32),
            ('ryT', (PAIRS, P, ROWS), F32), ('og', (ROWS, DG), F32), ('h', (ROWS, D), F32),
            ('frame_of', (BLOCKS * P, 1), I32), ('ypad', (BLOCKS * P, D), F32)]


def kernel(**inputs):
    import numpy as np
    import concourse.bacc as bacc
    from concourse.bass_utils import run_bass_kernel_spmd

    nc = bacc.Bacc("TRN2", target_bir_lowering=False, num_devices=1)
    arrays, io = {}, {}
    for name in _INS:
        a = np.ascontiguousarray(inputs[name])
        arrays[f"in_{name}"] = a
        io[name] = nc.dram_tensor(f"in_{name}", a.shape, mybir.dt.from_np(a.dtype), kind="ExternalInput").ap()
    for name, shape, _ in _OUTS:
        io[name] = nc.dram_tensor(f"out_{name}", shape, F32, kind="ExternalOutput").ap()
    for name, shape, dt in _SCRATCH:
        io[name] = nc.dram_tensor(f"scratch_{name}", shape, dt, kind="Internal").ap()
    build(nc, io)
    r = run_bass_kernel_spmd(nc, [arrays], core_ids=[0])
    return tuple(r.results[0][f"out_{name}"].reshape(shape) for name, _, shape in _OUTS)
```

```python
from contextlib import ExitStack

import concourse.bass as bass
from concourse import mybir

F32 = mybir.dt.float32
I32 = mybir.dt.int32
U32 = mybir.dt.uint32
ALU = mybir.AluOpType
ACT = mybir.ActivationFunctionType
AX_X = mybir.AxisListType.X

P = 128
D = 1024
KD = D // P
SEQ = 2048
NEW = 32
PAST = 4096
NT = SEQ // P
TILES = NT + 1
ROWS = TILES * P
HEADS = 8
DH = 64
DG = HEADS * DH
PAIRS = HEADS // 2
LORA = 64
RCOLS = 3 * DG + 2 * LORA + P
FCOLS = 3 * DG + HEADS + DG
RCH = RCOLS // P
EXPERTS = 32
GROUPS = 4
PER_GROUP = EXPERTS // GROUPS
DE = D // 2
TOKENS = SEQ + NEW
BLOCKS = -(-2 * TOKENS // P) + EXPERTS
ALPHA = 2.0 ** 0.25
LN_EPS = 1e-5
GN_EPS = 64e-5
QK_EPS = 1e-6
SCALE = DH ** -0.5
DECAY = 0.6065306597126334
FAR = -1e30


class Steps:

    def __init__(self, sem, names, ahead=1):
        self.sem, self.names, self.ahead, self.at = sem, names, ahead, 0
        assert len(set(names)) == len(names)

    def begin(self, eng):
        eng.nop().then_inc(self.sem, self.ahead * len(self.names))

    def done(self, name):
        assert self.names[self.at % len(self.names)] == name, (self.names[self.at % len(self.names)], name)
        self.at += 1
        return self.sem, 1

    def after(self, name, t):
        return self.sem, (t + self.ahead) * len(self.names) + self.names.index(name) + 1


def hold(eng, sem):
    eng.sem_inc(sem, 1)


def begin_stores(eng, stored, per_tile=16):
    for s in stored:
        eng.sem_inc(s, per_tile)


def over_tiles(eng, tile):
    with eng.Fori(0, NT // 2) as j:
        for slot in (0, 1):
            tile(2 * j + slot, slot, j)
    tile(NT, 0, NT // 2)
def constants(nc, ctx):
    keep = {}

    def sb(name, shape, dt=F32):
        keep[name] = ctx.enter_context(nc.sbuf_tensor(name, shape, dt))
        return keep[name]

    ready = ctx.enter_context(nc.semaphore("constants_ready"))
    keep["constants_ready"] = ready
    ident, ones, upto, before, after = (sb(n, [P, P]) for n in ("ident", "ones", "upto", "before", "after"))
    halves, causal = sb("halves", [P, P]), sb("causal", [P, P])
    sb("expert_id", [P, EXPERTS])
    sb("group_of", [P, EXPERTS])
    sb("expert", [P, TILES, 2])
    sb("logits", [P, TILES, EXPERTS])
    sb("gate", [P, TILES, 2])
    sb("rank", [P, TILES, 2])
    sb("counts", [P, EXPERTS])
    sb("row", [P, TILES, 2], I32)
    sb("frame_of", [P, BLOCKS], I32)
    sb("block_expert", [1, BLOCKS], I32)
    sb("block_fresh", [1, BLOCKS], I32)
    sb("block_place", [1, BLOCKS], I32)
    ids = sb("ids", [P, 2, EXPERTS], I32)
    shapes = [
        (ident, 0.0, ALU.not_equal, -1, 1, 0, 1.0),
        (ones, 1.0, None, 0, 0, 0, 0.0),
        (upto, 1.0, ALU.is_ge, 1, -1, 0, 0.0),
        (before, 1.0, ALU.is_gt, 1, -1, 0, 0.0),
        (after, 1.0, ALU.is_gt, -1, 1, 0, 0.0),
        (causal, 0.0, ALU.is_ge, -1, 1, 0, FAR),
    ]
    n = [0]
    with nc.Block() as block:
        @block.gpsimd
        def _(pool):
            def step(ins):
                n[0] += 1
                ins.then_inc(ready, 1)
                return n[0]

            for out, back, op, col, row, base, fill in shapes:
                count = step(pool.memset(out[:, :], back))
                if op is not None:
                    pool.wait_ge(ready, count)
                    step(pool.affine_select(out=out[:, :], in_=out[:, :], compare_op=op, fill=fill, base=base,
                                            pattern=[[col, P]], channel_multiplier=row))
            step(pool.iota(ids[:, 0, :], pattern=[[1, EXPERTS]], base=0, channel_multiplier=0))
            count = step(pool.iota(ids[:, 1, :], pattern=[[1, GROUPS], [0, PER_GROUP]], base=0, channel_multiplier=0))
            pool.wait_ge(ready, count)
            step(pool.tensor_copy(keep["expert_id"][:, :], ids[:, 0, :]))
            step(pool.tensor_copy(keep["group_of"][:, :], ids[:, 1, :]))
            count = step(pool.memset(halves[:, :], 0.0))
            pool.wait_ge(ready, count)
            step(pool.memset(halves[0:DH, 0:DH], 1.0))
            step(pool.memset(halves[DH:P, DH:P], 1.0))
            pool.wait_ge(ready, n[0])
    keep["constants"] = n[0]
    return keep
def fox_projection(nc, io, keep):
    with ExitStack() as ctx:
        def sb(name, shape, dt=F32):
            return ctx.enter_context(nc.sbuf_tensor(name, shape, dt))

        def sem(name):
            return ctx.enter_context(nc.semaphore(name))

        psum = [ctx.enter_context(nc.psum_tensor(f"fp{b}", [P, 512], F32)) for b in range(8)]
        X, Q, K, V, G, S, T = psum[0:2], psum[2], psum[3], psum[4], psum[5], psum[6], psum[7]
        w = sb("f_w", [P, KD, FCOLS])
        x = sb("f_x", [P, 2, D])
        xT = sb("f_xT", [P, KD, P])
        bf = sb("f_bf", [P, HEADS])
        qg = sb("f_qg", [P, DH])
        kg = sb("f_kg", [P, DH])
        carry = sb("f_carry", [P, HEADS])
        fb = sb("f_fb", [P, 4, HEADS])
        qk = sb("f_qk", [P, 2, DG])
        sq = sb("f_sq", [P, 2, DG])
        ss = sb("f_ss", [P, 3, 2 * HEADS])
        qn = sb("f_qn", [P, DG])
        kn = sb("f_kn", [P, 2, DG])
        vn = sb("f_vn", [P, 2, DG])
        og = sb("f_og", [P, 2, DG])
        lf = sb("f_lf", [P, 2, HEADS])
        negc = sb("f_negc", [P, HEADS])
        qT = sb("f_qT", [P, 2, DG])
        kT = sb("f_kT", [P, 2, DG])
        cT = sb("f_cT", [HEADS, 2, P])

        weights_loaded = sem("f_weights_loaded")
        x_loaded = [sem(f"f_x_loaded{s}") for s in (0, 1)]
        stored = [sem(f"f_stored{s}") for s in (0, 1)]
        pool_ready = sem("f_pool_ready")
        carry_zeroed = sem("f_carry_zeroed")
        pe = Steps(sem("f_pe_steps"), ["xT0", "xT1", "f", "q", "k", "v", "g", "cum", "qT", "kT", "cT"])
        act = Steps(sem("f_act_steps"), ["xT0", "xT1", "e", "l", "q", "k", "v", "g", "rms", "qT"])
        dve = Steps(sem("f_dve_steps"), [
            "fb", "negabs", "logf", "negc", "carry", "sq0", "ss0", "sq1", "ss1", "mean", "rs",
            "q1", "q2", "k1", "k2", "kT", "cT"])
        STORES = 7

        block = ctx.enter_context(nc.Block())
        w_rows = io["w_in"][0].rearrange("(p k) n -> p k n", k=KD)

        @block.sync
        def _(sp):
            begin_stores(sp, stored, 16 * STORES)
            sp.dma_start(w[:, :, :], w_rows[:, :, RCOLS:]).then_inc(weights_loaded, 16)
            with nc.allow_non_contiguous_dma(reason="small rows for all partitions"):
                sp.dma_start(bf[:, :], io["fox_b_f"].broadcast_to([P, HEADS])).then_inc(weights_loaded, 16)
                sp.dma_start(qg[:, :], io["fox_q_g"].broadcast_to([P, DH])).then_inc(weights_loaded, 16)
                sp.dma_start(kg[:, :], io["fox_k_g"].broadcast_to([P, DH])).then_inc(weights_loaded, 16)

            def stores(t, slot, rows, dst_row, k_out, v_out, lf_out):
                sp.wait_ge(*act.after("qT", t))
                sp.wait_ge(*dve.after("cT", t))
                with nc.allow_non_contiguous_dma(reason="rows of 8 gates"):
                    sp.dma_start(lf_out, lf[0:rows, slot, :]).then_inc(stored[slot], 16)
                sp.dma_start(k_out, kn[0:rows, slot, :]).then_inc(stored[slot], 16)
                sp.dma_start(v_out, vn[0:rows, slot, :]).then_inc(stored[slot], 16)
                sp.dma_start(io["og"][bass.ds(dst_row, P), :], og[:, slot, :]).then_inc(stored[slot], 16)
                for kind, src in (("qT", qT), ("kT", kT)):
                    sp.dma_start(io[kind][:, :, bass.ds(dst_row, P)].rearrange("a p t -> p a t"),
                                 src[:, slot, :].rearrange("p (a t) -> p a t", a=PAIRS)).then_inc(stored[slot], 16)
                sp.dma_start(io["cT"][:, bass.ds(dst_row, P)], cT[:, slot, :]).then_inc(stored[slot], 16)

            def stores_of(t, slot):
                at = t * P
                stores(t, slot, P, at, io["p_k"][bass.ds(at, P), :], io["p_v"][bass.ds(at, P), :],
                       io["p_lf"][bass.ds(at, P), :])

            sp.dma_start(x[:, 0, :], io["x_prompt"][0, 0:P, :]).then_inc(x_loaded[0], 16)
            with sp.Fori(0, NT // 2 - 1) as j:
                for slot in (0, 1):
                    t = 2 * j + slot
                    sp.wait_ge(*pe.after("xT1", t - 1))
                    sp.dma_start(x[:, 1 - slot, :], io["x_prompt"][0, bass.ds((t + 1) * P, P), :]).then_inc(
                        x_loaded[1 - slot], 16)
                    stores_of(t, slot)
            t = NT - 2
            sp.wait_ge(*pe.after("xT1", t - 1))
            sp.dma_start(x[:, 1, :], io["x_prompt"][0, (t + 1) * P:(t + 2) * P, :]).then_inc(x_loaded[1], 16)
            stores_of(t, 0)
            sp.wait_ge(pool_ready, 1)
            sp.dma_start(x[0:NEW, 0, :], io["x_sample"][0]).then_inc(x_loaded[0], 16)
            stores_of(NT - 1, 1)
            stores(NT, 0, NEW, NT * P, io["s_k"], io["s_v"], io["s_lf"])
            sp.wait_ge(stored[0], 16 * STORES * (NT // 2 + 2))
            sp.wait_ge(stored[1], 16 * STORES * (NT // 2 + 1))

        @block.gpsimd
        def _(pool):
            pool.wait_ge(*pe.after("xT1", NT - 2))
            pool.memset(x[:, 0, :], 0.0).then_inc(pool_ready, 1)

        @block.tensor
        def _(eng):
            pe.begin(eng)
            eng.wait_ge(keep["constants_ready"], keep["constants"])
            eng.wait_ge(weights_loaded, 64)

            def tile(t, slot, j):
                eng.wait_ge(x_loaded[slot], 16 * (j + 1))
                for half in (0, 1):
                    eng.wait_ge(*act.after(f"xT{half}", t - 1))
                    for k in range(4):
                        c = half * 4 + k
                        mm = eng.transpose(X[half][:, k * P:(k + 1) * P], x[:, slot, c:D:KD], keep["ident"][:, :])
                    mm.then_inc(*pe.done(f"xT{half}"))
                eng.wait_ge(*act.after("xT1", t))
                for name, a, n, out, owner in (("f", 3 * DG, HEADS, S[:, 0:HEADS], (dve, "fb")),
                                               ("q", 0, DG, Q[:, :], (act, "q")),
                                               ("k", DG, DG, K[:, :], (act, "k")),
                                               ("v", 2 * DG, DG, V[:, :], (act, "v")),
                                               ("g", 3 * DG + HEADS, DG, G[:, :], (act, "g"))):
                    if name == "f":
                        eng.wait_ge(*dve.after("cT", t - 1))
                    else:
                        eng.wait_ge(*owner[0].after(owner[1], t - 1))
                    for k in range(KD):
                        mm = eng.matmul(out, xT[:, k, :], w[:, k, a:a + n], start=(k == 0), stop=(k == KD - 1))
                    mm.then_inc(*pe.done(name))
                eng.wait_ge(*dve.after("logf", t))
                eng.matmul(S[:, 8:16], keep["upto"][:, :], lf[:, slot, :], start=True, stop=True)
                eng.matmul(S[:, 16:24], keep["ones"][:, :], lf[:, slot, :], start=True, stop=True)\
                   .then_inc(*pe.done("cum"))
                eng.wait_ge(*dve.after("q2", t))
                eng.wait_ge(*dve.after("kT", t - 1))
                for a in range(PAIRS):
                    mm = eng.transpose(T[:, a * P:(a + 1) * P], qn[:, a * P:(a + 1) * P], keep["ident"][:, :])
                mm.then_inc(*pe.done("qT"))
                eng.wait_ge(*dve.after("k2", t))
                eng.wait_ge(*act.after("qT", t))
                for a in range(PAIRS):
                    mm = eng.transpose(T[:, a * P:(a + 1) * P], kn[:, slot, a * P:(a + 1) * P], keep["ident"][:, :])
                mm.then_inc(*pe.done("kT"))
                eng.wait_ge(*dve.after("negc", t))
                eng.transpose(S[0:HEADS, 128:128 + P], negc[:, :], keep["ident"][:, :]).then_inc(*pe.done("cT"))

            over_tiles(eng, tile)

        @block.scalar
        def _(eng):
            act.begin(eng)

            def tile(t, slot, j):
                for half in (0, 1):
                    eng.wait_ge(*pe.after(f"xT{half}", t))
                    eng.wait_ge(*pe.after("g", t - 1))
                    eng.copy(xT[:, half * 4:half * 4 + 4, :], X[half][:, :].rearrange("p (k t) -> p k t", k=4))\
                       .then_inc(*act.done(f"xT{half}"))
                eng.wait_ge(*dve.after("negabs", t))
                eng.activation(fb[:, 2, :], fb[:, 1, :], ACT.Exp).then_inc(*act.done("e"))
                eng.wait_ge(*act.after("e", t))
                eng.activation(fb[:, 3, :], fb[:, 2, :], ACT.Ln, bias=1.0).then_inc(*act.done("l"))
                for n, (name, bank) in enumerate((("q", Q), ("k", K))):
                    eng.wait_ge(*pe.after(name, t))
                    eng.wait_ge(*dve.after(f"{name}1", t - 1))
                    eng.copy(qk[:, n, :], bank[:, :]).then_inc(*act.done(name))
                eng.wait_ge(stored[slot], 16 * STORES * (j + 1))
                eng.wait_ge(*pe.after("v", t))
                eng.copy(vn[:, slot, :], V[:, :]).then_inc(*act.done("v"))
                eng.wait_ge(*pe.after("g", t))
                eng.activation(og[:, slot, :], G[:, :], ACT.Sigmoid).then_inc(*act.done("g"))
                eng.wait_ge(*dve.after("mean", t))
                eng.activation(ss[:, 1, :], ss[:, 0, :], ACT.Sqrt).then_inc(*act.done("rms"))
                eng.wait_ge(*pe.after("qT", t))
                eng.copy(qT[:, slot, :], T[:, :]).then_inc(*act.done("qT"))

            over_tiles(eng, tile)

        @block.vector
        def _(eng):
            dve.begin(eng)
            eng.memset(carry[:, :], 0.0).then_inc(carry_zeroed, 1)
            eng.wait_ge(carry_zeroed, 1)
            eng.wait_ge(weights_loaded, 64)
            eng.tensor_scalar(qg[:, :], qg[:, :], SCALE, None, ALU.mult).then_inc(carry_zeroed, 1)
            eng.wait_ge(carry_zeroed, 2)

            def tile(t, slot, j):
                eng.wait_ge(*pe.after("f", t))
                eng.tensor_tensor(fb[:, 0, :], S[:, 0:HEADS], bf[:, :], ALU.add).then_inc(*dve.done("fb"))
                eng.wait_ge(*dve.after("fb", t))
                eng.scalar_tensor_tensor(out=fb[:, 1, :], in0=fb[:, 0, :], scalar=-1.0, in1=fb[:, 0, :],
                                         op0=ALU.mult, op1=ALU.min)\
                   .then_inc(*dve.done("negabs"))
                eng.wait_ge(*act.after("l", t))
                eng.wait_ge(stored[slot], 16 * STORES * (j + 1))
                eng.scalar_tensor_tensor(out=lf[:, slot, :], in0=fb[:, 0, :], scalar=0.0, in1=fb[:, 3, :],
                                         op0=ALU.min, op1=ALU.subtract).then_inc(*dve.done("logf"))
                eng.wait_ge(*pe.after("cum", t))
                eng.wait_ge(*pe.after("cT", t - 1))
                eng.wait_ge(*dve.after("carry", t - 1))
                eng.scalar_tensor_tensor(out=negc[:, :], in0=S[:, 8:16], scalar=-1.0, in1=carry[:, :],
                                         op0=ALU.mult, op1=ALU.subtract).then_inc(*dve.done("negc"))
                eng.wait_ge(*dve.after("negc", t))
                eng.tensor_tensor(carry[:, :], S[:, 16:24], carry[:, :], ALU.add).then_inc(*dve.done("carry"))
                for n, name in enumerate("qk"):
                    eng.wait_ge(*act.after(name, t))
                    eng.tensor_tensor(sq[:, n, :], qk[:, n, :], qk[:, n, :], ALU.mult).then_inc(*dve.done(f"sq{n}"))
                    eng.wait_ge(*dve.after(f"sq{n}", t))
                    eng.tensor_reduce(ss[:, 0, n * HEADS:(n + 1) * HEADS],
                                      sq[:, n, :].rearrange("p (h d) -> p h d", d=DH), AX_X, ALU.add)\
                       .then_inc(*dve.done(f"ss{n}"))
                eng.wait_ge(*dve.after("ss1", t))
                eng.tensor_scalar(ss[:, 0, :], ss[:, 0, :], 1.0 / DH, QK_EPS, ALU.mult, ALU.add)\
                   .then_inc(*dve.done("mean"))
                eng.wait_ge(*act.after("rms", t))
                eng.reciprocal(ss[:, 2, :], ss[:, 1, :]).then_inc(*dve.done("rs"))
                eng.wait_ge(*dve.after("rs", t))
                eng.wait_ge(*pe.after("qT", t - 1))
                for n, (name, out, g) in enumerate((("q", qn[:, :], qg), ("k", kn[:, slot, :], kg))):
                    heads = out.rearrange("p (h d) -> p h d", d=DH)
                    rs = ss[:, 2, n * HEADS:(n + 1) * HEADS].unsqueeze(2).broadcast_to([P, HEADS, DH])
                    eng.tensor_tensor(heads, qk[:, n, :].rearrange("p (h d) -> p h d", d=DH), rs, ALU.mult)\
                       .then_inc(*dve.done(f"{name}1"))
                    eng.wait_ge(*dve.after(f"{name}1", t))
                    eng.tensor_tensor(heads, heads, g[:, :].unsqueeze(1).broadcast_to([P, HEADS, DH]), ALU.mult)\
                       .then_inc(*dve.done(f"{name}2"))
                eng.wait_ge(*pe.after("kT", t))
                eng.tensor_copy(kT[:, slot, :], T[:, :]).then_inc(*dve.done("kT"))
                eng.wait_ge(*pe.after("cT", t))
                eng.tensor_copy(cT[:, slot, :], S[0:HEADS, 128:128 + P]).then_inc(*dve.done("cT"))

            with eng.Fori(0, NT // 2) as j:
                for slot in (0, 1):
                    tile(2 * j + slot, slot, j)
            eng.wait_ge(*dve.after("carry", NT - 1))
            eng.memset(carry[:, :], 0.0).then_inc(carry_zeroed, 1)
            eng.wait_ge(carry_zeroed, 3)
            tile(NT, 0, NT // 2)
LEVELS = 7


def rwkv(nc, io, keep):
    with ExitStack() as ctx:
        def sb(name, shape, dt=F32):
            return ctx.enter_context(nc.sbuf_tensor(name, shape, dt))

        def sem(name):
            return ctx.enter_context(nc.semaphore(name))

        bank = [ctx.enter_context(nc.psum_tensor(f"rp{b}", [P, 512], F32)) for b in range(8)]
        w = sb("r_w", [P, KD, RCOLS])
        w2 = sb("r_w2", [P, DG])
        g2 = sb("r_g2", [P, DG])
        mu = sb("r_mu", [P, RCH])
        par = sb("r_par", [P, 7, PAIRS])
        one_ka = sb("r_one_ka", [P, PAIRS])
        x = sb("r_x", [P, 2, D])
        xT = sb("r_xT", [P, KD, P])
        pr = sb("r_pr", [P, RCH, P + 1])
        last = sb("r_last", [P, RCH])
        xs = sb("r_xs", [P, RCH, P])
        th = sb("r_th", [LORA, P])
        sg = sb("r_sg", [P, P])

        def quad(name, n=1):
            return sb(name, [P, PAIRS, n * P]) if n == 1 else sb(name, [P, PAIRS, n, P])

        ld, a, g, kk, sq, nrm, kf, beta = (quad("r_" + n) for n in ("ld", "a", "g", "kk", "sq", "nrm", "kf", "beta"))
        cum = sb("r_cum", [P, PAIRS, P + 1])
        e1 = sb("r_e1", [P, PAIRS, P + 1])
        e2, bt, kt, bv = (quad("r_" + n) for n in ("e2", "bt", "kt", "bv"))
        ar = quad("r_ar", 2)
        cm = sb("r_cm", [P, 3, PAIRS])
        vtok, btok, ktok = (quad("r_" + n) for n in ("vtok", "btok", "ktok"))
        mab = sb("r_mab", [P, 2, PAIRS, P])
        mrb = sb("r_mrb", [P, 2, PAIRS, P])
        mk = sb("r_mk", [P, 2, PAIRS, 2, P])
        X = sb("r_X", [P, 2, PAIRS, P])
        XT = sb("r_XT", [P, 2, PAIRS, P])
        t1 = sb("r_t1", [P, 2, PAIRS, P])
        rhs = sb("r_rhs", [P, 2, PAIRS, DH])
        sa = sb("r_sa", [P, 2, PAIRS, DH])
        st = sb("r_st", [P, PAIRS, DH])
        sbar = sb("r_sbar", [P, PAIRS, DH])
        y = quad("r_y")
        ysq = quad("r_ysq")
        ys = quad("r_ys")
        out = sb("r_out", [P, 2, PAIRS, P])
        io_st = sb("r_io_st", [DH, HEADS, DH])
        masks_f = sb("r_masks_f", [P, P])
        mask = sb("r_mask", [P, 2, LEVELS, P], I32)
        mask2 = sb("r_mask2", [P, 2, P])

        weights_loaded = sem("r_weights_loaded")
        x_loaded = [sem(f"r_x_loaded{s}") for s in (0, 1)]
        out_stored = [sem(f"r_out_stored{s}") for s in (0, 1)]
        masks_ready = sem("r_masks_ready")
        pad_zeroed = sem("r_pad_zeroed")
        prepared = sem("r_prepared")
        MASKS = 2 * LEVELS + 2
        cleared = sem("r_cleared")
        held = sem("r_held")
        state_pe, state_dve, state_dma = sem("r_state_pe"), sem("r_state_dve"), sem("r_state_dma")
        shift_dma = sem("r_shift_dma")

        uses = [("zw", 2, "act", "ld"), ("za", 3, "act", "a"), ("zg", 4, "act", "g"), ("ss", 5, "act", "nrm"),
                ("vT", 6, "act", "vT"), ("bs", 7, "dve", "bv"), ("bT", 6, "act", "bT"), ("kT", 7, "act", "kT"),
                ("mab0", 2, "dve", "x0_1"), ("mab1", 3, "dve", "x1_1"),
                ("mrb0", 4, "dve", "mrb0"), ("mrb1", 5, "dve", "mrb1"),
                ("mk00", 6, "dve", "mk00"), ("mk01", 7, "dve", "mk01"),
                ("t0_1", 2, "dve", "xT0_1"), ("t1_1", 3, "dve", "xT1_1"),
                ("mk10", 6, "dve", "mk10"), ("mk11", 7, "dve", "mk11")]
        for n in range(2, LEVELS + 1):
            uses += [(f"t0_{n}", 2, "act", f"t0_{n}"), (f"t1_{n}", 3, "act", f"t1_{n}")]
            for e in (0, 1):
                uses += [(f"ut{e}_{n}", 4 + e, "dve", f"xT{e}_{n}")]
                if n < LEVELS:
                    uses += [(f"u{e}_{n}", 6 + e, "dve", f"x{e}_{n}")]
        uses += [("rhs0", 2, "act", "rhs0"), ("rhs1", 3, "dve", "rhs1"), ("sa0", 4, "act", "sa0"),
                 ("sa1", 5, "dve", "sa1"), ("y0", 6, "act", "y0"), ("y1", 7, "act", "y1"), ("st", 2, "dve", "st1"),
                 ("mean", 3, "dve", "yc"), ("var", 4, "dve", "var")]
        pe = Steps(sem("r_pe_steps"), [u[0] for u in uses])
        act = Steps(sem("r_act_steps"), ["th", "sg", "ld", "a", "g", "nrm", "e1", "e2", "emid", "vT", "bT", "kT"]
                    + [f"t{e}_{n}" for n in range(2, LEVELS + 1) for e in (0, 1)]
                    + ["rhs0", "sa0", "y0", "y1", "std"])
        dve = Steps(sem("r_dve_steps"), [
            "head", "last", "diff", "mix", "xs", "kkr", "sq", "scan", "mid", "nmid", "nmax", "rn", "kk", "beta",
            "ka1", "ka2", "kf", "A", "R", "B", "K", "rk1", "rk2", "sbar", "bv"]
            + ["mab0", "x0_1", "mab1", "x1_1", "mrb0", "mrb1", "mk00", "mk01", "xT0_1", "xT1_1", "mk10", "mk11"]
            + [f"{k}{e}_{n}" for n in range(2, LEVELS + 1) for e in (0, 1) for k in ("xT", "x")
               if not (k == "x" and n == LEVELS)]
            + ["rhs1", "sa1", "st1", "st2", "yc", "ysq", "var", "rstd", "y1", "y2", "y3", "y4", "out"])
        pool = Steps(sem("r_pool_steps"), ["X", "XT"])
        ppe = Steps(sem("r_proj_pe_steps"), ["xT0", "xT1", "r", "k", "v", "l"])
        pact = Steps(sem("r_proj_act_steps"), ["xT0", "xT1", "r", "k", "v", "l"])
        engines = {"act": act, "dve": dve}

        def emptied(step, t):
            i = [u[0] for u in uses].index(step)
            b = uses[i][1]
            before = [u for u in uses[:i] if u[1] == b]
            u = before[-1] if before else [u for u in uses if u[1] == b][-1]
            return engines[u[2]].after(u[3], t if before else t - 1)

        def bank_of(step):
            return bank[[u[1] for u in uses if u[0] == step][0]]

        def four(b, n=P):
            return b[:, 0:PAIRS * n].rearrange("p (a t) -> p a t", a=PAIRS)

        def by_channel(ap):
            return ap.rearrange("o (c p) -> p (o c)", p=P)

        def over(ap, n=P):
            return ap.unsqueeze(2).broadcast_to([P, ap.shape[1], n])

        block = ctx.enter_context(nc.Block())

        @block.sync
        def _(sp):
            begin_stores(sp, out_stored)
            sp.dma_start(x[:, 0, :], io["x_prompt"][0, 0:P, :]).then_inc(x_loaded[0], 16)
            sp.dma_start(x[:, 1, :], io["x_prompt"][0, P:2 * P, :]).then_inc(x_loaded[1], 16)
            with nc.allow_non_contiguous_dma(reason="vectors of parameters, channels in rows"):
                loads = [(w[:, :, :], io["w_in"][0].rearrange("(p k) n -> p k n", k=KD)[:, :, 0:RCOLS]),
                         (w2[0:LORA, :], io["rwkv_w2"][0]), (w2[LORA:P, :], io["rwkv_a2"][0]),
                         (g2[:, :], io["rwkv_g2"][0]), (mu[:, :], by_channel(io["rwkv_mu"]))]
                for n, name in enumerate(("w0", "a0", "k_k", "k_a", "r_k", "lnx_w", "lnx_b")):
                    v = io["rwkv_" + name]
                    v = v.rearrange("o h d -> o (h d)") if name == "r_k" else v
                    loads.append((par[:, n, :], by_channel(v)))
                for dst, src in loads:
                    sp.dma_start(dst, src).then_inc(weights_loaded, 16)

            def store(t, slot):
                sp.wait_ge(*dve.after("out", t))
                sp.dma_start(io["ryT"][:, :, bass.ds(t * P, P)].rearrange("a p t -> p a t"), out[:, slot, :, :])\
                  .then_inc(out_stored[slot], 16)

            with sp.Fori(0, NT // 2 - 1) as j:
                for slot in (0, 1):
                    t = 2 * j + slot
                    sp.wait_ge(*ppe.after("xT1", t))
                    sp.dma_start(x[:, slot, :], io["x_prompt"][0, bass.ds((t + 2) * P, P), :])\
                      .then_inc(x_loaded[slot], 16)
                    store(t, slot)
            sp.wait_ge(pad_zeroed, 1)
            sp.dma_start(x[0:NEW, 0, :], io["x_sample"][0]).then_inc(x_loaded[0], 16)
            store(NT - 2, 0)
            with nc.allow_non_contiguous_dma(reason="one frame, channels in rows"):
                sp.wait_ge(*dve.after("last", NT - 1))
                sp.dma_start(by_channel(io["p_shift"]), last[:, :]).then_inc(shift_dma, 16)
                sp.wait_ge(shift_dma, 16)
                sp.dma_start(last[:, :], by_channel(io["state_rwkv_shift"][0, 0])).then_inc(shift_dma, 16)
                store(NT - 1, 1)
                sp.wait_ge(state_dve, 1)
                sp.dma_start(io["p_rwkv"].rearrange("h v k -> v h k"), io_st[:, :, :]).then_inc(state_dma, 16)
                sp.wait_ge(state_dma, 16)
                sp.dma_start(io_st[:, :, :], io["state_rwkv"][0, 0].rearrange("h v k -> v h k"))\
                  .then_inc(state_dma, 16)
                sp.wait_ge(*pact.after("l", NT))
                sp.dma_start(by_channel(io["s_shift"]), pr[:, :, NEW]).then_inc(shift_dma, 16)
                store(NT, 0)
                sp.wait_ge(state_dve, 3)
                sp.dma_start(io["s_rwkv"].rearrange("h v k -> v h k"), io_st[:, :, :]).then_inc(state_dma, 16)
            sp.wait_ge(shift_dma, 48)
            sp.wait_ge(state_dma, 48)
            sp.wait_ge(out_stored[0], 16 * (NT // 2 + 2))
            sp.wait_ge(out_stored[1], 16 * (NT // 2 + 1))

        @block.gpsimd
        def _(eng):
            pool.begin(eng)
            n = 0
            for turned in (0, 1):
                for level in range(LEVELS):
                    s = 1 << level
                    if n:
                        eng.wait_ge(prepared, n)
                    eng.memset(masks_f[:, :], 0.0).then_inc(masks_ready, 1)
                    eng.wait_ge(masks_ready, 5 * n + 1)
                    cols = masks_f[:, :].rearrange("p (b h i) -> p b h i", h=2, i=s)[:, :, turned, :]
                    nb = P // (2 * s)
                    eng.memset(cols, 1.0).then_inc(masks_ready, 1)
                    eng.wait_ge(masks_ready, 5 * n + 2)
                    low = 0 if turned else s
                    eng.affine_select(out=cols, in_=cols, compare_op=ALU.is_ge, fill=0.0, base=-low,
                                      pattern=[[-2 * s, nb], [0, s]], channel_multiplier=1).then_inc(masks_ready, 1)
                    eng.wait_ge(masks_ready, 5 * n + 3)
                    eng.affine_select(out=cols, in_=cols, compare_op=ALU.is_ge, fill=0.0, base=low + s - 1,
                                      pattern=[[2 * s, nb], [0, s]], channel_multiplier=-1).then_inc(masks_ready, 2)
                    n += 1

            def tile(t, slot, j):
                eng.wait_ge(*pe.after(f"ut1_{LEVELS}", t - 1))
                hold(eng, held)
                eng.tensor_copy(X[:, :, :, :].rearrange("p e a t -> p (e a) t"),
                                keep["ident"][:, :].unsqueeze(1).broadcast_to([P, HEADS, P]))\
                   .then_inc(*pool.done("X"))
                eng.wait_ge(*pe.after("sa1", t - 1))
                hold(eng, held)
                eng.tensor_copy(XT[:, :, :, :].rearrange("p e a t -> p (e a) t"),
                                keep["ident"][:, :].unsqueeze(1).broadcast_to([P, HEADS, P]))\
                   .then_inc(*pool.done("XT"))

            with eng.Fori(0, NT // 2 - 1) as j:
                for slot in (0, 1):
                    tile(2 * j + slot, slot, j)
            eng.wait_ge(*ppe.after("xT1", NT - 2))
            eng.memset(x[:, 0, :], 0.0).then_inc(pad_zeroed, 1)
            for t in (NT - 2, NT - 1, NT):
                tile(t, t % 2, t // 2)

        @block.tensor
        def _(eng):
            pe.begin(eng)
            ppe.begin(eng)
            eng.wait_ge(keep["constants_ready"], keep["constants"])
            eng.wait_ge(weights_loaded, 16 * 12)
            eng.wait_ge(prepared, MASKS)
            ident = keep["ident"][:, :]

            def project_x(u, slot, turn):
                eng.wait_ge(x_loaded[slot], 16 * (turn + 1))
                for half in (0, 1):
                    eng.wait_ge(*pact.after("vl"[half], u - 1))
                    for k in range(4):
                        mm = eng.transpose(bank[half][:, k * P:(k + 1) * P], x[:, slot, half * 4 + k:D:KD], ident)
                    mm.then_inc(*ppe.done(f"xT{half}"))

            def project(u, name):
                n = "rkvl".index(name)
                eng.wait_ge(*pact.after(("xT1", "xT1", "r", "k")[n], u))
                b = four(bank[n % 2])
                for f in range(4 if n < 3 else 2):
                    c = (4 * n + f) * P
                    for k in range(KD):
                        mm = eng.matmul(b[:, f, :], w[:, k, c:c + P], xT[:, k, :], start=(k == 0), stop=(k == KD - 1))
                mm.then_inc(*ppe.done(name))

            def half_of(e):
                return slice(e * DH, (e + 1) * DH)

            def tile(t, slot, j, following=True):
                def start(step):
                    eng.wait_ge(*emptied(step, t))
                    return bank_of(step)

                if following:
                    project_x(t + 1, 1 - slot, j + slot)
                    project(t + 1, "r")
                b = four(start("zw"))
                eng.wait_ge(*act.after("th", t))
                for p in range(PAIRS):
                    mm = eng.matmul(b[:, p, :], w2[0:LORA, p * P:(p + 1) * P], th[:, :], start=True, stop=True)
                mm.then_inc(*pe.done("zw"))
                b = four(start("za"))
                for p in range(PAIRS):
                    mm = eng.matmul(b[:, p, :], w2[LORA:P, p * P:(p + 1) * P], xs[LORA:P, 12, :], start=True, stop=True)
                mm.then_inc(*pe.done("za"))
                b = four(start("zg"))
                eng.wait_ge(*act.after("sg", t))
                for p in range(PAIRS):
                    mm = eng.matmul(b[:, p, :], g2[:, p * P:(p + 1) * P], sg[:, :], start=True, stop=True)
                mm.then_inc(*pe.done("zg"))
                if following:
                    project(t + 1, "k")
                b = start("ss")
                eng.wait_ge(*dve.after("sq", t))
                eng.matmul(b[:, :], keep["halves"][:, :], sq[:, :, :].rearrange("p a t -> p (a t)"), start=True, stop=True)\
                   .then_inc(*pe.done("ss"))
                if following:
                    project(t + 1, "v")
                b = start("vT")
                for p in range(PAIRS):
                    mm = eng.transpose(b[:, p * P:(p + 1) * P], xs[:, 8 + p, :], ident)
                mm.then_inc(*pe.done("vT"))
                if following:
                    project(t + 1, "l")
                b = start("bs")
                eng.wait_ge(*dve.after("rk2", t))
                eng.matmul(b[:, :], keep["halves"][:, :], sq[:, :, :].rearrange("p a t -> p (a t)"), start=True, stop=True)\
                   .then_inc(*pe.done("bs"))
                for name, src in (("bT", bt), ("kT", kt)):
                    b = start(name)
                    for p in range(PAIRS):
                        mm = eng.transpose(b[:, p * P:(p + 1) * P], src[:, p, :], ident)
                    mm.then_inc(*pe.done(name))
                for e in (0, 1):
                    h = half_of(e)
                    b = four(start(f"mab{e}"))
                    for p in range(PAIRS):
                        mm = eng.matmul(b[:, p, :], ar[h, p, 0, :], bt[h, p, :], start=True, stop=True)
                    mm.then_inc(*pe.done(f"mab{e}"))
                for e in (0, 1):
                    h = half_of(e)
                    b = four(start(f"mrb{e}"))
                    for p in range(PAIRS):
                        mm = eng.matmul(b[:, p, :], bt[h, p, :], ar[h, p, 1, :], start=True, stop=True)
                    mm.then_inc(*pe.done(f"mrb{e}"))

                def mk_products(e):
                    h = half_of(e)
                    for n in (0, 1):
                        b = start(f"mk{e}{n}")
                        for i in (0, 1):
                            p = 2 * n + i
                            mm = eng.matmul(b[:, i * 2 * P:(i + 1) * 2 * P], kt[h, p, :],
                                            ar[h, p, :, :].rearrange("p a t -> p (a t)"), start=True, stop=True)
                        mm.then_inc(*pe.done(f"mk{e}{n}"))

                mk_products(0)
                for e in (0, 1):
                    b = four(start(f"t{e}_1"))
                    eng.wait_ge(*dve.after(f"mab{e}", t))
                    for p in range(PAIRS):
                        mm = eng.matmul(b[:, p, :], mab[:, e, p, :], ident, start=True, stop=True)
                    mm.then_inc(*pe.done(f"t{e}_1"))
                mk_products(1)
                for n in range(2, LEVELS + 1):
                    for e in (0, 1):
                        b = four(start(f"t{e}_{n}"))
                        eng.wait_ge(*dve.after(f"xT{e}_{n - 1}", t))
                        for p in range(PAIRS):
                            mm = eng.matmul(b[:, p, :], mab[:, e, p, :], XT[:, e, p, :], start=True, stop=True)
                        mm.then_inc(*pe.done(f"t{e}_{n}"))
                    for e in (0, 1):
                        b = four(start(f"ut{e}_{n}"))
                        eng.wait_ge(*dve.after(f"x{e}_{n - 1}", t))
                        eng.wait_ge(*act.after(f"t{e}_{n}", t))
                        for p in range(PAIRS):
                            mm = eng.matmul(b[:, p, :], X[:, e, p, :], t1[:, e, p, :], start=True, stop=True)
                        mm.then_inc(*pe.done(f"ut{e}_{n}"))
                        if n < LEVELS:
                            b = four(start(f"u{e}_{n}"))
                            for p in range(PAIRS):
                                mm = eng.matmul(b[:, p, :], t1[:, e, p, :], X[:, e, p, :], start=True, stop=True)
                            mm.then_inc(*pe.done(f"u{e}_{n}"))
                for e in (0, 1):
                    h = half_of(e)
                    b = four(start(f"rhs{e}"), DH)
                    eng.wait_ge(*dve.after("sbar", t))
                    for p in range(PAIRS):
                        eng.matmul(b[:, p, :], ar[h, p, 0, :], sbar[h, p, :], start=True, stop=False)
                        mm = eng.matmul(b[:, p, :], mk[:, e, p, 0, :], vtok[:, p, h], start=False, stop=True)
                    mm.then_inc(*pe.done(f"rhs{e}"))
                for e in (0, 1):
                    b = four(start(f"sa{e}"), DH)
                    eng.wait_ge(*(act, dve)[e].after(f"rhs{e}", t))
                    eng.wait_ge(*dve.after(f"xT{e}_{LEVELS}", t))
                    for p in range(PAIRS):
                        mm = eng.matmul(b[:, p, :], XT[:, e, p, :], rhs[:, e, p, :], start=True, stop=True)
                    mm.then_inc(*pe.done(f"sa{e}"))
                for e in (0, 1):
                    h = half_of(e)
                    b = four(start(f"y{e}"))
                    eng.wait_ge(*(act, dve)[e].after(f"sa{e}", t))
                    for p in range(PAIRS):
                        eng.matmul(b[h, p, :], sa[:, e, p, :], mrb[:, e, p, :], start=True, stop=False)
                        eng.matmul(b[h, p, :], sbar[h, p, :], ar[h, p, 1, :], start=False, stop=False)
                        mm = eng.matmul(b[h, p, :], vtok[:, p, h], mk[:, e, p, 1, :], start=False, stop=True)
                    mm.then_inc(*pe.done(f"y{e}"))
                b = four(start("st"), DH)
                for e in (0, 1):
                    h = half_of(e)
                    for p in range(PAIRS):
                        eng.matmul(b[h, p, :], btok[:, p, h], sa[:, e, p, :], start=True, stop=False)
                        mm = eng.matmul(b[h, p, :], ktok[:, p, h], vtok[:, p, h], start=False, stop=True)
                mm.then_inc(*pe.done("st"))
                b = start("mean")
                eng.wait_ge(*act.after("y1", t))
                eng.matmul(b[:, :], keep["halves"][:, :], y[:, :, :].rearrange("p a t -> p (a t)"), start=True, stop=True)\
                   .then_inc(*pe.done("mean"))
                b = start("var")
                eng.wait_ge(*dve.after("ysq", t))
                eng.matmul(b[:, :], keep["halves"][:, :], ysq[:, :, :].rearrange("p a t -> p (a t)"), start=True, stop=True)\
                   .then_inc(*pe.done("var"))

            project_x(0, 0, 0)
            for name in "rkvl":
                project(0, name)
            with eng.Fori(0, NT // 2) as j:
                for slot in (0, 1):
                    tile(2 * j + slot, slot, j)

            def state_out():
                for p in range(PAIRS):
                    mm = eng.transpose(bank[5][0:DH, p * P:(p + 1) * P], st[:, p, :], ident)
                mm.then_inc(state_pe, 1)

            eng.wait_ge(*dve.after("st2", NT - 1))
            state_out()
            eng.wait_ge(state_dma, 32)
            for p in range(PAIRS):
                mm = eng.transpose(bank[6][:, p * DH:(p + 1) * DH],
                                   io_st[:, 2 * p:2 * p + 2, :].rearrange("v h k -> v (h k)"), ident[0:DH, 0:DH])
            mm.then_inc(state_pe, 1)
            eng.wait_ge(state_dve, 2)
            tile(NT, 0, NT // 2, following=False)
            eng.wait_ge(*dve.after("st2", NT))
            state_out()

        @block.scalar
        def _(eng):
            act.begin(eng)
            pact.begin(eng)

            def project_x(u):
                for half in (0, 1):
                    eng.wait_ge(*ppe.after(f"xT{half}", u))
                    eng.copy(xT[:, half * 4:half * 4 + 4, :], four(bank[half])).then_inc(*pact.done(f"xT{half}"))

            def project(u, name):
                n = "rkvl".index(name)
                eng.wait_ge(*ppe.after(name, u))
                eng.wait_ge(*dve.after("xs", u - 1))
                m = 4 if n < 3 else 2
                eng.copy(pr[:, 4 * n:4 * n + m, 1:P + 1], four(bank[n % 2])[:, 0:m, :]).then_inc(*pact.done(name))

            def tile(t, slot, j, following=True):
                if following:
                    project_x(t + 1)
                eng.wait_ge(*dve.after("xs", t))
                eng.wait_ge(*pe.after("zw", t - 1))
                eng.activation(th[:, :], xs[0:LORA, 12, :], ACT.Tanh).then_inc(*act.done("th"))
                eng.wait_ge(*pe.after("zg", t - 1))
                eng.activation(sg[:, :], xs[:, 13, :], ACT.Sigmoid).then_inc(*act.done("sg"))
                for name, dst, n, readers in (("ld", ld, 0, "scan"), ("a", a, 1, "ka1")):
                    eng.wait_ge(*pe.after({"ld": "zw", "a": "za"}[name], t))
                    eng.wait_ge(*dve.after(readers, t - 1))
                    for p in range(PAIRS):
                        ins = eng.activation(dst[:, p, :], four(bank_of({"ld": "zw", "a": "za"}[name]))[:, p, :],
                                             ACT.Sigmoid, bias=par[:, n, p:p + 1])
                    ins.then_inc(*act.done(name))
                eng.wait_ge(*pe.after("zg", t))
                eng.wait_ge(*dve.after("out", t - 1))
                eng.copy(g[:, :, :], four(bank_of("zg"))).then_inc(*act.done("g"))
                if following:
                    project(t + 1, "r")
                eng.wait_ge(*pe.after("ss", t))
                eng.wait_ge(*dve.after("rn", t - 1))
                eng.activation(nrm[:, :, :], four(bank_of("ss")), ACT.Sqrt).then_inc(*act.done("nrm"))
                if following:
                    project(t + 1, "k")
                eng.wait_ge(*dve.after("nmid", t))
                eng.wait_ge(*dve.after("st2", t - 1))
                for p in range(PAIRS):
                    ins = eng.activation(e1[:, p, :], cum[:, p, :], ACT.Exp, scale=-DECAY, bias=cm[:, 0, p:p + 1])
                ins.then_inc(*act.done("e1"))
                for p in range(PAIRS):
                    ins = eng.activation(e2[:, p, :], cum[:, p, 1:P + 1], ACT.Exp, scale=DECAY, bias=cm[:, 1, p:p + 1])
                ins.then_inc(*act.done("e2"))
                eng.activation(cm[:, 2, :], cm[:, 1, :], ACT.Exp).then_inc(*act.done("emid"))
                if following:
                    project(t + 1, "v")
                eng.wait_ge(*pe.after("vT", t))
                eng.wait_ge(*pe.after("st", t - 1))
                eng.copy(vtok[:, :, :], four(bank_of("vT"))).then_inc(*act.done("vT"))
                if following:
                    project(t + 1, "l")
                for name, dst in (("bT", btok), ("kT", ktok)):
                    eng.wait_ge(*pe.after(name, t))
                    eng.copy(dst[:, :, :], four(bank_of(name))).then_inc(*act.done(name))
                for n in range(2, LEVELS + 1):
                    for e in (0, 1):
                        eng.wait_ge(*pe.after(f"t{e}_{n}", t))
                        eng.wait_ge(*pe.after(f"u{e}_{n - 1}", t) if n > 2 else pe.after(f"ut{e}_{LEVELS}", t - 1))
                        eng.copy(t1[:, e, :, :], four(bank_of(f"t{e}_{n}"))).then_inc(*act.done(f"t{e}_{n}"))
                eng.wait_ge(*pe.after("rhs0", t))
                eng.copy(rhs[:, 0, :, :], four(bank_of("rhs0"), DH)).then_inc(*act.done("rhs0"))
                eng.wait_ge(*pe.after("sa0", t))
                eng.copy(sa[:, 0, :, :], four(bank_of("sa0"), DH)).then_inc(*act.done("sa0"))
                for e in (0, 1):
                    h = slice(e * DH, (e + 1) * DH)
                    eng.wait_ge(*pe.after(f"y{e}", t))
                    eng.wait_ge(*dve.after("yc", t - 1))
                    eng.copy(y[h, :, :], four(bank_of(f"y{e}"))[h, :, :]).then_inc(*act.done(f"y{e}"))
                eng.wait_ge(*dve.after("var", t))
                eng.activation(ysq[:, :, :], ys[:, :, :], ACT.Sqrt).then_inc(*act.done("std"))

            project_x(0)
            for name in "rkvl":
                project(0, name)
            with eng.Fori(0, NT // 2) as j:
                for slot in (0, 1):
                    tile(2 * j + slot, slot, j)
            tile(NT, 0, NT // 2, following=False)

        @block.vector
        def _(eng):
            n = 0
            for turned in (0, 1):
                for level in range(LEVELS):
                    eng.wait_ge(masks_ready, 5 * (n + 1))
                    eng.tensor_copy(mask[:, turned, level, :], masks_f[:, :]).then_inc(prepared, 1)
                    n += 1
            eng.wait_ge(keep["constants_ready"], keep["constants"])
            eng.tensor_copy(mask2[:, 0, :], keep["before"][:, :])
            eng.tensor_copy(mask2[:, 1, :], keep["upto"][:, :])
            eng.memset(cum[:, :, 0:1], 0.0)
            eng.memset(last[:, :], 0.0)
            eng.memset(st[:, :, :], 0.0)
            eng.wait_ge(weights_loaded, 16 * 12)
            eng.tensor_scalar(one_ka[:, :], par[:, 3, :], -1.0, 1.0, ALU.mult, ALU.add).then_inc(prepared, 2)
            eng.wait_ge(prepared, MASKS)
            dve.begin(eng)

            def chained(*step_t):
                eng.wait_ge(*dve.after(*step_t))

            def tt(name, out_, a_, b_, op, t):
                eng.tensor_tensor(out_, a_, b_, op).then_inc(*dve.done(name))

            def heads4(ap):
                return ap.unsqueeze(1).broadcast_to([P, PAIRS, P])

            def tile(t, slot, j, final=False):
                chained("last", t - 1)
                chained("xs", t - 1)
                if final:
                    eng.wait_ge(shift_dma, 32)
                eng.tensor_copy(pr[:, :, 0:1], last[:, :].unsqueeze(2)).then_inc(*dve.done("head"))
                chained("head", t)
                eng.wait_ge(*pact.after("l", t))
                eng.tensor_copy(last[:, :].unsqueeze(2), pr[:, :, P:P + 1]).then_inc(*dve.done("last"))
                eng.wait_ge(*pe.after("vT", t - 1))
                chained("bv", t - 1)
                tt("diff", xs[:, :, :], pr[:, :, 0:P], pr[:, :, 1:P + 1], ALU.subtract, t)
                chained("diff", t)
                tt("mix", xs[:, :, :], xs[:, :, :], over(mu[:, :]), ALU.mult, t)
                chained("mix", t)
                tt("xs", xs[:, :, :], xs[:, :, :], pr[:, :, 1:P + 1], ALU.add, t)
                chained("xs", t)
                xr, xk, xv = xs[:, 0:4, :], xs[:, 4:8, :], xs[:, 8:12, :]
                eng.wait_ge(*pe.after("bs", t - 1))
                tt("kkr", kk[:, :, :], xk, over(par[:, 2, :]), ALU.mult, t)
                chained("kkr", t)
                tt("sq", sq[:, :, :], kk[:, :, :], kk[:, :, :], ALU.mult, t)
                eng.wait_ge(*act.after("ld", t))
                if final:
                    eng.memset(ld[:, :, NEW:P], 0.0).then_inc(cleared, 1)
                    eng.wait_ge(cleared, 1)
                for p in range(PAIRS):
                    ins = eng.tensor_tensor_scan(out=cum[:, p, 1:P + 1], data0=keep["ones"][:, :], data1=ld[:, p, :],
                                                 initial=0.0, op0=ALU.mult, op1=ALU.add)
                ins.then_inc(*dve.done("scan"))
                chained("scan", t)
                eng.tensor_scalar(cm[:, 0, :], cum[:, :, DH], DECAY, None, ALU.mult).then_inc(*dve.done("mid"))
                eng.tensor_scalar(cm[:, 1, :], cum[:, :, DH], -DECAY, None, ALU.mult).then_inc(*dve.done("nmid"))
                eng.wait_ge(*act.after("nrm", t))
                eng.tensor_scalar(nrm[:, :, :], nrm[:, :, :], 1e-12, None, ALU.max).then_inc(*dve.done("nmax"))
                chained("nmax", t)
                eng.reciprocal(nrm[:, :, :], nrm[:, :, :]).then_inc(*dve.done("rn"))
                chained("rn", t)
                tt("kk", kk[:, :, :], kk[:, :, :], nrm[:, :, :], ALU.mult, t)
                chained("kk", t)
                eng.wait_ge(*act.after("a", t))
                tt("beta", beta[:, :, :], kk[:, :, :], a[:, :, :], ALU.mult, t)
                chained("beta", t)
                tt("ka1", kf[:, :, :], a[:, :, :], over(par[:, 3, :]), ALU.mult, t)
                chained("ka1", t)
                tt("ka2", kf[:, :, :], kf[:, :, :], over(one_ka[:, :]), ALU.add, t)
                chained("ka2", t)
                tt("kf", kf[:, :, :], kf[:, :, :], xk, ALU.mult, t)
                chained("kf", t)
                if final:
                    eng.memset(kf[:, :, NEW:P], 0.0).then_inc(cleared, 1)
                    eng.memset(beta[:, :, NEW:P], 0.0).then_inc(cleared, 1)
                    eng.wait_ge(cleared, 3)
                eng.wait_ge(*act.after("emid", t))
                eng.wait_ge(*pe.after("y1", t - 1))
                eng.scalar_tensor_tensor(out=ar[:, :, 0, :], in0=kk[:, :, :], scalar=-1.0, in1=e1[:, :, 0:P],
                                         op0=ALU.mult, op1=ALU.mult).then_inc(*dve.done("A"))
                tt("R", ar[:, :, 1, :], xr, e1[:, :, 1:P + 1], ALU.mult, t)
                tt("B", bt[:, :, :], beta[:, :, :], e2[:, :, :], ALU.mult, t)
                tt("K", kt[:, :, :], kf[:, :, :], e2[:, :, :], ALU.mult, t)
                eng.wait_ge(*pe.after("ss", t))
                tt("rk1", sq[:, :, :], xr, kf[:, :, :], ALU.mult, t)
                chained("rk1", t)
                tt("rk2", sq[:, :, :], sq[:, :, :], over(par[:, 4, :]), ALU.mult, t)
                if final:
                    eng.wait_ge(state_dve, 2)
                chained("st2", t - 1)
                tt("sbar", sbar[:, :, :], st[:, :, :], over(cm[:, 2, :], DH), ALU.mult, t)
                chained("out", t - 1)
                eng.wait_ge(*pe.after("bs", t))
                tt("bv", bv[:, :, :], four(bank_of("bs")), xv, ALU.mult, t)
                for e in (0, 1):
                    eng.wait_ge(*pe.after(f"mab{e}", t))
                    b = four(bank_of(f"mab{e}"))
                    eng.wait_ge(*pe.after(f"t{e}_{LEVELS}", t - 1))
                    tt(f"mab{e}", mab[:, e, :, :], b, heads4(keep["after"][:, :]), ALU.mult, t)
                    eng.wait_ge(*pool.after("X", t))
                    hold(eng, held)
                    eng.copy_predicated(X[:, e, :, :], heads4(mask[:, 0, 0, :]), b).then_inc(*dve.done(f"x{e}_1"))
                for e in (0, 1):
                    eng.wait_ge(*pe.after(f"mrb{e}", t))
                    tt(f"mrb{e}", mrb[:, e, :, :], four(bank_of(f"mrb{e}")), heads4(keep["upto"][:, :]), ALU.mult, t)

                def mk_masked(e):
                    for n in (0, 1):
                        eng.wait_ge(*pe.after(f"mk{e}{n}", t))
                        tt(f"mk{e}{n}", mk[:, e, 2 * n:2 * n + 2, :, :].rearrange("p a b t -> p a (b t)"),
                           bank_of(f"mk{e}{n}")[:, :].rearrange("p (a x) -> p a x", a=2),
                           mask2[:, :, :].rearrange("p b t -> p (b t)").unsqueeze(1).broadcast_to([P, 2, 2 * P]),
                           ALU.mult, t)

                mk_masked(0)
                eng.wait_ge(*pool.after("XT", t))
                for e in (0, 1):
                    eng.wait_ge(*pe.after(f"t{e}_1", t))
                    hold(eng, held)
                    eng.copy_predicated(XT[:, e, :, :], heads4(mask[:, 1, 0, :]), four(bank_of(f"t{e}_1")))\
                       .then_inc(*dve.done(f"xT{e}_1"))
                mk_masked(1)
                for n in range(2, LEVELS + 1):
                    for e in (0, 1):
                        eng.wait_ge(*pe.after(f"ut{e}_{n}", t))
                        hold(eng, held)
                        eng.copy_predicated(XT[:, e, :, :], heads4(mask[:, 1, n - 1, :]), four(bank_of(f"ut{e}_{n}")))\
                           .then_inc(*dve.done(f"xT{e}_{n}"))
                        if n < LEVELS:
                            eng.wait_ge(*pe.after(f"u{e}_{n}", t))
                            hold(eng, held)
                            eng.copy_predicated(X[:, e, :, :], heads4(mask[:, 0, n - 1, :]),
                                                four(bank_of(f"u{e}_{n}"))).then_inc(*dve.done(f"x{e}_{n}"))
                eng.wait_ge(*pe.after("rhs1", t))
                eng.tensor_copy(rhs[:, 1, :, :], four(bank_of("rhs1"), DH)).then_inc(*dve.done("rhs1"))
                eng.wait_ge(*pe.after("sa1", t))
                eng.tensor_copy(sa[:, 1, :, :], four(bank_of("sa1"), DH)).then_inc(*dve.done("sa1"))
                eng.wait_ge(*pe.after("st", t))
                tt("st1", st[:, :, :], four(bank_of("st"), DH), sbar[:, :, :], ALU.add, t)
                chained("st1", t)
                tt("st2", st[:, :, :], st[:, :, :], e1[:, :, P:P + 1].broadcast_to([P, PAIRS, DH]), ALU.mult, t)
                eng.wait_ge(*pe.after("mean", t))
                eng.scalar_tensor_tensor(out=y[:, :, :], in0=four(bank_of("mean")), scalar=-1.0 / DH, in1=y[:, :, :],
                                         op0=ALU.mult, op1=ALU.add).then_inc(*dve.done("yc"))
                chained("yc", t)
                tt("ysq", ysq[:, :, :], y[:, :, :], y[:, :, :], ALU.mult, t)
                eng.wait_ge(*pe.after("var", t))
                eng.tensor_scalar(ys[:, :, :], four(bank_of("var")), 1.0 / DH, GN_EPS, ALU.mult, ALU.add)\
                   .then_inc(*dve.done("var"))
                eng.wait_ge(*act.after("std", t))
                eng.reciprocal(ys[:, :, :], ysq[:, :, :]).then_inc(*dve.done("rstd"))
                chained("rstd", t)
                tt("y1", ys[:, :, :], ys[:, :, :], y[:, :, :], ALU.mult, t)
                chained("y1", t)
                tt("y2", ys[:, :, :], ys[:, :, :], over(par[:, 5, :]), ALU.mult, t)
                chained("y2", t)
                tt("y3", ys[:, :, :], ys[:, :, :], over(par[:, 6, :]), ALU.add, t)
                chained("y3", t)
                tt("y4", ys[:, :, :], ys[:, :, :], bv[:, :, :], ALU.add, t)
                chained("y4", t)
                eng.wait_ge(*act.after("g", t))
                eng.wait_ge(out_stored[slot], 16 * (j + 1))
                tt("out", out[:, slot, :, :], ys[:, :, :], g[:, :, :], ALU.mult, t)

            with eng.Fori(0, NT // 2) as j:
                for slot in (0, 1):
                    tile(2 * j + slot, slot, j)
            eng.wait_ge(state_pe, 1)
            eng.tensor_copy(io_st[:, :, :], bank[5][0:DH, :].rearrange("v (h k) -> v h k", h=HEADS))\
               .then_inc(state_dve, 1)
            eng.wait_ge(state_pe, 2)
            eng.tensor_copy(st[:, :, :], bank[6][:, 0:PAIRS * DH].rearrange("p (a v) -> p a v", a=PAIRS))\
               .then_inc(state_dve, 1)
            tile(NT, 0, NT // 2, final=True)
            eng.wait_ge(state_pe, 3)
            eng.tensor_copy(io_st[:, :, :], bank[5][0:DH, :].rearrange("v (h k) -> v h k", h=HEADS))\
               .then_inc(state_dve, 1)
def fox_prompt(nc, io, keep):
    with ExitStack() as ctx:
        def sb(name, shape, dt=F32):
            return ctx.enter_context(nc.sbuf_tensor(name, shape, dt))

        def sem(name):
            return ctx.enter_context(nc.semaphore(name))

        logits = ctx.enter_context(nc.psum_tensor("a_logits", [P, SEQ], F32))
        turned = [ctx.enter_context(nc.psum_tensor(f"a_turned{b}", [P, 512], F32)) for b in range(2)]
        o = [ctx.enter_context(nc.psum_tensor(f"a_o{b}", [P, 512], F32)) for b in range(2)]
        q = sb("a_q", [DH + 1, 2, SEQ])
        k = sb("a_k", [DH + 1, 2, SEQ])
        v = sb("a_v", [P, NT, DG])
        pr = sb("a_p", [P, 2, SEQ])
        pT = sb("a_pT", [P, 2, SEQ])
        nmax = sb("a_nmax", [P, 2])
        total = sb("a_total", [P, 2])
        inv = sb("a_inv", [P, 2])
        fy = keep["fy"]

        v_loaded = sem("a_v_loaded")
        qk_loaded = [sem(f"a_qk_loaded{s}") for s in (0, 1)]
        ones_set = sem("a_ones_set")
        quads = [-(-(t + 1) // 4) for t in range(NT)]
        all_quads = [(t, c) for t in range(NT) for c in range(quads[t])]
        owner = {tc: n % 2 for n, tc in enumerate(all_quads)}
        pe_names, dve_names, act_names = [], [], []
        for t in range(NT + 1):
            if t < NT:
                pe_names.append(f"s{t}")
                dve_names.append(f"max{t}")
                act_names.append(f"exp{t}")
            if t > 0:
                for c in range(quads[t - 1]):
                    pe_names.append(f"T{t - 1}_{c}")
                    (act_names if owner[t - 1, c] else dve_names).append(f"T{t - 1}_{c}")
                pe_names.append(f"o{t - 1}")
                dve_names += [f"inv{t - 1}", f"o{t - 1}"]
        pe = Steps(sem("a_pe_steps"), pe_names)
        act = Steps(sem("a_act_steps"), act_names)
        dve = Steps(sem("a_dve_steps"), dve_names)

        def emptied(n, h):
            if n >= 2:
                t, c = all_quads[n - 2]
                return (act if owner[t, c] else dve).after(f"T{t}_{c}", h)
            t, c = all_quads[n - 2]
            return (act if owner[t, c] else dve).after(f"T{t}_{c}", h - 1)

        block = ctx.enter_context(nc.Block())

        @block.sync
        def _(sp):
            sp.dma_start(v[:, :, :], io["p_v"].rearrange("(n p) c -> p n c", p=P)).then_inc(v_loaded, 16)
            with sp.Fori(0, PAIRS) as j:
                for e in (0, 1):
                    sp.wait_ge(*pe.after(f"s{NT - 1}", 2 * j + e - 1) if e else pe.after(f"s{NT - 1}", 2 * j - 1))
                    rows = slice(e * DH, (e + 1) * DH)
                    sp.dma_start(q[0:DH, e, :], io["qT"][bass.ds(j, 1), rows, 0:SEQ].rearrange("a p t -> p (a t)"))\
                      .then_inc(qk_loaded[e], 16)
                    sp.dma_start(k[0:DH, e, :], io["kT"][bass.ds(j, 1), rows, 0:SEQ].rearrange("a p t -> p (a t)"))\
                      .then_inc(qk_loaded[e], 16)
                    sp.dma_start(k[DH:DH + 1, e, :], io["cT"][bass.ds(2 * j + e, 1), 0:SEQ]).then_inc(qk_loaded[e], 16)

        @block.gpsimd
        def _(eng):
            eng.memset(q[DH:DH + 1, :, :], 1.0).then_inc(ones_set, 1)

        @block.tensor
        def _(eng):
            pe.begin(eng)
            eng.wait_ge(v_loaded, 16)
            eng.wait_ge(ones_set, 1)

            def head(h, e, j):
                eng.wait_ge(qk_loaded[e], 48 * (j + 1))

                def scores(t):
                    eng.wait_ge(*(act.after(f"exp{t - 1}", h) if t else act.after(f"exp{NT - 1}", h - 1)))
                    n = (t + 1) * P
                    for a in range(0, n, 512):
                        m = min(512, n - a)
                        last = a + m == n
                        mm = eng.matmul(logits[:, a:a + m], q[:, e, t * P:(t + 1) * P], k[:, e, a:a + m],
                                        start=True, stop=not last)
                    eng.matmul(logits[:, n - P:n], keep["ident"][:, :], keep["causal"][:, :], start=False, stop=True)\
                       .then_inc(*pe.done(f"s{t}"))

                def attend(t):
                    eng.wait_ge(*act.after(f"exp{t}", h))
                    for c in range(quads[t]):
                        n = all_quads.index((t, c))
                        eng.wait_ge(*emptied(n, h))
                        for i in range(min(4, t + 1 - 4 * c)):
                            mm = eng.transpose(turned[n % 2][:, i * P:(i + 1) * P],
                                               pr[:, t % 2, (4 * c + i) * P:(4 * c + i + 1) * P], keep["ident"][:, :])
                        mm.then_inc(*pe.done(f"T{t}_{c}"))
                    eng.wait_ge(*(dve.after(f"o{t - 2}", h) if t > 1 else dve.after(f"o{NT - 2 + t}", h - 1)))
                    for c in range(quads[t]):
                        eng.wait_ge(*(act if owner[t, c] else dve).after(f"T{t}_{c}", h))
                        for i in range(4 * c, min(4 * c + 4, t + 1)):
                            mm = eng.matmul(o[t % 2][:, 0:DH], pT[:, t % 2, i * P:(i + 1) * P],
                                            v[:, i, bass.ds(h * DH, DH)], start=(i == 0), stop=(i == t))
                    mm.then_inc(*pe.done(f"o{t}"))

                for t in range(NT + 1):
                    if t < NT:
                        scores(t)
                    if t > 0:
                        attend(t - 1)

            with eng.Fori(0, PAIRS) as j:
                for e in (0, 1):
                    head(2 * j + e, e, j)

        def empty_quad(eng, copy, t, c, h):
            n = min(4, t + 1 - 4 * c) * P
            eng.wait_ge(*pe.after(f"T{t}_{c}", h))
            eng.wait_ge(*(pe.after(f"o{t - 2}", h) if t > 1 else pe.after(f"o{NT - 2 + t}", h - 1)))
            return copy(pT[:, t % 2, 4 * c * P:4 * c * P + n], turned[all_quads.index((t, c)) % 2][:, 0:n])

        @block.scalar
        def _(eng):
            act.begin(eng)

            def head(h, e, j):
                for t in range(NT + 1):
                    if t < NT:
                        n = (t + 1) * P
                        eng.wait_ge(*dve.after(f"max{t}", h))
                        prev = (t - 2, h) if t > 1 else (NT - 2 + t, h - 1)
                        eng.wait_ge(*pe.after(f"o{prev[0]}", prev[1]))
                        eng.wait_ge(*dve.after(f"inv{prev[0]}", prev[1]))
                        eng.activation(pr[:, t % 2, 0:n], logits[:, 0:n], ACT.Exp, bias=nmax[:, t % 2:t % 2 + 1],
                                       accum_out=total[:, t % 2:t % 2 + 1]).then_inc(*act.done(f"exp{t}"))
                    if t > 0:
                        for c in range(quads[t - 1]):
                            if owner[t - 1, c]:
                                empty_quad(eng, eng.copy, t - 1, c, h).then_inc(*act.done(f"T{t - 1}_{c}"))

            with eng.Fori(0, PAIRS) as j:
                for e in (0, 1):
                    head(2 * j + e, e, j)

        @block.vector
        def _(eng):
            dve.begin(eng)

            def head(h, e, j):
                for t in range(NT + 1):
                    if t < NT:
                        n = (t + 1) * P
                        eng.wait_ge(*pe.after(f"s{t}", h))
                        prev = (t - 2, h) if t > 1 else (NT - 2 + t, h - 1)
                        eng.wait_ge(*act.after(f"exp{prev[0]}", prev[1]))
                        eng.tensor_reduce(nmax[:, t % 2:t % 2 + 1], logits[:, 0:n], AX_X, ALU.max, negate=True)\
                           .then_inc(*dve.done(f"max{t}"))
                    if t > 0:
                        u = t - 1
                        for c in range(quads[u]):
                            if not owner[u, c]:
                                empty_quad(eng, eng.tensor_copy, u, c, h).then_inc(*dve.done(f"T{u}_{c}"))
                        eng.wait_ge(*act.after(f"exp{u}", h))
                        eng.reciprocal(inv[:, u % 2:u % 2 + 1], total[:, u % 2:u % 2 + 1])\
                           .then_inc(*dve.done(f"inv{u}"))
                        eng.wait_ge(*pe.after(f"o{u}", h))
                        eng.wait_ge(*dve.after(f"inv{u}", h))
                        eng.tensor_scalar(fy[:, u, bass.ds(h * DH, DH)], o[u % 2][:, 0:DH], inv[:, u % 2:u % 2 + 1],
                                          None, ALU.mult).then_inc(*dve.done(f"o{u}"))

            with eng.Fori(0, PAIRS) as j:
                for e in (0, 1):
                    head(2 * j + e, e, j)


def fox_sample(nc, io, keep):
    CT = PAST // P
    KEYS = PAST + NEW
    HG = HEADS // 2
    with ExitStack() as ctx:
        def sb(name, shape, dt=F32):
            return ctx.enter_context(nc.sbuf_tensor(name, shape, dt))

        def sem(name):
            return ctx.enter_context(nc.semaphore(name))

        bank = [ctx.enter_context(nc.psum_tensor(f"sp{b}", [P, 512], F32)) for b in range(8)]
        q = sb("c_q", [P, PAIRS, NEW])
        qbd = sb("c_qbd", [P, PAIRS, P])
        knew = sb("c_knew", [P, PAIRS, NEW])
        negc = sb("c_negc", [HEADS, NEW])
        lf = sb("c_lf", [P, CT, HEADS])
        suffix = sb("c_suffix", [HEADS, CT, P])
        totals = sb("c_totals", [HEADS, CT])
        cum = sb("c_cum", [HEADS, CT + 1])
        pick = sb("c_pick", [HEADS, 2, P])
        spread = sb("c_spread", [NEW, P])
        kc = sb("c_kc", [P, 2, DG])
        kT = sb("c_kT", [P, 2, DG])
        v = sb("c_v", [P, CT + 1, DG])
        logit = sb("c_logit", [P, 2, KEYS])
        nmax = sb("c_nmax", [P, 2])
        total = sb("c_total", [P, 2])
        inv = sb("c_inv", [P, 2])
        pn = sb("c_pn", [P, 2, 2, P])
        pT = sb("c_pT", [P, 2, 2, P])
        zeros = sb("c_zeros", [P, NEW])

        small_loaded = sem("c_small_loaded")
        k_loaded = [sem(f"c_k_loaded{s}") for s in (0, 1)]
        v_loaded = sem("c_v_loaded")
        made = sem("c_made")
        ready = sem("c_ready")
        tails = sem("c_tails")
        kpe = Steps(sem("c_key_pe_steps"), ["T", "s"])
        kact = Steps(sem("c_key_act_steps"), ["T", "s"])
        final_pe = sem("c_final_pe")
        soft = sem("c_soft")
        exped = sem("c_exped")
        vpe = Steps(sem("c_val_pe_steps"), ["T", "o"])
        vdve = Steps(sem("c_val_dve_steps"), ["p0", "p1"])
        vact = Steps(sem("c_val_act_steps"), ["T"])

        block = ctx.enter_context(nc.Block())
        k_dram = io["cache_fox_k"][0, 0].rearrange("t h d -> t (h d)")
        v_dram = io["cache_fox_v"][0, 0].rearrange("t h d -> t (h d)")

        @block.sync
        def _(sp):
            at = NT * P
            with nc.allow_non_contiguous_dma(reason="32 queries, 8 gates"):
                sp.dma_start(q[:, :, :], io["qT"][:, :, at:at + NEW].rearrange("a p t -> p a t")).then_inc(small_loaded, 16)
                sp.dma_start(knew[:, :, :], io["kT"][:, :, at:at + NEW].rearrange("a p t -> p a t"))\
                  .then_inc(small_loaded, 16)
                sp.dma_start(negc[:, :], io["cT"][:, at:at + NEW]).then_inc(small_loaded, 16)
                sp.dma_start(lf[:, :, :], io["cache_fox_logf"][0, 0].rearrange("(n p) h -> p n h", p=P))\
                  .then_inc(small_loaded, 16)
            sp.dma_start(v[0:NEW, CT, :], io["s_v"]).then_inc(small_loaded, 16)
            with sp.Fori(0, CT // 2) as j:
                for s in (0, 1):
                    row = sp.snap(j * (-2 * P) + (CT - 1 - s) * P)
                    sp.wait_ge(*kpe.after("T", 2 * j + s - 1) if s else kpe.after("T", 2 * j - 1))
                    sp.dma_start(kc[:, s, :], k_dram[bass.ds(row, P), :]).then_inc(k_loaded[s], 16)
            sp.dma_start(v[:, 0:CT, :], v_dram.rearrange("(n p) c -> p n c", p=P)).then_inc(v_loaded, 16)

        @block.gpsimd
        def _(eng):
            eng.memset(qbd[:, :, :], 0.0).then_inc(made, 1)
            eng.memset(zeros[:, :], 0.0)
            eng.memset(cum[:, 0:1], 0.0)
            eng.memset(pick[:, :, :], 1.0)
            eng.memset(spread[:, :], 0.0).then_inc(made, 1)
            eng.wait_ge(made, 2)
            eng.affine_select(out=pick[:, :, :].rearrange("h g (a i) -> h g a i", i=NEW),
                              in_=pick[:, :, :].rearrange("h g (a i) -> h g a i", i=NEW),
                              compare_op=ALU.is_equal, fill=0.0, base=0,
                              pattern=[[-HG, 2], [-1, HG], [0, NEW]], channel_multiplier=1).then_inc(made, 1)
            eng.affine_select(out=spread[:, :].rearrange("t (a i) -> t a i", i=NEW),
                              in_=spread[:, :].rearrange("t (a i) -> t a i", i=NEW),
                              compare_op=ALU.not_equal, fill=1.0, base=0,
                              pattern=[[0, HG], [-1, NEW]], channel_multiplier=1).then_inc(made, 1)

        @block.tensor
        def _(eng):
            kpe.begin(eng)
            vpe.begin(eng)
            ident = keep["ident"][:, :]
            eng.wait_ge(small_loaded, 80)
            eng.wait_ge(made, 4)
            for n in range(CT):
                b = bank[n // 4 % 2]
                if n >= 8 and n % 4 == 0:
                    eng.wait_ge(tails, n // 4 - 1)
                mm = eng.matmul(b[0:HEADS, (n % 4) * P:(n % 4 + 1) * P], lf[:, CT - 1 - n, :], keep["after"][:, :],
                                start=True, stop=True)
                mm = eng.matmul(bank[2][0:HEADS, n:n + 1], lf[:, CT - 1 - n, :], keep["ones"][:, 0:1],
                                start=True, stop=True)
                if n % 4 == 3:
                    mm.then_inc(final_pe, 1)
            eng.wait_ge(ready, 1)

            def keys(n, s, j, past=True):
                slot_kT = kT[:, s, :] if past else None
                if past:
                    eng.wait_ge(k_loaded[s], 16 * (j + 1))
                    eng.wait_ge(*kact.after("T", n - 1))
                    for a in range(PAIRS):
                        mm = eng.transpose(bank[3][:, a * P:(a + 1) * P], kc[:, s, a * P:(a + 1) * P], ident)
                    mm.then_inc(*kpe.done("T"))
                    eng.wait_ge(*kact.after("T", n))
                    eng.wait_ge(*kact.after("s", n - 1))
                w = P if past else NEW
                for g in (0, 1):
                    out = bank[4][:, g * P:g * P + w]
                    for i in (0, 1):
                        a = 2 * g + i
                        rhs = kT[:, s, a * P:(a + 1) * P] if past else knew[:, a, :]
                        eng.matmul(out, qbd[:, a, :], rhs, start=(i == 0), stop=False)
                    if past:
                        mm = eng.matmul(out, pick[:, g, :], suffix[:, bass.ds(n, 1), :].rearrange("h o t -> h (o t)"),
                                        start=False, stop=True)
                    else:
                        eng.matmul(out, pick[:, g, :], negc[:, :], start=False, stop=False)
                        mm = eng.matmul(out, spread[:, :], keep["causal"][0:NEW, 0:NEW], start=False, stop=True)
                if past:
                    mm.then_inc(*kpe.done("s"))
                else:
                    mm.then_inc(final_pe, 1)

            with eng.Fori(0, CT // 2) as j:
                for s in (0, 1):
                    keys(2 * j + s, s, j)
            eng.wait_ge(*kact.after("s", CT - 1))
            keys(CT, 0, 0, past=False)

            eng.matmul(bank[5][0:NEW, :], zeros[0:NEW, :], v[0:NEW, CT, :], start=True, stop=False)
            eng.wait_ge(v_loaded, 16)

            def values(n, s, stop, w=P):
                tile = eng.snap(n * -1 + (CT - 1)) if w == P else None
                eng.wait_ge(*vact.after("T", n - 1))
                eng.wait_ge(*vdve.after("p1", n))
                for g in (0, 1):
                    mm = eng.transpose(bank[6][0:w, g * P:(g + 1) * P], pn[:, s, g, 0:w], ident)
                mm.then_inc(*vpe.done("T"))
                eng.wait_ge(*vact.after("T", n))
                for h in range(HEADS):
                    g, i = divmod(h, HG)
                    r = v[0:w, CT, h * DH:(h + 1) * DH] if w < P else v[:, bass.ds(tile, 1), h * DH:(h + 1) * DH]\
                        .rearrange("p o c -> p (o c)")
                    mm = eng.matmul(bank[5][0:NEW, h * DH:(h + 1) * DH], pT[0:w, s, g, i * NEW:(i + 1) * NEW], r,
                                    start=False, stop=stop and h == HEADS - 1)
                mm.then_inc(*vpe.done("o"))

            with eng.Fori(0, CT // 2) as j:
                for s in (0, 1):
                    values(2 * j + s, s, False)
            values(CT, 0, True, NEW)

        @block.scalar
        def _(eng):
            kact.begin(eng)
            vact.begin(eng)

            def keys(n, s, j):
                eng.wait_ge(*kpe.after("T", n))
                eng.wait_ge(*kpe.after("s", n - 1))
                eng.copy(kT[:, s, :], bank[3][:, :]).then_inc(*kact.done("T"))
                eng.wait_ge(*kpe.after("s", n))
                eng.copy(logit[:, :, bass.ds(n * P, P)], bank[4][:, 0:2 * P].rearrange("p (g t) -> p g t", g=2))\
                   .then_inc(*kact.done("s"))

            with eng.Fori(0, CT // 2) as j:
                for s in (0, 1):
                    keys(2 * j + s, s, j)
            eng.wait_ge(final_pe, CT // 4 + 1)
            eng.copy(logit[:, :, PAST:KEYS], bank[4][:, 0:2 * P].rearrange("p (g t) -> p g t", g=2)[:, :, 0:NEW])\
               .then_inc(exped, 1)
            for g in (0, 1):
                eng.wait_ge(soft, g + 1)
                eng.activation(logit[:, g, :], logit[:, g, :], ACT.Exp, bias=nmax[:, g:g + 1],
                               accum_out=total[:, g:g + 1]).then_inc(exped, 1)

            def values(n, s, w=P):
                eng.wait_ge(*vpe.after("T", n))
                eng.wait_ge(*vpe.after("o", n - 1))
                eng.copy(pT[0:w, s, :, :], bank[6][0:w, 0:2 * P].rearrange("p (g t) -> p g t", g=2))\
                   .then_inc(*vact.done("T"))

            with eng.Fori(0, CT // 2) as j:
                for s in (0, 1):
                    values(2 * j + s, s)
            values(CT, 0, NEW)

        @block.vector
        def _(eng):
            vdve.begin(eng)
            for c in range(CT // 4):
                eng.wait_ge(final_pe, c + 1)
                eng.tensor_copy(suffix[:, 4 * c:4 * c + 4, :],
                                bank[c % 2][0:HEADS, :].rearrange("h (n t) -> h n t", n=4)).then_inc(tails, 1)
            eng.tensor_copy(totals[:, :], bank[2][0:HEADS, 0:CT]).then_inc(tails, 1)
            eng.wait_ge(tails, CT // 4 + 1)
            eng.wait_ge(made, 4)
            eng.tensor_tensor_scan(out=cum[:, 1:CT + 1], data0=keep["ones"][0:HEADS, 0:CT], data1=totals[:, :],
                                   initial=0.0, op0=ALU.mult, op1=ALU.add).then_inc(tails, 1)
            eng.wait_ge(tails, CT // 4 + 2)
            eng.tensor_tensor(suffix[:, :, :], suffix[:, :, :], cum[:, 0:CT].unsqueeze(2).broadcast_to([HEADS, CT, P]),
                              ALU.add)
            eng.wait_ge(small_loaded, 80)
            for h in range(HEADS):
                a, e = divmod(h, 2)
                rows, i = slice(e * DH, (e + 1) * DH), h % HG
                ins = eng.tensor_copy(qbd[rows, a, i * NEW:(i + 1) * NEW], q[rows, a, :])
            ins.then_inc(ready, 1)
            eng.wait_ge(exped, 1)
            for g in (0, 1):
                eng.tensor_reduce(nmax[:, g:g + 1], logit[:, g, :], AX_X, ALU.max, negate=True).then_inc(soft, 1)
            eng.wait_ge(exped, 3)
            eng.reciprocal(inv[:, :], total[:, :]).then_inc(soft, 1)
            eng.wait_ge(soft, 3)

            def values(n, s, w=P):
                eng.wait_ge(*vpe.after("T", n - 1))
                for g in (0, 1):
                    eng.tensor_scalar(pn[:, s, g, 0:w], logit[:, g, bass.ds(n * P, w)], inv[:, g:g + 1], None, ALU.mult)\
                       .then_inc(*vdve.done(f"p{g}"))

            with eng.Fori(0, CT // 2) as j:
                for s in (0, 1):
                    values(2 * j + s, s)
            values(CT, 0, NEW)
            eng.wait_ge(*vpe.after("o", CT))
            eng.tensor_copy(keep["fy"][0:NEW, NT, :], bank[5][0:NEW, :])
def layer_norm_steps(eng, dve, held, act_after, z, stats, mv, std, out, gain, offset, pre, t):
    for half in (0, 1):
        ins = eng.bn_stats(stats[:, half, :], z[:, half * 512:(half + 1) * 512])
    ins.then_inc(*dve.done(pre + "stats"))
    eng.wait_ge(*dve.after(pre + "stats", t))
    hold(eng, held)
    eng.bn_aggr(mv[:, 0:2], stats[:, :, :].rearrange("p a b -> p (a b)")).then_inc(*dve.done(pre + "mv"))
    eng.wait_ge(*dve.after(pre + "mv", t))
    eng.tensor_scalar(mv[:, 2:3], mv[:, 1:2], 1.0, LN_EPS, ALU.mult, ALU.add).then_inc(*dve.done(pre + "eps"))
    eng.wait_ge(*act_after)
    eng.reciprocal(mv[:, 3:4], std).then_inc(*dve.done(pre + "rstd"))
    eng.wait_ge(*dve.after(pre + "rstd", t))
    eng.tensor_scalar(z, z, mv[:, 0:1], mv[:, 3:4], ALU.subtract, ALU.mult).then_inc(*dve.done(pre + "norm"))
    eng.wait_ge(*dve.after(pre + "norm", t))
    eng.tensor_tensor(z, z, gain, ALU.mult).then_inc(*dve.done(pre + "gain"))
    eng.wait_ge(*dve.after(pre + "gain", t))
    eng.tensor_tensor(out, z, offset, ALU.add).then_inc(*dve.done(pre + "out"))


def mix(nc, io, keep):
    with ExitStack() as ctx:
        def sb(name, shape, dt=F32):
            return ctx.enter_context(nc.sbuf_tensor(name, shape, dt))

        def sem(name):
            return ctx.enter_context(nc.semaphore(name))

        FT = ctx.enter_context(nc.psum_tensor("m_FT", [P, 512], F32))
        M = [[ctx.enter_context(nc.psum_tensor(f"m_M{s}{b}", [P, 512], F32)) for b in range(2)] for s in range(2)]
        HT = [ctx.enter_context(nc.psum_tensor(f"m_HT{b}", [P, 512], F32)) for b in range(2)]
        SC = ctx.enter_context(nc.psum_tensor("m_SC", [P, 512], F32))
        w = sb("m_w", [P, KD, D])
        rw = sb("m_rw", [P, KD, EXPERTS])
        gain, offset = sb("m_gain", [P, D]), sb("m_offset", [P, D])
        x = sb("m_x", [P, 2, D])
        ry = sb("m_ry", [P, 2, PAIRS, P])
        og = sb("m_og", [P, 2, DG])
        f = sb("m_f", [P, DG])
        fT = sb("m_fT", [P, PAIRS, P])
        z = sb("m_z", [P, D])
        stats, mv, std = sb("m_stats", [P, 2, 6]), sb("m_mv", [P, 4]), sb("m_std", [P, 1])
        h = sb("m_h", [P, 2, D])
        hT = sb("m_hT", [P, KD, P])

        weights_loaded = sem("m_weights_loaded")
        loaded = [sem(f"m_loaded{s}") for s in (0, 1)]
        stored = [sem(f"m_stored{s}") for s in (0, 1)]
        rest_zeroed, rows_padded = sem("m_rest_zeroed"), sem("m_rows_padded")
        held = sem("m_held")
        mpe = Steps(sem("m_product_pe_steps"), ["fT", "m"])
        mact = Steps(sem("m_product_act_steps"), ["fT"])
        mdve = Steps(sem("m_product_dve_steps"), ["f"])
        pe = Steps(sem("m_pe_steps"), ["hT0", "hT1", "score"])
        act = Steps(sem("m_act_steps"), ["std", "hT0", "hT1", "score"])
        dve = Steps(sem("m_dve_steps"), ["z0", "z1", "stats", "mv", "eps", "rstd", "norm", "gain", "out"])
        block = ctx.enter_context(nc.Block())

        def ahead_over_tiles(eng, product, tile):
            product(0, 0, 0)
            with eng.Fori(0, NT // 2) as j:
                for slot in (0, 1):
                    product(2 * j + slot + 1, 1 - slot, j + slot)
                    tile(2 * j + slot, slot, j)
            tile(NT, 0, NT // 2)

        @block.sync
        def _(sp):
            begin_stores(sp, stored)

            def loads(t, slot, x_src, rows=P):
                sp.dma_start(ry[:, slot, :, :], io["ryT"][:, :, bass.ds(t * P, P)].rearrange("a p t -> p a t"))\
                  .then_inc(loaded[slot], 16)
                sp.dma_start(og[:, slot, :], io["og"][bass.ds(t * P, P), :]).then_inc(loaded[slot], 16)
                sp.dma_start(x[0:rows, slot, :], x_src).then_inc(loaded[slot], 16)

            def store(t, slot):
                sp.wait_ge(*dve.after("out", t))
                sp.dma_start(io["h"][bass.ds(t * P, P), :], h[:, slot, :]).then_inc(stored[slot], 16)

            loads(0, 0, io["x_prompt"][0, 0:P, :])
            sp.dma_start(w[:, :, :], io["w_out"][0].rearrange("(c p) n -> p c n", p=P)).then_inc(weights_loaded, 16)
            loads(1, 1, io["x_prompt"][0, P:2 * P, :])
            with nc.allow_non_contiguous_dma(reason="small rows for all partitions"):
                sp.dma_start(rw[:, :, :], io["router_w"].rearrange("(c p) n -> p c n", p=P)).then_inc(weights_loaded, 16)
                sp.dma_start(gain[:, :], io["ln1_g"].broadcast_to([P, D])).then_inc(weights_loaded, 16)
                sp.dma_start(offset[:, :], io["ln1_b"].broadcast_to([P, D])).then_inc(weights_loaded, 16)
            with sp.Fori(0, NT // 2 - 1) as j:
                for slot in (0, 1):
                    t = 2 * j + slot
                    sp.wait_ge(*dve.after("z1", t))
                    loads(t + 2, slot, io["x_prompt"][0, bass.ds((t + 2) * P, P), :])
                    store(t, slot)
            sp.wait_ge(rows_padded, 1)
            loads(NT, 0, io["x_sample"][0], NEW)
            store(NT - 2, 0)
            store(NT - 1, 1)
            store(NT, 0)
            sp.wait_ge(stored[0], 16 * (NT // 2 + 2))
            sp.wait_ge(stored[1], 16 * (NT // 2 + 1))

        @block.gpsimd
        def _(eng):
            eng.memset(keep["fy"][NEW:2 * NEW, NT, :], 0.0).then_inc(rest_zeroed, 1)
            eng.memset(keep["fy"][DH:P, NT, :], 0.0).then_inc(rest_zeroed, 1)
            eng.wait_ge(rest_zeroed, 2)
            eng.wait_ge(*dve.after("z1", NT - 2))
            eng.memset(x[:, 0, :], 0.0).then_inc(rows_padded, 1)

        @block.tensor
        def _(eng):
            mpe.begin(eng)
            pe.begin(eng)
            ident = keep["ident"][:, :]

            def product(t, slot, turn):
                eng.wait_ge(*mdve.after("f", t))
                eng.wait_ge(*mact.after("fT", t - 1))
                for a in range(PAIRS):
                    mm = eng.transpose(FT[:, a * P:(a + 1) * P], f[:, a * P:(a + 1) * P], ident)
                mm.then_inc(*mpe.done("fT"))
                if not (isinstance(t, int) and t == 0):
                    eng.wait_ge(*dve.after("z1", t - 2))
                for c in range(PAIRS):
                    for half in (0, 1):
                        eng.matmul(M[slot][half][:, :], ry[:, slot, c, :], w[:, c, half * 512:(half + 1) * 512],
                                   start=(c == 0), stop=False)
                eng.wait_ge(*mact.after("fT", t))
                for c in range(PAIRS):
                    for half in (0, 1):
                        mm = eng.matmul(M[slot][half][:, :], fT[:, c, :],
                                        w[:, PAIRS + c, half * 512:(half + 1) * 512], start=False, stop=(c == PAIRS - 1))
                mm.then_inc(*mpe.done("m"))

            def tile(t, slot, j):
                eng.wait_ge(*dve.after("out", t))
                for half in (0, 1):
                    eng.wait_ge(*act.after(f"hT{half}", t - 1))
                    for k in range(4):
                        c = 4 * half + k
                        mm = eng.transpose(HT[half][:, k * P:(k + 1) * P], h[:, slot, c * P:(c + 1) * P], ident)
                    mm.then_inc(*pe.done(f"hT{half}"))
                eng.wait_ge(*act.after("hT1", t))
                eng.wait_ge(*act.after("score", t - 1))
                for c in range(KD):
                    mm = eng.matmul(SC[:, 0:EXPERTS], hT[:, c, :], rw[:, c, :], start=(c == 0), stop=(c == KD - 1))
                mm.then_inc(*pe.done("score"))

            eng.wait_ge(weights_loaded, 64)
            ahead_over_tiles(eng, product, tile)

        @block.scalar
        def _(eng):
            mact.begin(eng)
            act.begin(eng)

            def product(t, slot, turn):
                eng.wait_ge(*mpe.after("fT", t))
                eng.wait_ge(*mpe.after("m", t - 1))
                eng.copy(fT[:, :, :], FT[:, :].rearrange("p (a t) -> p a t", a=PAIRS)).then_inc(*mact.done("fT"))

            def tile(t, slot, j):
                eng.wait_ge(*dve.after("eps", t))
                eng.activation(std[:, :], mv[:, 2:3], ACT.Sqrt).then_inc(*act.done("std"))
                for half in (0, 1):
                    eng.wait_ge(*pe.after(f"hT{half}", t))
                    eng.wait_ge(*pe.after("score", t - 1))
                    eng.copy(hT[:, 4 * half:4 * half + 4, :], HT[half][:, :].rearrange("p (a t) -> p a t", a=4))\
                       .then_inc(*act.done(f"hT{half}"))
                eng.wait_ge(*pe.after("score", t))
                eng.copy(keep["logits"][:, bass.ds(t, 1), :], SC[:, 0:EXPERTS].unsqueeze(1)).then_inc(*act.done("score"))

            ahead_over_tiles(eng, product, tile)

        @block.vector
        def _(eng):
            mdve.begin(eng)
            dve.begin(eng)
            eng.wait_ge(rest_zeroed, 2)

            def product(t, slot, turn):
                eng.wait_ge(loaded[slot], 48 * (turn + 1))
                eng.wait_ge(*mpe.after("fT", t - 1))
                eng.tensor_tensor(f[:, :].unsqueeze(1), keep["fy"][:, bass.ds(t, 1), :], og[:, slot, :].unsqueeze(1),
                                  ALU.mult).then_inc(*mdve.done("f"))

            def tile(t, slot, j):
                eng.wait_ge(*mpe.after("m", t))
                eng.wait_ge(*dve.after("out", t - 1))
                for half in (0, 1):
                    c = slice(half * 512, (half + 1) * 512)
                    eng.scalar_tensor_tensor(out=z[:, c], in0=x[:, slot, c], scalar=ALPHA, in1=M[slot][half][:, :],
                                             op0=ALU.mult, op1=ALU.add).then_inc(*dve.done(f"z{half}"))
                eng.wait_ge(*dve.after("z1", t))
                eng.wait_ge(stored[slot], 16 * (j + 1))
                eng.wait_ge(*pe.after("hT1", t - 1))
                layer_norm_steps(eng, dve, held, act.after("std", t), z[:, :], stats, mv, std[:, :], h[:, slot, :],
                                 gain[:, :], offset[:, :], "", t)

            eng.wait_ge(weights_loaded, 64)
            ahead_over_tiles(eng, product, tile)


def route(nc, io, keep):
    with ExitStack() as ctx:
        def sb(name, shape, dt=F32):
            return ctx.enter_context(nc.sbuf_tensor(name, shape, dt))

        def sem(name):
            return ctx.enter_context(nc.semaphore(name))

        before = [ctx.enter_context(nc.psum_tensor(f"t_before{s}", [P, 512], F32)) for s in (0, 1)]
        total = [ctx.enter_context(nc.psum_tensor(f"t_total{s}", [P, 512], F32)) for s in (0, 1)]
        rb = sb("t_rb", [P, EXPERTS])
        score, sel, selm, gm, both, rank, base = (sb("t_" + n, [P, TILES, EXPERTS]) for n in (
            "score", "sel", "selm", "gm", "both", "rank", "base"))
        top = sb("t_top", [P, TILES, GROUPS, 8])
        gs, gbest, ebest = (sb("t_" + n, [P, TILES, 8]) for n in ("gs", "gbest", "ebest"))
        gidx, eidx = sb("t_gidx", [P, TILES, 8], U32), sb("t_eidx", [P, TILES, 8], U32)
        gid, gsum, ginv = (sb("t_" + n, [P, TILES]) for n in ("gid", "gsum", "ginv"))
        pick = sb("t_pick", [P, TILES, 2, EXPERTS])
        prod = sb("t_prod", [P, TILES, 2, EXPERTS])
        graw = sb("t_graw", [P, TILES, 2])
        bias_loaded, scored, padded, ranked = sem("t_bias_loaded"), sem("t_scored"), sem("t_padded"), sem("t_ranked")
        steps = sem("t_steps")
        chosen = sem("t_chosen")
        counted = sem("t_counted")
        picked = sem("t_picked")
        block = ctx.enter_context(nc.Block())

        @block.sync
        def _(sp):
            with nc.allow_non_contiguous_dma(reason="one row for all partitions"):
                sp.dma_start(rb[:, :], io["router_b"].unsqueeze(0).broadcast_to([P, EXPERTS])).then_inc(bias_loaded, 16)

        @block.gpsimd
        def _(eng):
            eng.memset(gs[:, :, :], FAR).then_inc(padded, 1)

        @block.scalar
        def _(eng):
            eng.activation(score[:, :, :], keep["logits"][:, :, :], ACT.Sigmoid).then_inc(scored, 1)

        @block.tensor
        def _(eng):
            eng.wait_ge(picked, 1)
            cols = NT * EXPERTS
            for s, (rows, tiles) in enumerate(((P, slice(0, NT)), (NEW, slice(NT, TILES)))):
                n = (tiles.stop - tiles.start) * EXPERTS
                rhs = both[0:rows, tiles, :].rearrange("p t e -> p (t e)")
                eng.matmul(before[s][:, 0:n], keep["before"][0:rows, :], rhs, start=True, stop=True)
                eng.matmul(total[s][:, 0:n], keep["ones"][0:rows, :], rhs, start=True, stop=True).then_inc(ranked, 1)

        @block.vector
        def _(eng):
            n = [0]

            def at(ins):
                n[0] += 1
                ins.then_inc(steps, 1)
                eng.wait_ge(steps, n[0])

            def over(ap, rest):
                return ap.unsqueeze(2).broadcast_to([P, TILES, rest])

            def row(ap):
                return ap.unsqueeze(1).broadcast_to([P, TILES, EXPERTS])

            def maxima(done, values, best, index):
                for t in range(TILES):
                    eng.max(out=best[:, t, :], in_=values[:, t, :]).then_inc(chosen, 1)
                eng.wait_ge(chosen, done + TILES)
                for t in range(TILES):
                    eng.max_index(out=index[:, t, :], in_max=best[:, t, :], in_values=values[:, t, :])\
                       .then_inc(chosen, 1)
                eng.wait_ge(chosen, done + 2 * TILES)

            eng.wait_ge(scored, 1)
            eng.wait_ge(bias_loaded, 16)
            at(eng.tensor_tensor(sel[:, :, :], score[:, :, :], row(rb[:, :]), ALU.add))
            for t in range(TILES):
                for g in range(GROUPS):
                    ins = eng.max(out=top[:, t, g, :], in_=sel[:, t, g * PER_GROUP:(g + 1) * PER_GROUP])
                ins.then_inc(chosen, 1)
            eng.wait_ge(chosen, TILES)
            eng.wait_ge(padded, 1)
            at(eng.tensor_tensor(gs[:, :, 0:GROUPS].unsqueeze(3), top[:, :, :, 0:1], top[:, :, :, 1:2], ALU.add))
            maxima(TILES, gs, gbest, gidx)
            at(eng.tensor_copy(gid[:, :], gidx[:, :, 0:1].rearrange("p t o -> p (t o)")))
            at(eng.tensor_tensor(gm[:, :, :], row(keep["group_of"][:, :]), over(gid[:, :], EXPERTS), ALU.is_equal))
            at(eng.tensor_scalar(selm[:, :, :], gm[:, :, :], -FAR, FAR, ALU.mult, ALU.add))
            at(eng.tensor_tensor(gm[:, :, :], gm[:, :, :], sel[:, :, :], ALU.mult))
            at(eng.tensor_tensor(selm[:, :, :], selm[:, :, :], gm[:, :, :], ALU.add))
            maxima(3 * TILES, selm, ebest, eidx)
            at(eng.tensor_copy(keep["expert"][:, :, :], eidx[:, :, 0:2]))
            for i in (0, 1):
                at(eng.tensor_tensor(pick[:, :, i, :], row(keep["expert_id"][:, :]),
                                     keep["expert"][:, :, i:i + 1].broadcast_to([P, TILES, EXPERTS]), ALU.is_equal))
            eng.tensor_tensor(both[:, :, :], pick[:, :, 0, :], pick[:, :, 1, :], ALU.add).then_inc(picked, 1)
            for i in (0, 1):
                at(eng.tensor_tensor(prod[:, :, i, :], pick[:, :, i, :], score[:, :, :], ALU.mult))
            at(eng.tensor_reduce(graw[:, :, :], prod[:, :, :, :], AX_X, ALU.add))
            at(eng.tensor_tensor(gsum[:, :].unsqueeze(2), graw[:, :, 0:1], graw[:, :, 1:2], ALU.add))
            at(eng.reciprocal(ginv[:, :], gsum[:, :]))
            at(eng.tensor_tensor(keep["gate"][:, :, :], graw[:, :, :], over(ginv[:, :], 2), ALU.mult))
            eng.wait_ge(ranked, 2)
            eng.memset(base[:, 0, :], 0.0).then_inc(counted, 1)
            with eng.Fori(0, NT) as t:
                eng.wait_ge(counted, t + 1)
                eng.tensor_tensor(base[:, bass.ds(t + 1, 1), :], base[:, bass.ds(t, 1), :],
                                  total[0][:, bass.ds(t * EXPERTS, EXPERTS)].unsqueeze(1), ALU.add).then_inc(counted, 1)
            eng.wait_ge(counted, TILES)
            at(eng.tensor_tensor(keep["counts"][:, :], base[:, NT, :], total[1][:, 0:EXPERTS], ALU.add))
            at(eng.tensor_tensor(rank[:, 0:NT, :].rearrange("p t e -> p (t e)"), before[0][:, :],
                                 base[:, 0:NT, :].rearrange("p t e -> p (t e)"), ALU.add))
            at(eng.tensor_tensor(rank[:, NT, :], before[1][:, 0:EXPERTS], base[:, NT, :], ALU.add))
            for i in (0, 1):
                at(eng.tensor_tensor(prod[:, :, i, :], pick[:, :, i, :], rank[:, :, :], ALU.mult))
            at(eng.tensor_reduce(keep["rank"][:, :, :], prod[:, :, :, :], AX_X, ALU.add))


def dispatch(nc, io, keep):
    with ExitStack() as ctx:
        def sb(name, shape, dt=F32):
            return ctx.enter_context(nc.sbuf_tensor(name, shape, dt))

        def sem(name):
            return ctx.enter_context(nc.semaphore(name))

        frames = ctx.enter_context(nc.psum_tensor("d_frames", [P, 512], F32))
        ci = sb("d_ci", [P, EXPERTS], I32)
        nb = sb("d_nb", [P, EXPERTS])
        end, first = sb("d_end", [P, EXPERTS]), sb("d_first", [P, EXPERTS])
        N2 = 2 * TILES
        eq = sb("d_eq", [P, N2, EXPERTS])
        base = sb("d_base", [P, N2])
        part = sb("d_part", [P, 2, N2], I32)
        partf = sb("d_partf", [P, 2, N2])
        cmp = sb("d_cmp", [1, BLOCKS, EXPERTS])
        be, bf, fresh = (sb("d_" + n, [1, BLOCKS]) for n in ("be", "bf", "fresh"))
        count_i, count = sb("d_count_i", [P, P], I32), sb("d_count", [P, P])
        frame_i, frame = sb("d_frame_i", [P, N2], I32), sb("d_frame", [P, N2])
        in_block = sb("d_in_block", [P, N2, BLOCKS])
        in_row = sb("d_in_row", [P, N2, P])
        numbered, steps, marked, placed = sem("d_numbered"), sem("d_steps"), sem("d_marked"), sem("d_placed")
        block = ctx.enter_context(nc.Block())

        @block.vector
        def _(eng):
            n = [0]

            def at(ins):
                n[0] += 1
                ins.then_inc(steps, 1)
                eng.wait_ge(steps, n[0])

            at(eng.tensor_scalar(ci[:, :], keep["counts"][:, :], float(P - 1), None, ALU.add))
            at(eng.tensor_scalar(ci[:, :], ci[:, :], 7, None, ALU.arith_shift_right))
            at(eng.tensor_copy(nb[:, :], ci[:, :]))
            at(eng.tensor_tensor_scan(out=end[:, :], data0=keep["ones"][:, 0:EXPERTS], data1=nb[:, :], initial=0.0,
                                      op0=ALU.mult, op1=ALU.add))
            at(eng.tensor_tensor(first[:, :], end[:, :], nb[:, :], ALU.subtract))
            at(eng.tensor_tensor(eq[:, :, :], keep["expert_id"][:, :].unsqueeze(1).broadcast_to([P, N2, EXPERTS]),
                                 keep["expert"][:, :, :].rearrange("p n i -> p (n i)").unsqueeze(2)
                                 .broadcast_to([P, N2, EXPERTS]), ALU.is_equal))
            at(eng.tensor_tensor(eq[:, :, :], eq[:, :, :], first[:, :].unsqueeze(1).broadcast_to([P, N2, EXPERTS]),
                                 ALU.mult))
            at(eng.tensor_reduce(base[:, :], eq[:, :, :], AX_X, ALU.add))
            row = keep["row"][:, :, :].rearrange("p n i -> p (n i)")
            at(eng.scalar_tensor_tensor(out=row, in0=base[:, :], scalar=float(P),
                                        in1=keep["rank"][:, :, :].rearrange("p n i -> p (n i)"),
                                        op0=ALU.mult, op1=ALU.add))
            at(eng.tensor_scalar(part[:, 0, :], row, 7, None, ALU.arith_shift_right))
            at(eng.tensor_scalar(part[:, 1, :], row, P - 1, None, ALU.bitwise_and))
            at(eng.tensor_copy(partf[:, :, :], part[:, :, :]))
            eng.wait_ge(numbered, 2)
            at(eng.tensor_copy(count[:, :], count_i[:, :]))
            at(eng.tensor_copy(frame[:, :], frame_i[:, :]))
            at(eng.tensor_tensor(in_row[:, :, :], count[:, :].unsqueeze(1).broadcast_to([P, N2, P]),
                                 partf[:, 1, :].unsqueeze(2).broadcast_to([P, N2, P]), ALU.is_equal))
            at(eng.tensor_tensor(in_block[:, :, :], count[:, 0:BLOCKS].unsqueeze(1).broadcast_to([P, N2, BLOCKS]),
                                 partf[:, 0, :].unsqueeze(2).broadcast_to([P, N2, BLOCKS]), ALU.is_equal))
            eng.tensor_tensor(in_block[:, :, :], in_block[:, :, :], frame[:, :].unsqueeze(2)
                              .broadcast_to([P, N2, BLOCKS]), ALU.mult).then_inc(marked, 1)
            at(eng.tensor_tensor(cmp[:, :, :], end[0:1, :].unsqueeze(1).broadcast_to([1, BLOCKS, EXPERTS]),
                                 count[0:1, 0:BLOCKS].unsqueeze(2).broadcast_to([1, BLOCKS, EXPERTS]), ALU.is_le))
            at(eng.tensor_reduce(be[:, :], cmp[:, :, :], AX_X, ALU.add))
            at(eng.tensor_scalar(be[:, :], be[:, :], float(EXPERTS - 1), None, ALU.min))
            at(eng.tensor_copy(keep["block_expert"][:, :], be[:, :]))
            at(eng.memset(fresh[:, 0:1], 1.0))
            at(eng.tensor_tensor(fresh[:, 1:BLOCKS], be[:, 1:BLOCKS], be[:, 0:BLOCKS - 1], ALU.not_equal))
            at(eng.tensor_copy(keep["block_fresh"][:, :], fresh[:, :]))
            at(eng.tensor_tensor_scan(out=bf[:, :], data0=keep["ones"][0:1, 0:BLOCKS], data1=fresh[:, :], initial=0.0,
                                      op0=ALU.mult, op1=ALU.add))
            at(eng.tensor_copy(keep["block_place"][:, :], bf[:, :]))
            at(eng.tensor_scalar(keep["block_place"][:, :], keep["block_place"][:, :], 1, None, ALU.bitwise_and))
            eng.wait_ge(placed, 1)
            at(eng.tensor_copy(keep["frame_of"][:, :], frames[:, 0:BLOCKS]))

        @block.tensor
        def _(eng):
            eng.wait_ge(marked, 1)
            for n in range(N2):
                rows = P if n < 2 * NT else NEW
                mm = eng.matmul(frames[:, 0:BLOCKS], in_row[0:rows, n, :], in_block[0:rows, n, :],
                                start=(n == 0), stop=(n == N2 - 1))
            mm.then_inc(placed, 1)

        @block.gpsimd
        def _(eng):
            eng.iota(count_i[:, :], pattern=[[1, P]], base=0, channel_multiplier=0).then_inc(numbered, 1)
            eng.wait_ge(numbered, 1)
            eng.iota(frame_i[:, :], pattern=[[P, TILES], [0, 2]], base=0, channel_multiplier=1).then_inc(numbered, 1)


def experts(nc, io, keep):
    with ExitStack() as ctx:
        def sb(name, shape, dt=F32):
            return ctx.enter_context(nc.sbuf_tensor(name, shape, dt))

        def sem(name):
            return ctx.enter_context(nc.semaphore(name))

        KE = DE // P
        XT = [ctx.enter_context(nc.psum_tensor(f"e_XT{b}", [P, 512], F32)) for b in range(2)]
        H1 = ctx.enter_context(nc.psum_tensor("e_H1", [P, 512], F32))
        H3 = ctx.enter_context(nc.psum_tensor("e_H3", [P, 512], F32))
        GT = ctx.enter_context(nc.psum_tensor("e_GT", [P, 512], F32))
        Y = [ctx.enter_context(nc.psum_tensor(f"e_Y{b}", [P, 512], F32)) for b in range(2)]
        w1, w3 = sb("e_w1", [P, 2, KD, DE]), sb("e_w3", [P, 2, KD, DE])
        w2 = sb("e_w2", [P, 2, KE, D])
        idx = sb("e_idx", [P, 2], I32)
        x = sb("e_x", [P, 2, D])
        xT = sb("e_xT", [P, 2, KD, P])
        a = sb("e_a", [P, DE])
        g = sb("e_g", [P, DE])
        gT = sb("e_gT", [P, KE, P])
        y = sb("e_y", [P, 2, D])

        w13_loaded = [sem(f"e_w13_loaded{s}") for s in (0, 1)]
        w2_loaded = [sem(f"e_w2_loaded{s}") for s in (0, 1)]
        pool = Steps(sem("e_pool_steps"), ["idx"])
        x_loaded = [sem(f"e_x_loaded{s}") for s in (0, 1)]
        stored = [sem(f"e_stored{s}") for s in (0, 1)]
        held, sp_held = sem("e_pool_held"), sem("e_sp_held")
        xpe = Steps(sem("e_x_pe_steps"), ["xT0", "xT1"], ahead=2)
        xact = Steps(sem("e_x_act_steps"), ["xT0"])
        xdve = Steps(sem("e_x_dve_steps"), ["xT1"])
        pe = Steps(sem("e_pe_steps"), ["h1", "h3", "gT", "y0", "y1"], ahead=2)
        act = Steps(sem("e_act_steps"), ["a", "y0"])
        dve = Steps(sem("e_dve_steps"), ["g", "gT", "y1"])
        block = ctx.enter_context(nc.Block())
        PAIRED = BLOCKS // 2
        assert BLOCKS % 2 == 1

        def over_blocks(eng, body):
            with eng.Fori(0, PAIRED) as j:
                for s in (0, 1):
                    body(2 * j + s, s, j)
            body(BLOCKS - 1, 0, PAIRED)

        @block.sync
        def _(sp):
            def body(b, s, j):
                e = sp.value_load(keep["block_expert"][0:1, bass.ds(b, 1)], min_val=0, max_val=EXPERTS - 1)
                place = sp.value_load(keep["block_place"][0:1, bass.ds(b, 1)], min_val=0, max_val=1)
                fresh = sp.value_load(keep["block_fresh"][0:1, bass.ds(b, 1)], min_val=0, max_val=1)
                sp.wait_ge(*pe.after("h3", b - 2))
                hold(sp, sp_held)
                for w, name in ((w1, "moe_w1"), (w3, "moe_w3")):
                    sp.dma_start(w[:, bass.ds(place, 1), :, :],
                                 io[name][0, bass.ds(e, 1)].rearrange("o (p k) n -> p o k n", k=KD), cond=fresh)\
                      .then_inc(w13_loaded[s], 16)
                sp.wait_ge(*pe.after("y1", b - 2))
                hold(sp, sp_held)
                sp.dma_start(w2[:, bass.ds(place, 1), :, :],
                             io["moe_w2"][0, bass.ds(e, 1)].rearrange("o (p k) n -> p o k n", k=KE), cond=fresh)\
                  .then_inc(w2_loaded[s], 16)

            over_blocks(sp, body)

        @block.gpsimd
        def _(eng):
            pool.begin(eng)

            def body(b, s, j):
                eng.wait_ge(*xpe.after("xT1", b - 2))
                hold(eng, held)
                eng.tensor_copy(idx[:, s:s + 1], keep["frame_of"][:, bass.ds(b, 1)]).then_inc(*pool.done("idx"))
                eng.wait_ge(*pool.after("idx", b))
                hold(eng, held)
                eng.indirect_dma_start(out=x[:, s, :], out_offset=None, in_=io["h"][:, :],
                                       in_offset=bass.IndirectOffsetOnAxis(ap=idx[:, s:s + 1], axis=0),
                                       bounds_check=ROWS - 1, oob_is_err=False).then_inc(x_loaded[s], 16)

            over_blocks(eng, body)

        @block.tensor
        def _(eng):
            xpe.begin(eng)
            pe.begin(eng)
            ident = keep["ident"][:, :]

            def turn_x(b, s, j):
                eng.wait_ge(x_loaded[s], 16 * (j + 1))
                for half in (0, 1):
                    eng.wait_ge(*(xdve.after("xT1", b - 1) if half else xact.after("xT0", b - 1)))
                    for k in range(4):
                        mm = eng.transpose(XT[half][:, k * P:(k + 1) * P], x[:, s, 4 * half + k:D:KD], ident)
                    mm.then_inc(*xpe.done(f"xT{half}"))

            def body(b, s, j, following=True):
                place = eng.value_load(keep["block_place"][0:1, bass.ds(b, 1)], min_val=0, max_val=1)
                eng.wait_ge(*xact.after("xT0", b))
                eng.wait_ge(*xdve.after("xT1", b))
                eng.wait_ge(w13_loaded[s], 32 * (j + 1))
                for name, w, out, free in (("h1", w1, H1, act.after("a", b - 1)), ("h3", w3, H3, dve.after("g", b - 1))):
                    eng.wait_ge(*free)
                    for k in range(KD):
                        mm = eng.matmul(out[:, :], xT[:, s, k, :], w[:, bass.ds(place, 1), k, :], start=(k == 0), stop=(k == KD - 1))
                    mm.then_inc(*pe.done(name))
                if following:
                    turn_x(b + 1, 1 - s, j + s)
                eng.wait_ge(*dve.after("g", b))
                eng.wait_ge(*dve.after("gT", b - 1))
                for k in range(KE):
                    mm = eng.transpose(GT[:, k * P:(k + 1) * P], g[:, k:DE:KE], ident)
                mm.then_inc(*pe.done("gT"))
                eng.wait_ge(w2_loaded[s], 16 * (j + 1))
                eng.wait_ge(*dve.after("gT", b))
                for half in (0, 1):
                    eng.wait_ge(*(dve.after("y1", b - 1) if half else act.after("y0", b - 1)))
                    for k in range(KE):
                        mm = eng.matmul(Y[half][:, :], gT[:, k, :], w2[:, bass.ds(place, 1), k, half * 512:(half + 1) * 512],
                                        start=(k == 0), stop=(k == KE - 1))
                    mm.then_inc(*pe.done(f"y{half}"))

            turn_x(0, 0, 0)
            with eng.Fori(0, PAIRED) as j:
                for s in (0, 1):
                    body(2 * j + s, s, j)
            body(BLOCKS - 1, 0, PAIRED, following=False)

        @block.scalar
        def _(eng):
            act.begin(eng)
            xact.begin(eng)
            begin_stores(eng, stored)

            def copy_x(b, s):
                eng.wait_ge(*xpe.after("xT0", b))
                eng.wait_ge(*pe.after("h3", b - 1))
                eng.copy(xT[:, s, 0:4, :], XT[0][:, :].rearrange("p (k t) -> p k t", k=4)).then_inc(*xact.done("xT0"))

            def body(b, s, j, following=True):
                eng.wait_ge(*pe.after("h1", b))
                eng.wait_ge(*dve.after("g", b - 1))
                eng.activation(a[:, :], H1[:, :], ACT.Silu).then_inc(*act.done("a"))
                if following:
                    copy_x(b + 1, 1 - s)
                eng.wait_ge(*pe.after("y0", b))
                eng.wait_ge(stored[s], 16 * (j + 1))
                eng.copy(y[:, s, 0:512], Y[0][:, :]).then_inc(*act.done("y0"))
                eng.wait_ge(*act.after("y0", b))
                eng.wait_ge(*dve.after("y1", b))
                eng.dma_start(io["ypad"][bass.ds(b * P, P), :], y[:, s, :]).then_inc(stored[s], 16)

            copy_x(0, 0)
            with eng.Fori(0, PAIRED) as j:
                for s in (0, 1):
                    body(2 * j + s, s, j)
            body(BLOCKS - 1, 0, PAIRED, following=False)
            eng.wait_ge(stored[0], 16 * (PAIRED + 2))
            eng.wait_ge(stored[1], 16 * (PAIRED + 1))

        @block.vector
        def _(eng):
            dve.begin(eng)
            xdve.begin(eng)

            def copy_x(b, s):
                eng.wait_ge(*xpe.after("xT1", b))
                eng.wait_ge(*pe.after("h3", b - 1))
                eng.tensor_copy(xT[:, s, 4:8, :], XT[1][:, :].rearrange("p (k t) -> p k t", k=4))\
                   .then_inc(*xdve.done("xT1"))

            def body(b, s, j, following=True):
                eng.wait_ge(*act.after("a", b))
                eng.wait_ge(*pe.after("h3", b))
                eng.wait_ge(*pe.after("gT", b - 1))
                eng.tensor_tensor(g[:, :], a[:, :], H3[:, :], ALU.mult).then_inc(*dve.done("g"))
                if following:
                    copy_x(b + 1, 1 - s)
                eng.wait_ge(*pe.after("gT", b))
                eng.wait_ge(*pe.after("y1", b - 1))
                eng.tensor_copy(gT[:, :, :], GT[:, :].rearrange("p (k t) -> p k t", k=KE)).then_inc(*dve.done("gT"))
                eng.wait_ge(*pe.after("y1", b))
                eng.wait_ge(stored[s], 16 * (j + 1))
                eng.tensor_copy(y[:, s, 512:D], Y[1][:, :]).then_inc(*dve.done("y1"))

            copy_x(0, 0)
            with eng.Fori(0, PAIRED) as j:
                for s in (0, 1):
                    body(2 * j + s, s, j)
            body(BLOCKS - 1, 0, PAIRED, following=False)


def combine(nc, io, keep):
    with ExitStack() as ctx:
        def sb(name, shape, dt=F32):
            return ctx.enter_context(nc.sbuf_tensor(name, shape, dt))

        def sem(name):
            return ctx.enter_context(nc.semaphore(name))

        gain, offset = sb("z_gain", [P, D]), sb("z_offset", [P, D])
        h = sb("z_h", [P, 2, D])
        idx = sb("z_idx", [P, 2, 2], I32)
        y = sb("z_y", [P, 2, 2, D])
        z = sb("z_z", [P, D])
        stats, mv, std = sb("z_stats", [P, 2, 6]), sb("z_mv", [P, 4]), sb("z_std", [P, 1])
        out = sb("z_out", [P, 2, D])
        weights_loaded = sem("z_weights_loaded")
        h_loaded = [sem(f"z_h_loaded{s}") for s in (0, 1)]
        y_loaded = [sem(f"z_y_loaded{s}") for s in (0, 1)]
        stored = [sem(f"z_stored{s}") for s in (0, 1)]
        held, pool_held = sem("z_held"), sem("z_pool_held")
        pool = Steps(sem("z_pool_steps"), ["idx"])
        act = Steps(sem("z_act_steps"), ["std"])
        dve = Steps(sem("z_dve_steps"), ["y0", "y1", "z", "stats", "mv", "eps", "rstd", "norm", "gain", "out"])
        block = ctx.enter_context(nc.Block())

        @block.sync
        def _(sp):
            begin_stores(sp, stored)
            sp.dma_start(gain[:, :], io["ln2_g"].broadcast_to([P, D])).then_inc(weights_loaded, 16)
            sp.dma_start(offset[:, :], io["ln2_b"].broadcast_to([P, D])).then_inc(weights_loaded, 16)

            def load(t, s):
                sp.dma_start(h[:, s, :], io["h"][bass.ds(t * P, P), :]).then_inc(h_loaded[s], 16)

            def store(t, s, dst, rows=P):
                sp.wait_ge(*dve.after("out", t))
                sp.dma_start(dst, out[0:rows, s, :]).then_inc(stored[s], 16)

            load(0, 0)
            load(1, 1)
            with sp.Fori(0, NT // 2 - 1) as j:
                for s in (0, 1):
                    t = 2 * j + s
                    store(t, s, io["y_prompt"][0, bass.ds(t * P, P), :])
                    load(t + 2, s)
            store(NT - 2, 0, io["y_prompt"][0, (NT - 2) * P:(NT - 1) * P, :])
            load(NT, 0)
            store(NT - 1, 1, io["y_prompt"][0, (NT - 1) * P:NT * P, :])
            store(NT, 0, io["y_sample"][0], NEW)
            sp.wait_ge(stored[0], 16 * (NT // 2 + 2))
            sp.wait_ge(stored[1], 16 * (NT // 2 + 1))

        @block.gpsimd
        def _(eng):
            pool.begin(eng)

            def tile(t, s, j):
                rows = NEW if isinstance(t, int) and t == NT else P
                eng.wait_ge(*dve.after("y1", t - 1))
                hold(eng, pool_held)
                eng.tensor_copy(idx[:, s, :].unsqueeze(1), keep["row"][:, bass.ds(t, 1), :]).then_inc(*pool.done("idx"))
                eng.wait_ge(*pool.after("idx", t))
                hold(eng, pool_held)
                for i in (0, 1):
                    eng.indirect_dma_start(out=y[0:rows, s, i, :], out_offset=None, in_=io["ypad"][:, :],
                                           in_offset=bass.IndirectOffsetOnAxis(ap=idx[0:rows, s, i:i + 1], axis=0),
                                           bounds_check=BLOCKS * P - 1, oob_is_err=False).then_inc(y_loaded[s], 16)

            over_tiles(eng, tile)

        @block.scalar
        def _(eng):
            act.begin(eng)

            def tile(t, s, j):
                eng.wait_ge(*dve.after("eps", t))
                eng.activation(std[:, :], mv[:, 2:3], ACT.Sqrt).then_inc(*act.done("std"))

            over_tiles(eng, tile)

        @block.vector
        def _(eng):
            dve.begin(eng)
            eng.wait_ge(weights_loaded, 32)

            def tile(t, s, j):
                g = keep["gate"][:, bass.ds(t, 1), :]
                eng.wait_ge(y_loaded[s], 32 * (j + 1))
                eng.wait_ge(*dve.after("out", t - 1))
                g0, g1 = (g[:, :, i:i + 1].rearrange("p o i -> p (o i)") for i in (0, 1))
                eng.tensor_scalar(z[:, :], y[:, s, 0, :], g0, None, ALU.mult).then_inc(*dve.done("y0"))
                eng.wait_ge(*dve.after("y0", t))
                eng.scalar_tensor_tensor(out=z[:, :], in0=y[:, s, 1, :], scalar=g1, in1=z[:, :], op0=ALU.mult,
                                         op1=ALU.add).then_inc(*dve.done("y1"))
                eng.wait_ge(h_loaded[s], 16 * (j + 1))
                eng.wait_ge(*dve.after("y1", t))
                eng.scalar_tensor_tensor(out=z[:, :], in0=h[:, s, :], scalar=ALPHA, in1=z[:, :], op0=ALU.mult,
                                         op1=ALU.add).then_inc(*dve.done("z"))
                eng.wait_ge(*dve.after("z", t))
                eng.wait_ge(stored[s], 16 * (j + 1))
                layer_norm_steps(eng, dve, held, act.after("std", t), z[:, :], stats, mv, std[:, :], out[:, s, :],
                                 gain[:, :], offset[:, :], "", t)

            over_tiles(eng, tile)


def build(nc, io):
    with ExitStack() as ctx:
        keep = constants(nc, ctx)
        fox_projection(nc, io, keep)
        rwkv(nc, io, keep)
        with ExitStack() as inner:
            keep["fy"] = inner.enter_context(nc.sbuf_tensor("fy", [P, TILES, DG], F32))
            fox_prompt(nc, io, keep)
            fox_sample(nc, io, keep)
            mix(nc, io, keep)
        route(nc, io, keep)
        dispatch(nc, io, keep)
        experts(nc, io, keep)
        combine(nc, io, keep)


_INS = ['x_prompt', 'x_sample', 'cache_fox_k', 'cache_fox_v', 'cache_fox_logf', 'state_rwkv', 'state_rwkv_shift',
        'w_in', 'rwkv_mu', 'rwkv_w0', 'rwkv_w2', 'rwkv_a0', 'rwkv_a2', 'rwkv_g2', 'rwkv_k_k', 'rwkv_k_a', 'rwkv_r_k',
        'rwkv_lnx_w', 'rwkv_lnx_b', 'fox_b_f', 'fox_q_g', 'fox_k_g', 'w_out', 'ln1_g', 'ln1_b', 'ln2_g', 'ln2_b',
        'router_w', 'router_b', 'moe_w1', 'moe_w3', 'moe_w2']
_OUTS = [('y_prompt', (1, SEQ, D), (1, SEQ, D)), ('y_sample', (1, NEW, D), (1, NEW, D)),
         ('p_k', (SEQ, DG), (1, 1, SEQ, HEADS, DH)), ('p_v', (SEQ, DG), (1, 1, SEQ, HEADS, DH)),
         ('p_lf', (SEQ, HEADS), (1, 1, SEQ, HEADS)), ('p_rwkv', (HEADS, DH, DH), (1, 1, HEADS, DH, DH)),
         ('p_shift', (1, RCOLS), (1, 1, 1, RCOLS)),
         ('s_k', (NEW, DG), (1, 1, NEW, HEADS, DH)), ('s_v', (NEW, DG), (1, 1, NEW, HEADS, DH)),
         ('s_lf', (NEW, HEADS), (1, 1, NEW, HEADS)), ('s_rwkv', (HEADS, DH, DH), (1, 1, HEADS, DH, DH)),
         ('s_shift', (1, RCOLS), (1, 1, 1, RCOLS))]
_SCRATCH = [('qT', (PAIRS, P, ROWS), F32), ('kT', (PAIRS, P, ROWS), F32), ('cT', (HEADS, ROWS), F32),
            ('ryT', (PAIRS, P, ROWS), F32), ('og', (ROWS, DG), F32), ('h', (ROWS, D), F32),
            ('ypad', (BLOCKS * P, D), F32)]


def kernel(**inputs):
    import numpy as np
    import concourse.bacc as bacc
    from concourse.bass_utils import run_bass_kernel_spmd

    nc = bacc.Bacc("TRN2", target_bir_lowering=False, num_devices=1)
    arrays, io = {}, {}
    for name in _INS:
        a = np.ascontiguousarray(inputs[name])
        arrays[f"in_{name}"] = a
        io[name] = nc.dram_tensor(f"in_{name}", a.shape, mybir.dt.from_np(a.dtype), kind="ExternalInput").ap()
    for name, shape, _ in _OUTS:
        io[name] = nc.dram_tensor(f"out_{name}", shape, F32, kind="ExternalOutput").ap()
    for name, shape, dt in _SCRATCH:
        io[name] = nc.dram_tensor(f"scratch_{name}", shape, dt, kind="Internal").ap()
    build(nc, io)
    r = run_bass_kernel_spmd(nc, [arrays], core_ids=[0])
    return tuple(r.results[0][f"out_{name}"].reshape(shape) for name, _, shape in _OUTS)
```

```python
from contextlib import ExitStack

import concourse.bass as bass
from concourse import mybir

F32 = mybir.dt.float32
I32 = mybir.dt.int32
U32 = mybir.dt.uint32
ALU = mybir.AluOpType
ACT = mybir.ActivationFunctionType
AX_X = mybir.AxisListType.X

P = 128
D = 1024
KD = D // P
SEQ = 2048
NEW = 32
PAST = 4096
NT = SEQ // P
TILES = NT + 1
ROWS = TILES * P
HEADS = 8
DH = 64
DG = HEADS * DH
PAIRS = HEADS // 2
LORA = 64
RCOLS = 3 * DG + 2 * LORA + P
FCOLS = 3 * DG + HEADS + DG
RCH = RCOLS // P
EXPERTS = 32
GROUPS = 4
PER_GROUP = EXPERTS // GROUPS
DE = D // 2
TOKENS = SEQ + NEW
BLOCKS = (2 * TOKENS + EXPERTS * (P - 1)) // P
ALPHA = 2.0 ** 0.25
LN_EPS = 1e-5
GN_EPS = 64e-5
QK_EPS = 1e-6
SCALE = DH ** -0.5
DECAY = 0.6065306597126334
FAR = -1e30


class Steps:

    def __init__(self, sem, names, ahead=1):
        self.sem, self.names, self.ahead, self.at = sem, names, ahead, 0
        assert len(set(names)) == len(names)

    def begin(self, eng):
        eng.nop().then_inc(self.sem, self.ahead * len(self.names))

    def done(self, name):
        assert self.names[self.at % len(self.names)] == name, (self.names[self.at % len(self.names)], name)
        self.at += 1
        return self.sem, 1

    def after(self, name, t):
        return self.sem, (t + self.ahead) * len(self.names) + self.names.index(name) + 1


def hold(eng, sem):
    eng.sem_inc(sem, 1)


def begin_stores(eng, stored, per_tile=16):
    for s in stored:
        eng.sem_inc(s, per_tile)


def over_tiles(eng, tile, **last):
    with eng.Fori(0, NT // 2) as j:
        for slot in (0, 1):
            tile(2 * j + slot, slot, j)
    tile(NT, 0, NT // 2, **last)
def constants(nc, ctx):
    keep = {}

    def sb(name, shape, dt=F32):
        keep[name] = ctx.enter_context(nc.sbuf_tensor(name, shape, dt))
        return keep[name]

    ready = ctx.enter_context(nc.semaphore("constants_ready"))
    keep["constants_ready"] = ready
    ident, ones, upto, before, after = (sb(n, [P, P]) for n in ("ident", "ones", "upto", "before", "after"))
    halves, causal = sb("halves", [P, P]), sb("causal", [P, P])
    sb("expert_id", [P, EXPERTS])
    sb("group_of", [P, EXPERTS])
    sb("expert", [P, TILES, 2])
    sb("logits", [P, TILES, EXPERTS])
    sb("gate", [P, TILES, 2])
    sb("rank", [P, TILES, 2])
    sb("counts", [P, EXPERTS])
    sb("row", [P, TILES, 2], I32)
    sb("frame_of", [P, BLOCKS], I32)
    sb("block_expert", [1, BLOCKS], I32)
    sb("block_fresh", [1, BLOCKS], I32)
    sb("block_place", [1, BLOCKS], I32)
    ids = sb("ids", [P, 2, EXPERTS], I32)
    shapes = [
        (ident, 0.0, ALU.not_equal, -1, 1, 0, 1.0),
        (ones, 1.0, None, 0, 0, 0, 0.0),
        (upto, 1.0, ALU.is_ge, 1, -1, 0, 0.0),
        (before, 1.0, ALU.is_gt, 1, -1, 0, 0.0),
        (after, 1.0, ALU.is_gt, -1, 1, 0, 0.0),
        (causal, 0.0, ALU.is_ge, -1, 1, 0, FAR),
    ]
    n = [0]
    with nc.Block() as block:
        @block.gpsimd
        def _(pool):
            def step(ins):
                n[0] += 1
                ins.then_inc(ready, 1)
                return n[0]

            for out, back, op, col, row, base, fill in shapes:
                count = step(pool.memset(out[:, :], back))
                if op is not None:
                    pool.wait_ge(ready, count)
                    step(pool.affine_select(out=out[:, :], in_=out[:, :], compare_op=op, fill=fill, base=base,
                                            pattern=[[col, P]], channel_multiplier=row))
            step(pool.iota(ids[:, 0, :], pattern=[[1, EXPERTS]], base=0, channel_multiplier=0))
            count = step(pool.iota(ids[:, 1, :], pattern=[[1, GROUPS], [0, PER_GROUP]], base=0, channel_multiplier=0))
            pool.wait_ge(ready, count)
            step(pool.tensor_copy(keep["expert_id"][:, :], ids[:, 0, :]))
            step(pool.tensor_copy(keep["group_of"][:, :], ids[:, 1, :]))
            count = step(pool.memset(halves[:, :], 0.0))
            pool.wait_ge(ready, count)
            step(pool.memset(halves[0:DH, 0:DH], 1.0))
            step(pool.memset(halves[DH:P, DH:P], 1.0))
            pool.wait_ge(ready, n[0])
    keep["constants"] = n[0]
    return keep
def fox_projection(nc, io, keep):
    with ExitStack() as ctx:
        def sb(name, shape, dt=F32):
            return ctx.enter_context(nc.sbuf_tensor(name, shape, dt))

        def sem(name):
            return ctx.enter_context(nc.semaphore(name))

        psum = [ctx.enter_context(nc.psum_tensor(f"fp{b}", [P, 512], F32)) for b in range(8)]
        X, Q, K, V, G, S, T = psum[0:2], psum[2], psum[3], psum[4], psum[5], psum[6], psum[7]
        w = sb("f_w", [P, KD, FCOLS])
        x = sb("f_x", [P, 2, D])
        xT = sb("f_xT", [P, 2, KD, P])
        bf = sb("f_bf", [P, HEADS])
        qg = sb("f_qg", [P, DH])
        kg = sb("f_kg", [P, DH])
        carry = sb("f_carry", [P, HEADS])
        fb = sb("f_fb", [P, 4, HEADS])
        qk = sb("f_qk", [P, 2, DG])
        sq = sb("f_sq", [P, 2, DG])
        ss = sb("f_ss", [P, 3, 2 * HEADS])
        qn = sb("f_qn", [P, DG])
        kn = sb("f_kn", [P, 2, DG])
        vn = sb("f_vn", [P, 2, DG])
        og = sb("f_og", [P, 2, DG])
        lf = sb("f_lf", [P, 2, HEADS])
        negc = sb("f_negc", [P, HEADS])
        qT = sb("f_qT", [P, 2, DG])
        kT = sb("f_kT", [P, 2, DG])
        cT = sb("f_cT", [HEADS, 2, P])

        weights_loaded = sem("f_weights_loaded")
        W_PARTS = {"fg": (3 * DG, FCOLS), "q": (0, DG), "k": (DG, 2 * DG), "v": (2 * DG, 3 * DG)}
        w_loaded = {name: sem(f"f_w_{name}_loaded") for name in W_PARTS}
        x_loaded = [sem(f"f_x_loaded{s}") for s in (0, 1)]
        stored = [sem(f"f_stored{s}") for s in (0, 1)]
        pool_ready = sem("f_pool_ready")
        carry_zeroed = sem("f_carry_zeroed")
        xpe = Steps(sem("f_x_pe_steps"), ["xT0", "xT1"])
        xact = Steps(sem("f_x_act_steps"), ["xT0", "xT1"])
        pe = Steps(sem("f_pe_steps"), ["f", "q", "k", "cum", "v", "g", "qT", "cT", "kT"])
        act = Steps(sem("f_act_steps"), ["e", "l", "q", "k", "rms", "v", "g", "qT"])
        dve = Steps(sem("f_dve_steps"), [
            "fb", "negabs", "logf", "negc", "carry", "sq0", "ss0", "sq1", "ss1", "mean", "rs",
            "q1", "q2", "k1", "k2", "cT", "kT"])
        STORES = 7

        block = ctx.enter_context(nc.Block())
        w_rows = io["w_in"][0].rearrange("(p k) n -> p k n", k=KD)

        @block.sync
        def _(sp):
            begin_stores(sp, stored, 16 * STORES)
            for slot in (0, 1):
                sp.dma_start(x[:, slot, :], io["x_prompt"][0, slot * P:(slot + 1) * P, :]).then_inc(x_loaded[slot], 16)
            with nc.allow_non_contiguous_dma(reason="small rows for all partitions"):
                sp.dma_start(bf[:, :], io["fox_b_f"].broadcast_to([P, HEADS])).then_inc(weights_loaded, 16)
                sp.dma_start(qg[:, :], io["fox_q_g"].broadcast_to([P, DH])).then_inc(weights_loaded, 16)
                sp.dma_start(kg[:, :], io["fox_k_g"].broadcast_to([P, DH])).then_inc(weights_loaded, 16)
            for name, (a, b) in W_PARTS.items():
                sp.dma_start(w[:, :, a:b], w_rows[:, :, RCOLS + a:RCOLS + b]).then_inc(w_loaded[name], 16)

            def stores(t, slot, rows, dst_row, k_out, v_out, lf_out):
                sp.wait_ge(*act.after("qT", t))
                sp.wait_ge(*dve.after("kT", t))
                with nc.allow_non_contiguous_dma(reason="rows of 8 gates"):
                    sp.dma_start(lf_out, lf[0:rows, slot, :]).then_inc(stored[slot], 16)
                sp.dma_start(k_out, kn[0:rows, slot, :]).then_inc(stored[slot], 16)
                sp.dma_start(v_out, vn[0:rows, slot, :]).then_inc(stored[slot], 16)
                sp.dma_start(io["og"][bass.ds(dst_row, P), :], og[:, slot, :]).then_inc(stored[slot], 16)
                for kind, src in (("qT", qT), ("kT", kT)):
                    sp.dma_start(io[kind][:, :, bass.ds(dst_row, P)].rearrange("a p t -> p a t"),
                                 src[:, slot, :].rearrange("p (a t) -> p a t", a=PAIRS)).then_inc(stored[slot], 16)
                sp.dma_start(io["cT"][:, bass.ds(dst_row, P)], cT[:, slot, :]).then_inc(stored[slot], 16)

            def stores_of(t, slot):
                at = t * P
                stores(t, slot, P, at, io["p_k"][bass.ds(at, P), :], io["p_v"][bass.ds(at, P), :],
                       io["p_lf"][bass.ds(at, P), :])

            sp.dma_start(keep["w_rwkv"][:, :, :], w_rows[:, :, 0:RCOLS]).then_inc(keep["w_rwkv_loaded"], 16)
            with sp.Fori(0, NT // 2 - 1) as j:
                for slot in (0, 1):
                    t = 2 * j + slot
                    sp.wait_ge(*xpe.after("xT1", t))
                    sp.dma_start(x[:, slot, :], io["x_prompt"][0, bass.ds((t + 2) * P, P), :]).then_inc(
                        x_loaded[slot], 16)
                    stores_of(t, slot)
            sp.wait_ge(pool_ready, 1)
            sp.dma_start(x[0:NEW, 0, :], io["x_sample"][0]).then_inc(x_loaded[0], 16)
            stores_of(NT - 2, 0)
            stores_of(NT - 1, 1)
            stores(NT, 0, NEW, NT * P, io["s_k"], io["s_v"], io["s_lf"])
            sp.wait_ge(stored[0], 16 * STORES * (NT // 2 + 2))
            sp.wait_ge(stored[1], 16 * STORES * (NT // 2 + 1))

        @block.gpsimd
        def _(pool):
            pool.wait_ge(*xpe.after("xT1", NT - 2))
            pool.memset(x[:, 0, :], 0.0).then_inc(pool_ready, 1)

        @block.tensor
        def _(eng):
            xpe.begin(eng)
            pe.begin(eng)
            eng.wait_ge(keep["constants_ready"], keep["constants"])

            def turn_x(u, slot, turn):
                eng.wait_ge(x_loaded[slot], 16 * (turn + 1))
                for half in (0, 1):
                    eng.wait_ge(*xact.after(f"xT{half}", u - 1))
                    for k in range(4):
                        c = half * 4 + k
                        mm = eng.transpose(X[half][:, k * P:(k + 1) * P], x[:, slot, c:D:KD], keep["ident"][:, :])
                    mm.then_inc(*xpe.done(f"xT{half}"))

            def tile(t, slot, j, following=True):
                eng.wait_ge(*xact.after("xT1", t))
                for name, a, n, out, owner in (("f", 3 * DG, HEADS, S[:, 0:HEADS], (dve, "fb")),
                                               ("q", 0, DG, Q[:, :], (act, "q")),
                                               ("k", DG, DG, K[:, :], (act, "k")),
                                               ("v", 2 * DG, DG, V[:, :], (act, "v")),
                                               ("g", 3 * DG + HEADS, DG, G[:, :], (act, "g"))):
                    if name != "g":
                        eng.wait_ge(w_loaded["fg" if name == "f" else name], 16)
                    if name == "g" and following:
                        turn_x(t + 1, 1 - slot, j + slot)
                    if name == "f":
                        eng.wait_ge(*dve.after("cT", t - 1))
                    else:
                        eng.wait_ge(*owner[0].after(owner[1], t - 1))
                    for k in range(KD):
                        mm = eng.matmul(out, xT[:, slot, k, :], w[:, k, a:a + n], start=(k == 0), stop=(k == KD - 1))
                    mm.then_inc(*pe.done(name))
                    if name == "k":
                        eng.wait_ge(*dve.after("logf", t))
                        eng.matmul(S[:, 8:16], keep["upto"][:, :], lf[:, slot, :], start=True, stop=True)
                        eng.matmul(S[:, 16:24], keep["ones"][:, :], lf[:, slot, :], start=True, stop=True)\
                           .then_inc(*pe.done("cum"))
                eng.wait_ge(*dve.after("q2", t))
                eng.wait_ge(*dve.after("kT", t - 1))
                for a in range(PAIRS):
                    mm = eng.transpose(T[:, a * P:(a + 1) * P], qn[:, a * P:(a + 1) * P], keep["ident"][:, :])
                mm.then_inc(*pe.done("qT"))
                eng.wait_ge(*dve.after("negc", t))
                eng.transpose(S[0:HEADS, 128:128 + P], negc[:, :], keep["ident"][:, :]).then_inc(*pe.done("cT"))
                eng.wait_ge(*dve.after("k2", t))
                eng.wait_ge(*act.after("qT", t))
                for a in range(PAIRS):
                    mm = eng.transpose(T[:, a * P:(a + 1) * P], kn[:, slot, a * P:(a + 1) * P], keep["ident"][:, :])
                mm.then_inc(*pe.done("kT"))

            turn_x(0, 0, 0)
            over_tiles(eng, tile, following=False)

        @block.scalar
        def _(eng):
            xact.begin(eng)
            act.begin(eng)

            def copy_x(u, slot):
                for half in (0, 1):
                    eng.wait_ge(*xpe.after(f"xT{half}", u))
                    if not (isinstance(u, int) and u == 0):
                        eng.wait_ge(*pe.after("g", u - 2))
                    eng.copy(xT[:, slot, half * 4:half * 4 + 4, :], X[half][:, :].rearrange("p (k t) -> p k t", k=4))\
                       .then_inc(*xact.done(f"xT{half}"))

            def tile(t, slot, j, following=True):
                eng.wait_ge(*dve.after("negabs", t))
                eng.activation(fb[:, 2, :], fb[:, 1, :], ACT.Exp).then_inc(*act.done("e"))
                eng.wait_ge(*act.after("e", t))
                eng.activation(fb[:, 3, :], fb[:, 2, :], ACT.Ln, bias=1.0).then_inc(*act.done("l"))
                for n, (name, bank) in enumerate((("q", Q), ("k", K))):
                    eng.wait_ge(*pe.after(name, t))
                    eng.wait_ge(*dve.after(f"{name}1", t - 1))
                    eng.copy(qk[:, n, :], bank[:, :]).then_inc(*act.done(name))
                eng.wait_ge(*dve.after("mean", t))
                eng.activation(ss[:, 1, :], ss[:, 0, :], ACT.Sqrt).then_inc(*act.done("rms"))
                eng.wait_ge(stored[slot], 16 * STORES * (j + 1))
                eng.wait_ge(*pe.after("v", t))
                eng.copy(vn[:, slot, :], V[:, :]).then_inc(*act.done("v"))
                if following:
                    copy_x(t + 1, 1 - slot)
                eng.wait_ge(*pe.after("g", t))
                eng.activation(og[:, slot, :], G[:, :], ACT.Sigmoid).then_inc(*act.done("g"))
                eng.wait_ge(*pe.after("qT", t))
                eng.copy(qT[:, slot, :], T[:, :]).then_inc(*act.done("qT"))

            copy_x(0, 0)
            over_tiles(eng, tile, following=False)

        @block.vector
        def _(eng):
            dve.begin(eng)
            eng.memset(carry[:, :], 0.0).then_inc(carry_zeroed, 1)
            eng.wait_ge(carry_zeroed, 1)
            eng.wait_ge(weights_loaded, 48)
            eng.tensor_scalar(qg[:, :], qg[:, :], SCALE, None, ALU.mult).then_inc(carry_zeroed, 1)
            eng.wait_ge(carry_zeroed, 2)

            def tile(t, slot, j):
                eng.wait_ge(*pe.after("f", t))
                eng.tensor_tensor(fb[:, 0, :], S[:, 0:HEADS], bf[:, :], ALU.add).then_inc(*dve.done("fb"))
                eng.wait_ge(*dve.after("fb", t))
                eng.scalar_tensor_tensor(out=fb[:, 1, :], in0=fb[:, 0, :], scalar=-1.0, in1=fb[:, 0, :],
                                         op0=ALU.mult, op1=ALU.min)\
                   .then_inc(*dve.done("negabs"))
                eng.wait_ge(*act.after("l", t))
                eng.wait_ge(stored[slot], 16 * STORES * (j + 1))
                eng.scalar_tensor_tensor(out=lf[:, slot, :], in0=fb[:, 0, :], scalar=0.0, in1=fb[:, 3, :],
                                         op0=ALU.min, op1=ALU.subtract).then_inc(*dve.done("logf"))
                eng.wait_ge(*pe.after("cum", t))
                eng.wait_ge(*pe.after("cT", t - 1))
                eng.wait_ge(*dve.after("carry", t - 1))
                eng.scalar_tensor_tensor(out=negc[:, :], in0=S[:, 8:16], scalar=-1.0, in1=carry[:, :],
                                         op0=ALU.mult, op1=ALU.subtract).then_inc(*dve.done("negc"))
                eng.wait_ge(*dve.after("negc", t))
                eng.tensor_tensor(carry[:, :], S[:, 16:24], carry[:, :], ALU.add).then_inc(*dve.done("carry"))
                for n, name in enumerate("qk"):
                    eng.wait_ge(*act.after(name, t))
                    eng.tensor_tensor(sq[:, n, :], qk[:, n, :], qk[:, n, :], ALU.mult).then_inc(*dve.done(f"sq{n}"))
                    eng.wait_ge(*dve.after(f"sq{n}", t))
                    eng.tensor_reduce(ss[:, 0, n * HEADS:(n + 1) * HEADS],
                                      sq[:, n, :].rearrange("p (h d) -> p h d", d=DH), AX_X, ALU.add)\
                       .then_inc(*dve.done(f"ss{n}"))
                eng.wait_ge(*dve.after("ss1", t))
                eng.tensor_scalar(ss[:, 0, :], ss[:, 0, :], 1.0 / DH, QK_EPS, ALU.mult, ALU.add)\
                   .then_inc(*dve.done("mean"))
                eng.wait_ge(*act.after("rms", t))
                eng.reciprocal(ss[:, 2, :], ss[:, 1, :]).then_inc(*dve.done("rs"))
                eng.wait_ge(*dve.after("rs", t))
                eng.wait_ge(*pe.after("qT", t - 1))
                for n, (name, out, g) in enumerate((("q", qn[:, :], qg), ("k", kn[:, slot, :], kg))):
                    heads = out.rearrange("p (h d) -> p h d", d=DH)
                    rs = ss[:, 2, n * HEADS:(n + 1) * HEADS].unsqueeze(2).broadcast_to([P, HEADS, DH])
                    eng.tensor_tensor(heads, qk[:, n, :].rearrange("p (h d) -> p h d", d=DH), rs, ALU.mult)\
                       .then_inc(*dve.done(f"{name}1"))
                    eng.wait_ge(*dve.after(f"{name}1", t))
                    eng.tensor_tensor(heads, heads, g[:, :].unsqueeze(1).broadcast_to([P, HEADS, DH]), ALU.mult)\
                       .then_inc(*dve.done(f"{name}2"))
                eng.wait_ge(*pe.after("cT", t))
                eng.tensor_copy(cT[:, slot, :], S[0:HEADS, 128:128 + P]).then_inc(*dve.done("cT"))
                eng.wait_ge(*pe.after("kT", t))
                eng.tensor_copy(kT[:, slot, :], T[:, :]).then_inc(*dve.done("kT"))

            with eng.Fori(0, NT // 2) as j:
                for slot in (0, 1):
                    tile(2 * j + slot, slot, j)
            eng.wait_ge(*dve.after("carry", NT - 1))
            eng.memset(carry[:, :], 0.0).then_inc(carry_zeroed, 1)
            eng.wait_ge(carry_zeroed, 3)
            tile(NT, 0, NT // 2)
LEVELS = 7


def rwkv(nc, io, keep):
    with ExitStack() as ctx:
        def sb(name, shape, dt=F32):
            return ctx.enter_context(nc.sbuf_tensor(name, shape, dt))

        def sem(name):
            return ctx.enter_context(nc.semaphore(name))

        bank = [ctx.enter_context(nc.psum_tensor(f"rp{b}", [P, 512], F32)) for b in range(8)]
        w = keep["w_rwkv"]
        w2 = sb("r_w2", [P, DG])
        g2 = sb("r_g2", [P, DG])
        mu = sb("r_mu", [P, RCH])
        par = sb("r_par", [P, 7, PAIRS])
        one_ka = sb("r_one_ka", [P, PAIRS])
        x = sb("r_x", [P, 2, D])
        xT = sb("r_xT", [P, KD, P])
        pr = sb("r_pr", [P, RCH, P + 1])
        last = sb("r_last", [P, RCH])
        xs = sb("r_xs", [P, RCH, P])
        th = sb("r_th", [LORA, P])
        sg = sb("r_sg", [P, P])

        def quad(name, n=1):
            return sb(name, [P, PAIRS, n * P]) if n == 1 else sb(name, [P, PAIRS, n, P])

        ld, a, g, kk, sq, nrm, kf, beta = (quad("r_" + n) for n in ("ld", "a", "g", "kk", "sq", "nrm", "kf", "beta"))
        cum = sb("r_cum", [P, PAIRS, P + 1])
        e1 = sb("r_e1", [P, PAIRS, P + 1])
        e2, bt, kt, bv = (quad("r_" + n) for n in ("e2", "bt", "kt", "bv"))
        ar = quad("r_ar", 2)
        cm = sb("r_cm", [P, 3, PAIRS])
        vtok, btok, ktok = (quad("r_" + n) for n in ("vtok", "btok", "ktok"))
        mab = sb("r_mab", [P, 2, PAIRS, P])
        mrb = sb("r_mrb", [P, 2, PAIRS, P])
        mk = sb("r_mk", [P, 2, PAIRS, 2, P])
        X = sb("r_X", [P, 2, PAIRS, P])
        XT = sb("r_XT", [P, 2, PAIRS, P])
        t1 = sb("r_t1", [P, 2, PAIRS, P])
        rhs = sb("r_rhs", [P, 2, PAIRS, DH])
        sa = sb("r_sa", [P, 2, PAIRS, DH])
        st = sb("r_st", [P, PAIRS, DH])
        sbar = sb("r_sbar", [P, PAIRS, DH])
        y = quad("r_y")
        ysq = quad("r_ysq")
        ys = quad("r_ys")
        out = sb("r_out", [P, 2, PAIRS, P])
        shift_in = sb("r_shift_in", [P, RCH])
        st_in = sb("r_st_in", [DH, HEADS, DH])
        io_st = sb("r_io_st", [DH, HEADS, DH])
        masks_f = sb("r_masks_f", [P, P])
        mask = sb("r_mask", [P, 2, LEVELS, P], I32)
        mask2 = sb("r_mask2", [P, 2, P])

        weights_loaded = sem("r_weights_loaded")
        x_loaded = [sem(f"r_x_loaded{s}") for s in (0, 1)]
        out_stored = [sem(f"r_out_stored{s}") for s in (0, 1)]
        masks_ready = sem("r_masks_ready")
        pad_zeroed = sem("r_pad_zeroed")
        prepared = sem("r_prepared")
        MASKS = 2 * LEVELS + 2
        cleared = sem("r_cleared")
        pool_held = sem("r_pool_held")
        held = sem("r_held")
        state_pe, state_dve, state_dma = sem("r_state_pe"), sem("r_state_dve"), sem("r_state_dma")
        shift_dma, stream_loaded = sem("r_shift_dma"), sem("r_stream_loaded")

        uses = [("zw", 2, "act", "ld"), ("za", 3, "act", "a"), ("zg", 4, "act", "g"), ("ss", 5, "act", "nrm"),
                ("vT", 6, "act", "vT"), ("bs", 7, "dve", "bv"), ("bT", 6, "act", "bT"), ("kT", 7, "act", "kT"),
                ("mab0", 2, "dve", "x0_1"), ("mab1", 3, "dve", "x1_1"),
                ("mrb0", 4, "dve", "mrb0"), ("mrb1", 5, "dve", "mrb1"),
                ("mk00", 6, "dve", "mk00"), ("mk01", 7, "dve", "mk01"),
                ("t0_1", 2, "dve", "xT0_1"), ("t1_1", 3, "dve", "xT1_1"),
                ("mk10", 6, "dve", "mk10"), ("mk11", 7, "dve", "mk11")]
        for n in range(2, LEVELS + 1):
            uses += [(f"t0_{n}", 2, "act", f"t0_{n}"), (f"t1_{n}", 3, "act", f"t1_{n}")]
            for e in (0, 1):
                uses += [(f"ut{e}_{n}", 4 + e, "dve", f"xT{e}_{n}")]
                if n < LEVELS:
                    uses += [(f"u{e}_{n}", 6 + e, "dve", f"x{e}_{n}")]
        uses += [("rhs0", 2, "act", "rhs0"), ("rhs1", 3, "dve", "rhs1"), ("sa0", 4, "act", "sa0"),
                 ("sa1", 5, "dve", "sa1"), ("y0", 6, "act", "y0"), ("y1", 7, "act", "y1"), ("st", 2, "dve", "st1"),
                 ("mean", 3, "dve", "yc"), ("var", 4, "dve", "var")]
        pe = Steps(sem("r_pe_steps"), [u[0] for u in uses])
        lora = Steps(sem("r_lora_steps"), ["th", "sg"])
        act = Steps(sem("r_act_steps"), ["ld", "a", "g", "nrm", "e1", "e2", "emid", "vT", "bT", "kT"]
                    + [f"t{e}_{n}" for n in range(2, LEVELS + 1) for e in (0, 1)]
                    + ["rhs0", "sa0", "y0", "y1", "std"])
        dve = Steps(sem("r_dve_steps"), [
            "kkr", "sq", "scan", "mid", "nmid", "nmax", "rn", "kk", "beta",
            "ka1", "ka2", "kf", "A", "R", "B", "K", "rk1", "rk2", "sbar", "bv"]
            + ["mab0", "x0_1", "mab1", "x1_1", "mrb0", "mrb1", "mk00", "mk01", "xT0_1", "xT1_1", "mk10", "mk11"]
            + [f"{k}{e}_{n}" for n in range(2, LEVELS + 1) for e in (0, 1) for k in ("xT", "x")
               if not (k == "x" and n == LEVELS)]
            + ["rhs1", "sa1", "st1", "st2", "yc", "ysq", "var", "rstd", "y1", "y2", "y3", "y4", "out"])
        pool = Steps(sem("r_pool_steps"), ["X", "XT"])
        mix = Steps(sem("r_mix_steps"), ["head", "last", "diff", "mix", "xs"])
        ppe = Steps(sem("r_proj_pe_steps"), ["xT0", "xT1", "r", "k", "v", "l"])
        pact = Steps(sem("r_proj_act_steps"), ["xT0", "xT1", "r", "k", "v", "l"])
        engines = {"act": act, "dve": dve}

        def emptied(step, t):
            i = [u[0] for u in uses].index(step)
            b = uses[i][1]
            before = [u for u in uses[:i] if u[1] == b]
            u = before[-1] if before else [u for u in uses if u[1] == b][-1]
            return engines[u[2]].after(u[3], t if before else t - 1)

        def bank_of(step):
            return bank[[u[1] for u in uses if u[0] == step][0]]

        def four(b, n=P):
            return b[:, 0:PAIRS * n].rearrange("p (a t) -> p a t", a=PAIRS)

        def by_channel(ap):
            return ap.rearrange("o (c p) -> p (o c)", p=P)

        def block_at(n):
            return (slice(0, P), slice(0, P)) if n < LEVELS else (slice(0, P // 2), slice(P // 2, P))

        def over(ap, n=P):
            return ap.unsqueeze(2).broadcast_to([P, ap.shape[1], n])

        block = ctx.enter_context(nc.Block())

        @block.sync
        def _(sp):
            begin_stores(sp, out_stored)
            sp.dma_start(x[:, 0, :], io["x_prompt"][0, 0:P, :]).then_inc(x_loaded[0], 16)
            sp.dma_start(x[:, 1, :], io["x_prompt"][0, P:2 * P, :]).then_inc(x_loaded[1], 16)
            with nc.allow_non_contiguous_dma(reason="vectors of parameters, channels in rows"):
                loads = [(w2[0:LORA, :], io["rwkv_w2"][0]), (w2[LORA:P, :], io["rwkv_a2"][0]),
                         (g2[:, :], io["rwkv_g2"][0]), (mu[:, :], by_channel(io["rwkv_mu"]))]
                for n, name in enumerate(("w0", "a0", "k_k", "k_a", "r_k", "lnx_w", "lnx_b")):
                    v = io["rwkv_" + name]
                    v = v.rearrange("o h d -> o (h d)") if name == "r_k" else v
                    loads.append((par[:, n, :], by_channel(v)))
                for dst, src in loads:
                    sp.dma_start(dst, src).then_inc(weights_loaded, 16)
                sp.dma_start(shift_in[:, :], by_channel(io["state_rwkv_shift"][0, 0])).then_inc(stream_loaded, 16)
                sp.dma_start(st_in[:, :, :], io["state_rwkv"][0, 0].rearrange("h v k -> v h k"))\
                  .then_inc(stream_loaded, 16)

            def store(t, slot):
                sp.wait_ge(*dve.after("out", t))
                sp.dma_start(io["ryT"][:, :, bass.ds(t * P, P)].rearrange("a p t -> p a t"), out[:, slot, :, :])\
                  .then_inc(out_stored[slot], 16)

            with sp.Fori(0, NT // 2 - 1) as j:
                for slot in (0, 1):
                    t = 2 * j + slot
                    sp.wait_ge(*ppe.after("xT1", t))
                    sp.dma_start(x[:, slot, :], io["x_prompt"][0, bass.ds((t + 2) * P, P), :])\
                      .then_inc(x_loaded[slot], 16)
                    store(t, slot)
            sp.wait_ge(pad_zeroed, 1)
            sp.dma_start(x[0:NEW, 0, :], io["x_sample"][0]).then_inc(x_loaded[0], 16)
            store(NT - 2, 0)
            with nc.allow_non_contiguous_dma(reason="one frame, channels in rows"):
                sp.wait_ge(*mix.after("last", NT - 1))
                sp.dma_start(by_channel(io["p_shift"]), last[:, :]).then_inc(shift_dma, 16)
                store(NT - 1, 1)
                sp.wait_ge(state_dve, 1)
                sp.dma_start(io["p_rwkv"].rearrange("h v k -> v h k"), io_st[:, :, :]).then_inc(state_dma, 16)
                sp.wait_ge(*pact.after("l", NT))
                sp.dma_start(by_channel(io["s_shift"]), pr[:, :, NEW]).then_inc(shift_dma, 16)
                store(NT, 0)
                sp.wait_ge(state_dve, 3)
                sp.dma_start(io["s_rwkv"].rearrange("h v k -> v h k"), io_st[:, :, :]).then_inc(state_dma, 16)
            sp.wait_ge(shift_dma, 32)
            sp.wait_ge(state_dma, 32)
            sp.wait_ge(out_stored[0], 16 * (NT // 2 + 2))
            sp.wait_ge(out_stored[1], 16 * (NT // 2 + 1))

        @block.gpsimd
        def _(eng):
            pool.begin(eng)
            mix.begin(eng)
            n = 0
            for turned in (0, 1):
                for level in range(LEVELS):
                    s = 1 << level
                    if n:
                        eng.wait_ge(prepared, n)
                    eng.memset(masks_f[:, :], 0.0).then_inc(masks_ready, 1)
                    eng.wait_ge(masks_ready, 5 * n + 1)
                    cols = masks_f[:, :].rearrange("p (b h i) -> p b h i", h=2, i=s)[:, :, turned, :]
                    nb = P // (2 * s)
                    eng.memset(cols, 1.0).then_inc(masks_ready, 1)
                    eng.wait_ge(masks_ready, 5 * n + 2)
                    low = 0 if turned else s
                    eng.affine_select(out=cols, in_=cols, compare_op=ALU.is_ge, fill=0.0, base=-low,
                                      pattern=[[-2 * s, nb], [0, s]], channel_multiplier=1).then_inc(masks_ready, 1)
                    eng.wait_ge(masks_ready, 5 * n + 3)
                    eng.affine_select(out=cols, in_=cols, compare_op=ALU.is_ge, fill=0.0, base=low + s - 1,
                                      pattern=[[2 * s, nb], [0, s]], channel_multiplier=-1).then_inc(masks_ready, 2)
                    n += 1

            def shift(u):
                def step(name, ins):
                    ins.then_inc(*mix.done(name))
                    eng.wait_ge(*mix.after(name, u))

                eng.wait_ge(*pact.after("l", u))
                eng.wait_ge(*mix.after("xs", u - 1))
                hold(eng, pool_held)
                before_first = shift_in if isinstance(u, int) and u == NT else last
                step("head", eng.tensor_copy(pr[:, :, 0:1], before_first[:, :].unsqueeze(2)))
                if isinstance(u, int) and u == NT:
                    eng.wait_ge(shift_dma, 16)
                hold(eng, pool_held)
                step("last", eng.tensor_copy(last[:, :].unsqueeze(2), pr[:, :, P:P + 1]))
                if not (isinstance(u, int) and u == 0):
                    eng.wait_ge(*pe.after("vT", u - 1))
                    eng.wait_ge(*dve.after("bv", u - 1))
                step("diff", eng.tensor_tensor(xs[:, :, :], pr[:, :, 0:P], pr[:, :, 1:P + 1], ALU.subtract))
                step("mix", eng.tensor_tensor(xs[:, :, :], xs[:, :, :], over(mu[:, :]), ALU.mult))
                step("xs", eng.tensor_tensor(xs[:, :, :], xs[:, :, :], pr[:, :, 1:P + 1], ALU.add))

            def tile(t, slot, j):
                eng.wait_ge(*pe.after(f"ut1_{LEVELS}", t - 1))
                hold(eng, pool_held)
                eng.tensor_copy(X[:, :, :, :].rearrange("p e a t -> p (e a) t"),
                                keep["ident"][:, :].unsqueeze(1).broadcast_to([P, HEADS, P]))\
                   .then_inc(*pool.done("X"))
                eng.wait_ge(*pe.after("sa1", t - 1))
                hold(eng, pool_held)
                eng.tensor_copy(XT[:, :, :, :].rearrange("p e a t -> p (e a) t"),
                                keep["ident"][:, :].unsqueeze(1).broadcast_to([P, HEADS, P]))\
                   .then_inc(*pool.done("XT"))

            eng.wait_ge(prepared, MASKS)
            shift(0)
            with eng.Fori(0, NT // 2 - 1) as j:
                for slot in (0, 1):
                    tile(2 * j + slot, slot, j)
                    shift(2 * j + slot + 1)
            tile(NT - 2, 0, NT // 2 - 1)
            eng.wait_ge(*ppe.after("xT1", NT - 2))
            eng.memset(x[:, 0, :], 0.0).then_inc(pad_zeroed, 1)
            shift(NT - 1)
            tile(NT - 1, 1, NT // 2 - 1)
            eng.wait_ge(stream_loaded, 32)
            shift(NT)
            tile(NT, 0, NT // 2)

        @block.tensor
        def _(eng):
            pe.begin(eng)
            ppe.begin(eng)
            eng.wait_ge(keep["constants_ready"], keep["constants"])
            eng.wait_ge(keep["w_rwkv_loaded"], 16)
            ident = keep["ident"][:, :]

            def project_x(u, slot, turn):
                eng.wait_ge(x_loaded[slot], 16 * (turn + 1))
                for half in (0, 1):
                    eng.wait_ge(*pact.after("vl"[half], u - 1))
                    for k in range(4):
                        mm = eng.transpose(bank[half][:, k * P:(k + 1) * P], x[:, slot, half * 4 + k:D:KD], ident)
                    mm.then_inc(*ppe.done(f"xT{half}"))

            def project(u, name):
                n = "rkvl".index(name)
                eng.wait_ge(*pact.after(("xT1", "xT1", "r", "k")[n], u))
                b = four(bank[n % 2])
                for f in range(4 if n < 3 else 2):
                    c = (4 * n + f) * P
                    for k in range(KD):
                        mm = eng.matmul(b[:, f, :], w[:, k, c:c + P], xT[:, k, :], start=(k == 0), stop=(k == KD - 1))
                mm.then_inc(*ppe.done(name))

            def half_of(e):
                return slice(e * DH, (e + 1) * DH)

            def tile(t, slot, j, following=True):
                def start(step):
                    eng.wait_ge(*emptied(step, t))
                    return bank_of(step)

                if following:
                    project_x(t + 1, 1 - slot, j + slot)
                b = four(start("zw"))
                eng.wait_ge(*lora.after("th", t))
                for p in range(PAIRS):
                    mm = eng.matmul(b[:, p, :], w2[0:LORA, p * P:(p + 1) * P], th[:, :], start=True, stop=True)
                mm.then_inc(*pe.done("zw"))
                b = four(start("za"))
                for p in range(PAIRS):
                    mm = eng.matmul(b[:, p, :], w2[LORA:P, p * P:(p + 1) * P], xs[LORA:P, 12, :], start=True, stop=True)
                mm.then_inc(*pe.done("za"))
                b = four(start("zg"))
                eng.wait_ge(*lora.after("sg", t))
                for p in range(PAIRS):
                    mm = eng.matmul(b[:, p, :], g2[:, p * P:(p + 1) * P], sg[:, :], start=True, stop=True)
                mm.then_inc(*pe.done("zg"))
                if following:
                    project(t + 1, "r")
                if not following:
                    eng.wait_ge(state_dve, 2)
                b = start("ss")
                eng.wait_ge(*dve.after("sq", t))
                eng.matmul(b[:, :], keep["halves"][:, :], sq[:, :, :].rearrange("p a t -> p (a t)"), start=True, stop=True)\
                   .then_inc(*pe.done("ss"))
                if following:
                    project(t + 1, "k")
                    project(t + 1, "v")
                b = start("vT")
                for p in range(PAIRS):
                    mm = eng.transpose(b[:, p * P:(p + 1) * P], xs[:, 8 + p, :], ident)
                mm.then_inc(*pe.done("vT"))
                if following:
                    project(t + 1, "l")
                b = start("bs")
                eng.wait_ge(*dve.after("rk2", t))
                eng.matmul(b[:, :], keep["halves"][:, :], sq[:, :, :].rearrange("p a t -> p (a t)"), start=True, stop=True)\
                   .then_inc(*pe.done("bs"))
                for name, src in (("bT", bt), ("kT", kt)):
                    b = start(name)
                    for p in range(PAIRS):
                        mm = eng.transpose(b[:, p * P:(p + 1) * P], src[:, p, :], ident)
                    mm.then_inc(*pe.done(name))
                for e in (0, 1):
                    h = half_of(e)
                    b = four(start(f"mab{e}"))
                    for p in range(PAIRS):
                        mm = eng.matmul(b[:, p, :], ar[h, p, 0, :], bt[h, p, :], start=True, stop=True)
                    mm.then_inc(*pe.done(f"mab{e}"))
                for e in (0, 1):
                    h = half_of(e)
                    b = four(start(f"mrb{e}"))
                    for p in range(PAIRS):
                        mm = eng.matmul(b[:, p, :], bt[h, p, :], ar[h, p, 1, :], start=True, stop=True)
                    mm.then_inc(*pe.done(f"mrb{e}"))

                def mk_products(e):
                    h = half_of(e)
                    for n in (0, 1):
                        b = start(f"mk{e}{n}")
                        for i in (0, 1):
                            p = 2 * n + i
                            mm = eng.matmul(b[:, i * 2 * P:(i + 1) * 2 * P], kt[h, p, :],
                                            ar[h, p, :, :].rearrange("p a t -> p (a t)"), start=True, stop=True)
                        mm.then_inc(*pe.done(f"mk{e}{n}"))

                mk_products(0)
                for e in (0, 1):
                    b = four(start(f"t{e}_1"))
                    eng.wait_ge(*dve.after(f"mab{e}", t))
                    for p in range(PAIRS):
                        mm = eng.matmul(b[:, p, :], mab[:, e, p, :], ident, start=True, stop=True)
                    mm.then_inc(*pe.done(f"t{e}_1"))
                mk_products(1)
                for n in range(2, LEVELS + 1):
                    rows, cols = block_at(n)
                    for e in (0, 1):
                        b = four(start(f"t{e}_{n}"))
                        eng.wait_ge(*dve.after(f"xT{e}_{n - 1}", t))
                        for p in range(PAIRS):
                            mm = eng.matmul(b[rows, p, cols], mab[:, e, p, rows], XT[:, e, p, cols], start=True, stop=True)
                        mm.then_inc(*pe.done(f"t{e}_{n}"))
                    for e in (0, 1):
                        b = four(start(f"ut{e}_{n}"))
                        eng.wait_ge(*dve.after(f"x{e}_{n - 1}", t))
                        eng.wait_ge(*act.after(f"t{e}_{n}", t))
                        for p in range(PAIRS):
                            mm = eng.matmul(b[rows, p, cols], X[:, e, p, rows], t1[:, e, p, cols], start=True, stop=True)
                        mm.then_inc(*pe.done(f"ut{e}_{n}"))
                        if n < LEVELS:
                            b = four(start(f"u{e}_{n}"))
                            for p in range(PAIRS):
                                mm = eng.matmul(b[:, p, :], t1[:, e, p, :], X[:, e, p, :], start=True, stop=True)
                            mm.then_inc(*pe.done(f"u{e}_{n}"))
                for e in (0, 1):
                    h = half_of(e)
                    b = four(start(f"rhs{e}"), DH)
                    eng.wait_ge(*dve.after("sbar", t))
                    for p in range(PAIRS):
                        eng.matmul(b[:, p, :], ar[h, p, 0, :], sbar[h, p, :], start=True, stop=False)
                        mm = eng.matmul(b[:, p, :], mk[:, e, p, 0, :], vtok[:, p, h], start=False, stop=True)
                    mm.then_inc(*pe.done(f"rhs{e}"))
                for e in (0, 1):
                    b = four(start(f"sa{e}"), DH)
                    eng.wait_ge(*(act, dve)[e].after(f"rhs{e}", t))
                    eng.wait_ge(*dve.after(f"xT{e}_{LEVELS}", t))
                    for p in range(PAIRS):
                        mm = eng.matmul(b[:, p, :], XT[:, e, p, :], rhs[:, e, p, :], start=True, stop=True)
                    mm.then_inc(*pe.done(f"sa{e}"))
                b = []
                for e in (0, 1):
                    b.append(four(start(f"y{e}")))
                    eng.wait_ge(*(act, dve)[e].after(f"sa{e}", t))
                both = [(e, half_of(e)) for e in (0, 1)]
                for p in range(PAIRS):
                    for e, h in both:
                        eng.matmul(b[e][h, p, :], sa[:, e, p, :], mrb[:, e, p, :], start=True, stop=False)
                    for e, h in both:
                        eng.matmul(b[e][h, p, :], sbar[h, p, :], ar[h, p, 1, :], start=False, stop=False)
                    for e, h in both:
                        mm = eng.matmul(b[e][h, p, :], vtok[:, p, h], mk[:, e, p, 1, :], start=False, stop=True)
                        if p == PAIRS - 1:
                            mm.then_inc(*pe.done(f"y{e}"))
                b = four(start("st"), DH)
                for p in range(PAIRS):
                    for e, h in both:
                        eng.matmul(b[h, p, :], btok[:, p, h], sa[:, e, p, :], start=True, stop=False)
                    for e, h in both:
                        mm = eng.matmul(b[h, p, :], ktok[:, p, h], vtok[:, p, h], start=False, stop=True)
                mm.then_inc(*pe.done("st"))
                b = start("mean")
                eng.wait_ge(*act.after("y1", t))
                eng.matmul(b[:, :], keep["halves"][:, :], y[:, :, :].rearrange("p a t -> p (a t)"), start=True, stop=True)\
                   .then_inc(*pe.done("mean"))
                b = start("var")
                eng.wait_ge(*dve.after("ysq", t))
                eng.matmul(b[:, :], keep["halves"][:, :], ysq[:, :, :].rearrange("p a t -> p (a t)"), start=True, stop=True)\
                   .then_inc(*pe.done("var"))

            project_x(0, 0, 0)
            for name in "rkvl":
                project(0, name)
            eng.wait_ge(weights_loaded, 16 * 11)
            eng.wait_ge(prepared, MASKS)
            with eng.Fori(0, NT // 2) as j:
                for slot in (0, 1):
                    tile(2 * j + slot, slot, j)

            def state_out():
                for p in range(PAIRS):
                    mm = eng.transpose(bank[5][0:DH, p * P:(p + 1) * P], st[:, p, :], ident)
                mm.then_inc(state_pe, 1)

            eng.wait_ge(*dve.after("st2", NT - 1))
            state_out()
            eng.wait_ge(stream_loaded, 32)
            for p in range(PAIRS):
                mm = eng.transpose(bank[6][:, p * DH:(p + 1) * DH],
                                   st_in[:, 2 * p:2 * p + 2, :].rearrange("v h k -> v (h k)"), ident[0:DH, 0:DH])
            mm.then_inc(state_pe, 1)
            tile(NT, 0, NT // 2, following=False)
            eng.wait_ge(*dve.after("st2", NT))
            state_out()

        @block.scalar
        def _(eng):
            act.begin(eng)
            lora.begin(eng)
            pact.begin(eng)

            def project_x(u):
                for half in (0, 1):
                    eng.wait_ge(*ppe.after(f"xT{half}", u))
                    eng.copy(xT[:, half * 4:half * 4 + 4, :], four(bank[half])).then_inc(*pact.done(f"xT{half}"))

            def project(u, name):
                n = "rkvl".index(name)
                eng.wait_ge(*ppe.after(name, u))
                eng.wait_ge(*mix.after("xs", u - 1))
                m = 4 if n < 3 else 2
                eng.copy(pr[:, 4 * n:4 * n + m, 1:P + 1], four(bank[n % 2])[:, 0:m, :]).then_inc(*pact.done(name))

            def lora_inputs(u):
                eng.wait_ge(*mix.after("xs", u))
                if not (isinstance(u, int) and u == 0):
                    eng.wait_ge(*pe.after("zg", u - 1))
                eng.activation(th[:, :], xs[0:LORA, 12, :], ACT.Tanh).then_inc(*lora.done("th"))
                eng.activation(sg[:, :], xs[:, 13, :], ACT.Sigmoid).then_inc(*lora.done("sg"))

            def tile(t, slot, j, following=True):
                if following:
                    project_x(t + 1)
                for name, dst, n, readers in (("ld", ld, 0, "scan"), ("a", a, 1, "ka1")):
                    eng.wait_ge(*pe.after({"ld": "zw", "a": "za"}[name], t))
                    eng.wait_ge(*dve.after(readers, t - 1))
                    for p in range(PAIRS):
                        ins = eng.activation(dst[:, p, :], four(bank_of({"ld": "zw", "a": "za"}[name]))[:, p, :],
                                             ACT.Sigmoid, bias=par[:, n, p:p + 1])
                    ins.then_inc(*act.done(name))
                eng.wait_ge(*pe.after("zg", t))
                eng.wait_ge(*dve.after("out", t - 1))
                eng.copy(g[:, :, :], four(bank_of("zg"))).then_inc(*act.done("g"))
                if following:
                    project(t + 1, "r")
                eng.wait_ge(*pe.after("ss", t))
                eng.wait_ge(*dve.after("rn", t - 1))
                eng.activation(nrm[:, :, :], four(bank_of("ss")), ACT.Sqrt).then_inc(*act.done("nrm"))
                if following:
                    project(t + 1, "k")
                eng.wait_ge(*dve.after("nmid", t))
                eng.wait_ge(*dve.after("st2", t - 1))
                for p in range(PAIRS):
                    ins = eng.activation(e1[:, p, :], cum[:, p, :], ACT.Exp, scale=-DECAY, bias=cm[:, 0, p:p + 1])
                ins.then_inc(*act.done("e1"))
                for p in range(PAIRS):
                    ins = eng.activation(e2[:, p, :], cum[:, p, 1:P + 1], ACT.Exp, scale=DECAY, bias=cm[:, 1, p:p + 1])
                ins.then_inc(*act.done("e2"))
                eng.activation(cm[:, 2, :], cm[:, 1, :], ACT.Exp).then_inc(*act.done("emid"))
                if following:
                    project(t + 1, "v")
                eng.wait_ge(*pe.after("vT", t))
                eng.wait_ge(*pe.after("st", t - 1))
                eng.copy(vtok[:, :, :], four(bank_of("vT"))).then_inc(*act.done("vT"))
                if following:
                    project(t + 1, "l")
                for name, dst in (("bT", btok), ("kT", ktok)):
                    eng.wait_ge(*pe.after(name, t))
                    eng.copy(dst[:, :, :], four(bank_of(name))).then_inc(*act.done(name))
                for n in range(2, LEVELS + 1):
                    for e in (0, 1):
                        eng.wait_ge(*pe.after(f"t{e}_{n}", t))
                        eng.wait_ge(*pe.after(f"u{e}_{n - 1}", t) if n > 2 else pe.after(f"ut{e}_{LEVELS}", t - 1))
                        rows, cols = block_at(n)
                        eng.copy(t1[rows, e, :, cols], four(bank_of(f"t{e}_{n}"))[rows, :, cols]).then_inc(*act.done(f"t{e}_{n}"))
                if following:
                    lora_inputs(t + 1)
                eng.wait_ge(*pe.after("rhs0", t))
                eng.copy(rhs[:, 0, :, :], four(bank_of("rhs0"), DH)).then_inc(*act.done("rhs0"))
                eng.wait_ge(*pe.after("sa0", t))
                eng.copy(sa[:, 0, :, :], four(bank_of("sa0"), DH)).then_inc(*act.done("sa0"))
                for e in (0, 1):
                    h = slice(e * DH, (e + 1) * DH)
                    eng.wait_ge(*pe.after(f"y{e}", t))
                    eng.wait_ge(*dve.after("yc", t - 1))
                    eng.copy(y[h, :, :], four(bank_of(f"y{e}"))[h, :, :]).then_inc(*act.done(f"y{e}"))
                eng.wait_ge(*dve.after("var", t))
                eng.activation(ysq[:, :, :], ys[:, :, :], ACT.Sqrt).then_inc(*act.done("std"))

            project_x(0)
            for name in "rkvl":
                project(0, name)
            lora_inputs(0)
            with eng.Fori(0, NT // 2) as j:
                for slot in (0, 1):
                    tile(2 * j + slot, slot, j)
            tile(NT, 0, NT // 2, following=False)

        @block.vector
        def _(eng):
            n = 0
            for turned in (0, 1):
                for level in range(LEVELS):
                    eng.wait_ge(masks_ready, 5 * (n + 1))
                    eng.tensor_copy(mask[:, turned, level, :], masks_f[:, :]).then_inc(prepared, 1)
                    n += 1
            eng.wait_ge(keep["constants_ready"], keep["constants"])
            eng.tensor_copy(mask2[:, 0, :], keep["before"][:, :])
            eng.tensor_copy(mask2[:, 1, :], keep["upto"][:, :])
            eng.memset(cum[:, :, 0:1], 0.0)
            eng.memset(last[:, :], 0.0)
            eng.memset(st[:, :, :], 0.0)
            eng.wait_ge(weights_loaded, 16 * 11)
            eng.tensor_scalar(one_ka[:, :], par[:, 3, :], -1.0, 1.0, ALU.mult, ALU.add).then_inc(prepared, 2)
            eng.wait_ge(prepared, MASKS)
            dve.begin(eng)

            def chained(*step_t):
                eng.wait_ge(*dve.after(*step_t))

            def tt(name, out_, a_, b_, op, t):
                eng.tensor_tensor(out_, a_, b_, op).then_inc(*dve.done(name))

            def heads4(ap):
                return ap.unsqueeze(1).broadcast_to([P, PAIRS, P])

            def tile(t, slot, j, final=False):
                eng.wait_ge(*mix.after("xs", t))
                xr, xk, xv = xs[:, 0:4, :], xs[:, 4:8, :], xs[:, 8:12, :]
                eng.wait_ge(*pe.after("bs", t - 1))
                tt("kkr", kk[:, :, :], xk, over(par[:, 2, :]), ALU.mult, t)
                chained("kkr", t)
                tt("sq", sq[:, :, :], kk[:, :, :], kk[:, :, :], ALU.mult, t)
                eng.wait_ge(*act.after("ld", t))
                if final:
                    eng.memset(ld[:, :, NEW:P], 0.0).then_inc(cleared, 1)
                    eng.wait_ge(cleared, 1)
                for p in range(PAIRS):
                    ins = eng.tensor_tensor_scan(out=cum[:, p, 1:P + 1], data0=keep["ones"][:, :], data1=ld[:, p, :],
                                                 initial=0.0, op0=ALU.mult, op1=ALU.add)
                ins.then_inc(*dve.done("scan"))
                chained("scan", t)
                eng.tensor_scalar(cm[:, 0, :], cum[:, :, DH], DECAY, None, ALU.mult).then_inc(*dve.done("mid"))
                eng.tensor_scalar(cm[:, 1, :], cum[:, :, DH], -DECAY, None, ALU.mult).then_inc(*dve.done("nmid"))
                eng.wait_ge(*act.after("nrm", t))
                eng.tensor_scalar(nrm[:, :, :], nrm[:, :, :], 1e-12, None, ALU.max).then_inc(*dve.done("nmax"))
                chained("nmax", t)
                eng.reciprocal(nrm[:, :, :], nrm[:, :, :]).then_inc(*dve.done("rn"))
                chained("rn", t)
                tt("kk", kk[:, :, :], kk[:, :, :], nrm[:, :, :], ALU.mult, t)
                chained("kk", t)
                eng.wait_ge(*act.after("a", t))
                tt("beta", beta[:, :, :], kk[:, :, :], a[:, :, :], ALU.mult, t)
                chained("beta", t)
                tt("ka1", kf[:, :, :], a[:, :, :], over(par[:, 3, :]), ALU.mult, t)
                chained("ka1", t)
                tt("ka2", kf[:, :, :], kf[:, :, :], over(one_ka[:, :]), ALU.add, t)
                chained("ka2", t)
                tt("kf", kf[:, :, :], kf[:, :, :], xk, ALU.mult, t)
                chained("kf", t)
                if final:
                    eng.memset(kf[:, :, NEW:P], 0.0).then_inc(cleared, 1)
                    eng.memset(beta[:, :, NEW:P], 0.0).then_inc(cleared, 1)
                    eng.wait_ge(cleared, 3)
                eng.wait_ge(*act.after("emid", t))
                eng.wait_ge(*pe.after("y1", t - 1))
                eng.scalar_tensor_tensor(out=ar[:, :, 0, :], in0=kk[:, :, :], scalar=-1.0, in1=e1[:, :, 0:P],
                                         op0=ALU.mult, op1=ALU.mult).then_inc(*dve.done("A"))
                tt("R", ar[:, :, 1, :], xr, e1[:, :, 1:P + 1], ALU.mult, t)
                tt("B", bt[:, :, :], beta[:, :, :], e2[:, :, :], ALU.mult, t)
                tt("K", kt[:, :, :], kf[:, :, :], e2[:, :, :], ALU.mult, t)
                eng.wait_ge(*pe.after("ss", t))
                tt("rk1", sq[:, :, :], xr, kf[:, :, :], ALU.mult, t)
                chained("rk1", t)
                tt("rk2", sq[:, :, :], sq[:, :, :], over(par[:, 4, :]), ALU.mult, t)
                if final:
                    eng.wait_ge(state_dve, 2)
                chained("st2", t - 1)
                tt("sbar", sbar[:, :, :], st[:, :, :], over(cm[:, 2, :], DH), ALU.mult, t)
                chained("out", t - 1)
                eng.wait_ge(*pe.after("bs", t))
                tt("bv", bv[:, :, :], four(bank_of("bs")), xv, ALU.mult, t)
                for e in (0, 1):
                    eng.wait_ge(*pe.after(f"mab{e}", t))
                    b = four(bank_of(f"mab{e}"))
                    eng.wait_ge(*pe.after(f"t{e}_{LEVELS}", t - 1))
                    tt(f"mab{e}", mab[:, e, :, :], b, heads4(keep["after"][:, :]), ALU.mult, t)
                    eng.wait_ge(*pool.after("X", t))
                    hold(eng, held)
                    eng.copy_predicated(X[:, e, :, :], heads4(mask[:, 0, 0, :]), b).then_inc(*dve.done(f"x{e}_1"))
                for e in (0, 1):
                    eng.wait_ge(*pe.after(f"mrb{e}", t))
                    tt(f"mrb{e}", mrb[:, e, :, :], four(bank_of(f"mrb{e}")), heads4(keep["upto"][:, :]), ALU.mult, t)

                def mk_masked(e):
                    for n in (0, 1):
                        eng.wait_ge(*pe.after(f"mk{e}{n}", t))
                        tt(f"mk{e}{n}", mk[:, e, 2 * n:2 * n + 2, :, :].rearrange("p a b t -> p a (b t)"),
                           bank_of(f"mk{e}{n}")[:, :].rearrange("p (a x) -> p a x", a=2),
                           mask2[:, :, :].rearrange("p b t -> p (b t)").unsqueeze(1).broadcast_to([P, 2, 2 * P]),
                           ALU.mult, t)

                mk_masked(0)
                eng.wait_ge(*pool.after("XT", t))
                for e in (0, 1):
                    eng.wait_ge(*pe.after(f"t{e}_1", t))
                    hold(eng, held)
                    eng.copy_predicated(XT[:, e, :, :], heads4(mask[:, 1, 0, :]), four(bank_of(f"t{e}_1")))\
                       .then_inc(*dve.done(f"xT{e}_1"))
                mk_masked(1)
                for n in range(2, LEVELS + 1):
                    for e in (0, 1):
                        eng.wait_ge(*pe.after(f"ut{e}_{n}", t))
                        hold(eng, held)
                        if n < LEVELS:
                            ins = eng.copy_predicated(XT[:, e, :, :], heads4(mask[:, 1, n - 1, :]),
                                                      four(bank_of(f"ut{e}_{n}")))
                        else:
                            rows, cols = block_at(n)
                            ins = eng.tensor_copy(XT[rows, e, :, cols], four(bank_of(f"ut{e}_{n}"))[rows, :, cols])
                        ins.then_inc(*dve.done(f"xT{e}_{n}"))
                        if n < LEVELS:
                            eng.wait_ge(*pe.after(f"u{e}_{n}", t))
                            hold(eng, held)
                            eng.copy_predicated(X[:, e, :, :], heads4(mask[:, 0, n - 1, :]),
                                                four(bank_of(f"u{e}_{n}"))).then_inc(*dve.done(f"x{e}_{n}"))
                eng.wait_ge(*pe.after("rhs1", t))
                eng.tensor_copy(rhs[:, 1, :, :], four(bank_of("rhs1"), DH)).then_inc(*dve.done("rhs1"))
                eng.wait_ge(*pe.after("sa1", t))
                eng.tensor_copy(sa[:, 1, :, :], four(bank_of("sa1"), DH)).then_inc(*dve.done("sa1"))
                eng.wait_ge(*pe.after("st", t))
                tt("st1", st[:, :, :], four(bank_of("st"), DH), sbar[:, :, :], ALU.add, t)
                chained("st1", t)
                tt("st2", st[:, :, :], st[:, :, :], e1[:, :, P:P + 1].broadcast_to([P, PAIRS, DH]), ALU.mult, t)
                eng.wait_ge(*pe.after("mean", t))
                eng.scalar_tensor_tensor(out=y[:, :, :], in0=four(bank_of("mean")), scalar=-1.0 / DH, in1=y[:, :, :],
                                         op0=ALU.mult, op1=ALU.add).then_inc(*dve.done("yc"))
                chained("yc", t)
                tt("ysq", ysq[:, :, :], y[:, :, :], y[:, :, :], ALU.mult, t)
                eng.wait_ge(*pe.after("var", t))
                eng.tensor_scalar(ys[:, :, :], four(bank_of("var")), 1.0 / DH, GN_EPS, ALU.mult, ALU.add)\
                   .then_inc(*dve.done("var"))
                eng.wait_ge(*act.after("std", t))
                eng.reciprocal(ys[:, :, :], ysq[:, :, :]).then_inc(*dve.done("rstd"))
                chained("rstd", t)
                tt("y1", ys[:, :, :], ys[:, :, :], y[:, :, :], ALU.mult, t)
                chained("y1", t)
                tt("y2", ys[:, :, :], ys[:, :, :], over(par[:, 5, :]), ALU.mult, t)
                chained("y2", t)
                tt("y3", ys[:, :, :], ys[:, :, :], over(par[:, 6, :]), ALU.add, t)
                chained("y3", t)
                tt("y4", ys[:, :, :], ys[:, :, :], bv[:, :, :], ALU.add, t)
                chained("y4", t)
                eng.wait_ge(*act.after("g", t))
                eng.wait_ge(out_stored[slot], 16 * (j + 1))
                tt("out", out[:, slot, :, :], ys[:, :, :], g[:, :, :], ALU.mult, t)

            with eng.Fori(0, NT // 2) as j:
                for slot in (0, 1):
                    tile(2 * j + slot, slot, j)
            eng.wait_ge(state_pe, 1)
            eng.tensor_copy(io_st[:, :, :], bank[5][0:DH, :].rearrange("v (h k) -> v h k", h=HEADS))\
               .then_inc(state_dve, 1)
            eng.wait_ge(state_pe, 2)
            eng.tensor_copy(st[:, :, :], bank[6][:, 0:PAIRS * DH].rearrange("p (a v) -> p a v", a=PAIRS))\
               .then_inc(state_dve, 1)
            tile(NT, 0, NT // 2, final=True)
            eng.wait_ge(state_pe, 3)
            eng.wait_ge(state_dma, 16)
            eng.tensor_copy(io_st[:, :, :], bank[5][0:DH, :].rearrange("v (h k) -> v h k", h=HEADS))\
               .then_inc(state_dve, 1)
def fox_prompt(nc, io, keep):
    with ExitStack() as ctx:
        def sb(name, shape, dt=F32):
            return ctx.enter_context(nc.sbuf_tensor(name, shape, dt))

        def sem(name):
            return ctx.enter_context(nc.semaphore(name))

        logits = ctx.enter_context(nc.psum_tensor("a_logits", [P, SEQ], F32))
        turned = [ctx.enter_context(nc.psum_tensor(f"a_turned{b}", [P, 512], F32)) for b in range(2)]
        oT = ctx.enter_context(nc.psum_tensor("a_oT", [P, 512], F32))
        o = ctx.enter_context(nc.psum_tensor("a_o", [P, 512], F32))
        q = sb("a_q", [DH + 1, 2, SEQ])
        k = sb("a_k", [DH + 1, 2, SEQ])
        v = sb("a_v", [P, 2, NT, DH])
        halves_sb = sb("a_halves", [P, 2, P])
        two_idents = sb("a_two_idents", [P, DH])
        pr = sb("a_p", [P, 2, SEQ])
        pT = sb("a_pT", [P, 2, SEQ])
        nmax = sb("a_nmax", [P, 2])
        total = sb("a_total", [P, 2])
        inv = sb("a_inv", [P, 2])
        fy = keep["fy"]

        idents_stacked = sem("a_idents_stacked")
        v_loaded = [sem(f"a_v_loaded{s}") for s in (0, 1)]
        qk_loaded = [sem(f"a_qk_loaded{s}") for s in (0, 1)]
        ones_set = sem("a_ones_set")
        quads = [-(-(t + 1) // 4) for t in range(NT)]
        all_quads = [(t, c) for t in range(NT) for c in range(quads[t])]
        owner = {(t, c): 2 * c < quads[t] for t, c in all_quads}
        half = SEQ // 2
        first_col = [half * (t % 2) if (t + 1) * P <= half else 0 for t in range(NT)]

        def tensor_steps():
            done = set()
            for t in range(NT + 1):
                if t < NT and t not in done:
                    yield "s", t, 0
                if t > 0:
                    for c in range(quads[t - 1]):
                        yield "T", t - 1, c
                        if c == 0 and t > 1:
                            yield "f", t - 2, 0
                        if c == quads[t - 1] - 1 and (t + 2) * P <= half:
                            done.add(t + 1)
                            yield "s", t + 1, 0
                        if c > 0:
                            yield "o", t - 1, c - 1
                    yield "o", t - 1, quads[t - 1] - 1
            yield "f", NT - 1, 0

        pe_names = [{"s": f"s{t}", "T": f"T{t}_{c}", "o": f"o{t}", "f": f"f{t}"}[kind] for kind, t, c in tensor_steps()
                    if kind != "o" or c == quads[t] - 1]
        dve_names, act_names = [], []
        for t in range(NT + 1):
            if t < NT:
                dve_names.append(f"max{t}")
            if t > 1:
                dve_names.append(f"f{t - 2}")
            if t > 0:
                for c in range(quads[t - 1]):
                    (act_names if owner[t - 1, c] else dve_names).append(f"T{t - 1}_{c}")
                dve_names += [f"inv{t - 1}", f"oT{t - 1}"]
            if t < NT:
                act_names.append(f"exp{t}")
        dve_names.append(f"f{NT - 1}")
        pe = Steps(sem("a_pe_steps"), pe_names, ahead=2)
        act = Steps(sem("a_act_steps"), act_names)
        dve = Steps(sem("a_dve_steps"), dve_names)

        def logits_read(t, h):
            if t == 0:
                return act.after(f"exp{NT - 1}", h - 1)
            return act.after(f"exp{t - 2 if (t + 1) * P <= half else t - 1}", h)

        def emptied(n, h):
            if n >= 2:
                t, c = all_quads[n - 2]
                return (act if owner[t, c] else dve).after(f"T{t}_{c}", h)
            t, c = all_quads[n - 2]
            return (act if owner[t, c] else dve).after(f"T{t}_{c}", h - 1)

        block = ctx.enter_context(nc.Block())

        @block.sync
        def _(sp):
            with sp.Fori(0, PAIRS) as j:
                for e in (0, 1):
                    sp.wait_ge(*pe.after(f"s{NT - 1}", 2 * j + e - 2))
                    rows = slice(e * DH, (e + 1) * DH)
                    sp.dma_start(q[0:DH, e, :], io["qT"][bass.ds(j, 1), rows, 0:SEQ].rearrange("a p t -> p (a t)"))\
                      .then_inc(qk_loaded[e], 16)
                    sp.dma_start(k[0:DH, e, :], io["kT"][bass.ds(j, 1), rows, 0:SEQ].rearrange("a p t -> p (a t)"))\
                      .then_inc(qk_loaded[e], 16)
                    sp.dma_start(k[DH:DH + 1, e, :], io["cT"][bass.ds(2 * j + e, 1), 0:SEQ]).then_inc(qk_loaded[e], 16)
                    sp.wait_ge(*pe.after(f"o{NT - 1}", 2 * j + e - 2))
                    sp.dma_start(v[:, e, :, :], io["p_v"].rearrange("(n p) c -> p n c", p=P)
                                 [:, :, bass.ds(j * P + e * DH, DH)]).then_inc(v_loaded[e], 16)
            sp.dma_start(keep["w_out"][:, :, :], io["w_out"][0].rearrange("(c p) n -> p c n", p=P))\
              .then_inc(keep["w_out_loaded"], 16)

        @block.gpsimd
        def _(eng):
            eng.memset(q[DH:DH + 1, :, :], 1.0).then_inc(ones_set, 1)

        @block.tensor
        def _(eng):
            pe.begin(eng)
            eng.wait_ge(ones_set, 1)
            eng.wait_ge(idents_stacked, 1)

            def head(h, e, j):
                eng.wait_ge(qk_loaded[e], 48 * (j + 1))

                def scores(t):
                    if t != 1:
                        eng.wait_ge(*logits_read(t, h))
                    n, at = (t + 1) * P, first_col[t]
                    for a in range(0, n, 512):
                        m = min(512, n - a)
                        last = a + m == n
                        mm = eng.matmul(logits[:, at + a:at + a + m], q[:, e, t * P:(t + 1) * P], k[:, e, a:a + m],
                                        start=True, stop=not last)
                    eng.matmul(logits[:, at + n - P:at + n], keep["ident"][:, :], keep["causal"][:, :], start=False, stop=True)\
                       .then_inc(*pe.done(f"s{t}"))

                def turn(t, c):
                    if c == 0:
                        eng.wait_ge(*act.after(f"exp{t}", h))
                    n = all_quads.index((t, c))
                    eng.wait_ge(*emptied(n, h))
                    for i in range(min(4, t + 1 - 4 * c)):
                        mm = eng.transpose(turned[n % 2][:, i * P:(i + 1) * P],
                                           pr[:, t % 2, (4 * c + i) * P:(4 * c + i + 1) * P], keep["ident"][:, :])
                    mm.then_inc(*pe.done(f"T{t}_{c}"))

                def attend(t, c):
                    if c == 0:
                        eng.wait_ge(*(dve.after(f"oT{t - 1}", h) if t else dve.after(f"oT{NT - 1}", h - 1)))
                        if t == 0:
                            eng.wait_ge(v_loaded[e], 16 * (j + 1))
                    eng.wait_ge(*(act if owner[t, c] else dve).after(f"T{t}_{c}", h))
                    for i in range(4 * c, min(4 * c + 4, t + 1)):
                        side = slice(i % 2 * DH, (i % 2 + 1) * DH)
                        mm = eng.matmul(oT[side, 0:P], v[:, e, i, :], pT[:, t % 2, i * P:(i + 1) * P],
                                        start=(i < 2), stop=(i >= t - 1))
                    if c == quads[t] - 1:
                        mm.then_inc(*pe.done(f"o{t}"))

                def turn_back(t):
                    eng.wait_ge(*dve.after(f"oT{t}", h))
                    eng.wait_ge(*(dve.after(f"f{t - 1}", h) if t else dve.after(f"f{NT - 1}", h - 1)))
                    rows = P if t else DH
                    eng.matmul(o[:, 0:DH], halves_sb[0:rows, t % 2, :], two_idents[0:rows, :], start=True, stop=True)\
                       .then_inc(*pe.done(f"f{t}"))

                for kind, t, c in tensor_steps():
                    if kind == "f":
                        turn_back(t)
                    elif kind == "s":
                        scores(t)
                    elif kind == "T":
                        turn(t, c)
                    else:
                        attend(t, c)

            with eng.Fori(0, PAIRS) as j:
                for e in (0, 1):
                    head(2 * j + e, e, j)

        def empty_quad(eng, copy, t, c, h):
            n = min(4, t + 1 - 4 * c) * P
            eng.wait_ge(*pe.after(f"T{t}_{c}", h))
            eng.wait_ge(*(pe.after(f"o{t - 2}", h) if t > 1 else pe.after(f"o{NT - 2 + t}", h - 1)))
            return copy(pT[:, t % 2, 4 * c * P:4 * c * P + n], turned[all_quads.index((t, c)) % 2][:, 0:n])

        @block.scalar
        def _(eng):
            act.begin(eng)

            def head(h, e, j):
                for t in range(NT + 1):
                    if t > 0:
                        for c in range(quads[t - 1]):
                            if owner[t - 1, c]:
                                empty_quad(eng, eng.copy, t - 1, c, h).then_inc(*act.done(f"T{t - 1}_{c}"))
                    if t < NT:
                        n = (t + 1) * P
                        eng.wait_ge(*dve.after(f"max{t}", h))
                        prev = (t - 2, h) if t > 1 else (NT - 2 + t, h - 1)
                        eng.wait_ge(*pe.after(f"o{prev[0]}", prev[1]))
                        eng.wait_ge(*dve.after(f"inv{prev[0]}", prev[1]))
                        eng.activation(pr[:, t % 2, 0:n], logits[:, first_col[t]:first_col[t] + n], ACT.Exp, bias=nmax[:, t % 2:t % 2 + 1],
                                       accum_out=total[:, t % 2:t % 2 + 1]).then_inc(*act.done(f"exp{t}"))

            with eng.Fori(0, PAIRS) as j:
                for e in (0, 1):
                    head(2 * j + e, e, j)

        @block.vector
        def _(eng):
            eng.tensor_tensor(two_idents[:, :], keep["ident"][:, 0:DH], keep["ident"][:, DH:P], ALU.add)\
               .then_inc(idents_stacked, 1)
            dve.begin(eng)

            def head(h, e, j):
                def finish(t):
                    eng.wait_ge(*pe.after(f"f{t}", h))
                    eng.wait_ge(*dve.after(f"inv{t}", h))
                    eng.tensor_scalar(fy[:, t, bass.ds(h * DH, DH)], o[:, 0:DH], inv[:, t % 2:t % 2 + 1], None,
                                      ALU.mult).then_inc(*dve.done(f"f{t}"))

                for t in range(NT + 1):
                    if t < NT:
                        n = (t + 1) * P
                        eng.wait_ge(*pe.after(f"s{t}", h))
                        prev = (t - 2, h) if t > 1 else (NT - 2 + t, h - 1)
                        eng.wait_ge(*act.after(f"exp{prev[0]}", prev[1]))
                        eng.tensor_reduce(nmax[:, t % 2:t % 2 + 1], logits[:, first_col[t]:first_col[t] + n], AX_X,
                                          ALU.max, negate=True).then_inc(*dve.done(f"max{t}"))
                    if t > 1:
                        finish(t - 2)
                    if t > 0:
                        u = t - 1
                        for c in range(quads[u]):
                            if not owner[u, c]:
                                empty_quad(eng, eng.tensor_copy, u, c, h).then_inc(*dve.done(f"T{u}_{c}"))
                        eng.wait_ge(*act.after(f"exp{u}", h))
                        eng.reciprocal(inv[:, u % 2:u % 2 + 1], total[:, u % 2:u % 2 + 1])\
                           .then_inc(*dve.done(f"inv{u}"))
                        eng.wait_ge(*pe.after(f"o{u}", h))
                        rows = P if u else DH
                        eng.tensor_copy(halves_sb[0:rows, u % 2, :], oT[0:rows, 0:P]).then_inc(*dve.done(f"oT{u}"))
                finish(NT - 1)

            with eng.Fori(0, PAIRS) as j:
                for e in (0, 1):
                    head(2 * j + e, e, j)


def fox_sample(nc, io, keep):
    CT = PAST // P
    KEYS = PAST + NEW
    HG = HEADS // 2
    with ExitStack() as ctx:
        def sb(name, shape, dt=F32):
            return ctx.enter_context(nc.sbuf_tensor(name, shape, dt))

        def sem(name):
            return ctx.enter_context(nc.semaphore(name))

        bank = [ctx.enter_context(nc.psum_tensor(f"sp{b}", [P, 512], F32)) for b in range(8)]
        q = sb("c_q", [P, PAIRS, NEW])
        qbd = sb("c_qbd", [P, PAIRS, P])
        knew = sb("c_knew", [P, PAIRS, NEW])
        negc = sb("c_negc", [HEADS, NEW])
        lf = sb("c_lf", [P, CT, HEADS])
        suffix = sb("c_suffix", [HEADS, CT, P])
        totals = sb("c_totals", [HEADS, CT])
        cum = sb("c_cum", [HEADS, CT + 1])
        pick = sb("c_pick", [HEADS, 2, P])
        spread = sb("c_spread", [NEW, P])
        kc = sb("c_kc", [P, 2, DG])
        kT = sb("c_kT", [P, 2, DG])
        v = sb("c_v", [P, CT + 1, DG])
        logit = sb("c_logit", [P, 2, KEYS])
        nmax = sb("c_nmax", [P, 2])
        total = sb("c_total", [P, 2])
        inv = sb("c_inv", [P, 2])
        pn = sb("c_pn", [P, 2, 2, P])
        pT = sb("c_pT", [P, 2, 2, P])
        zeros = sb("c_zeros", [P, NEW])

        small_loaded = sem("c_small_loaded")
        k_loaded = [sem(f"c_k_loaded{s}") for s in (0, 1)]
        v_loaded = sem("c_v_loaded")
        made = sem("c_made")
        ready = sem("c_ready")
        tails = sem("c_tails")
        tpe = Steps(sem("c_turn_pe_steps"), ["T"], ahead=2)
        kpe = Steps(sem("c_key_pe_steps"), ["s"], ahead=2)
        tact = Steps(sem("c_turn_act_steps"), ["T"], ahead=2)
        kact = Steps(sem("c_key_act_steps"), ["s"], ahead=2)
        turned = (bank[3], bank[7])
        final_pe = sem("c_final_pe")
        soft = sem("c_soft")
        exped = sem("c_exped")
        vtpe = Steps(sem("c_val_turn_pe_steps"), ["T"], ahead=2)
        vpe = Steps(sem("c_val_pe_steps"), ["o"], ahead=2)
        vdve = Steps(sem("c_val_dve_steps"), ["p0", "p1"])
        vact = Steps(sem("c_val_act_steps"), ["T"], ahead=2)
        turned_p = (bank[6], bank[0])

        block = ctx.enter_context(nc.Block())
        k_dram = io["cache_fox_k"][0, 0].rearrange("t h d -> t (h d)")
        v_dram = io["cache_fox_v"][0, 0].rearrange("t h d -> t (h d)")

        @block.sync
        def _(sp):
            at = NT * P
            with nc.allow_non_contiguous_dma(reason="32 queries, 8 gates"):
                sp.dma_start(q[:, :, :], io["qT"][:, :, at:at + NEW].rearrange("a p t -> p a t")).then_inc(small_loaded, 16)
                sp.dma_start(knew[:, :, :], io["kT"][:, :, at:at + NEW].rearrange("a p t -> p a t"))\
                  .then_inc(small_loaded, 16)
                sp.dma_start(negc[:, :], io["cT"][:, at:at + NEW]).then_inc(small_loaded, 16)
                sp.dma_start(lf[:, :, :], io["cache_fox_logf"][0, 0].rearrange("(n p) h -> p n h", p=P))\
                  .then_inc(small_loaded, 16)
            sp.dma_start(v[0:NEW, CT, :], io["s_v"]).then_inc(small_loaded, 16)
            with sp.Fori(0, CT // 2) as j:
                for s in (0, 1):
                    row = sp.snap(j * (-2 * P) + (CT - 1 - s) * P)
                    sp.wait_ge(*tpe.after("T", 2 * j + s - 2))
                    sp.dma_start(kc[:, s, :], k_dram[bass.ds(row, P), :]).then_inc(k_loaded[s], 16)
            sp.dma_start(v[:, 0:CT, :], v_dram.rearrange("(n p) c -> p n c", p=P)).then_inc(v_loaded, 16)

        @block.gpsimd
        def _(eng):
            eng.memset(qbd[:, :, :], 0.0).then_inc(made, 1)
            eng.memset(zeros[:, :], 0.0)
            eng.memset(cum[:, 0:1], 0.0)
            eng.memset(pick[:, :, :], 1.0)
            eng.memset(spread[:, :], 0.0).then_inc(made, 1)
            eng.wait_ge(made, 2)
            eng.affine_select(out=pick[:, :, :].rearrange("h g (a i) -> h g a i", i=NEW),
                              in_=pick[:, :, :].rearrange("h g (a i) -> h g a i", i=NEW),
                              compare_op=ALU.is_equal, fill=0.0, base=0,
                              pattern=[[-HG, 2], [-1, HG], [0, NEW]], channel_multiplier=1).then_inc(made, 1)
            eng.affine_select(out=spread[:, :].rearrange("t (a i) -> t a i", i=NEW),
                              in_=spread[:, :].rearrange("t (a i) -> t a i", i=NEW),
                              compare_op=ALU.not_equal, fill=1.0, base=0,
                              pattern=[[0, HG], [-1, NEW]], channel_multiplier=1).then_inc(made, 1)

        @block.tensor
        def _(eng):
            tpe.begin(eng)
            kpe.begin(eng)
            vtpe.begin(eng)
            vpe.begin(eng)
            ident = keep["ident"][:, :]
            eng.wait_ge(small_loaded, 80)
            eng.wait_ge(made, 4)
            for n in range(CT):
                b = bank[n // 4 % 2]
                if n >= 8 and n % 4 == 0:
                    eng.wait_ge(tails, n // 4 - 1)
                mm = eng.matmul(b[0:HEADS, (n % 4) * P:(n % 4 + 1) * P], lf[:, CT - 1 - n, :], keep["after"][:, :],
                                start=True, stop=True)
                mm = eng.matmul(bank[2][0:HEADS, n:n + 1], lf[:, CT - 1 - n, :], keep["ones"][:, 0:1],
                                start=True, stop=True)
                if n % 4 == 3:
                    mm.then_inc(final_pe, 1)
            eng.wait_ge(ready, 1)

            def turn(n, s, turn_no):
                eng.wait_ge(k_loaded[s], 16 * (turn_no + 1))
                if not (isinstance(n, int) and n < 2):
                    eng.wait_ge(*tact.after("T", n - 2))
                for a in range(PAIRS):
                    mm = eng.transpose(turned[s][:, a * P:(a + 1) * P], kc[:, s, a * P:(a + 1) * P], ident)
                mm.then_inc(*tpe.done("T"))

            def keys(n, s, past=True):
                if past:
                    eng.wait_ge(*tact.after("T", n))
                    eng.wait_ge(*kact.after("s", n - 1))
                w = P if past else NEW
                for g in (0, 1):
                    out = bank[4][:, g * P:g * P + w]
                    for i in (0, 1):
                        a = 2 * g + i
                        rhs = kT[:, s, a * P:(a + 1) * P] if past else knew[:, a, :]
                        eng.matmul(out, qbd[:, a, :], rhs, start=(i == 0), stop=False)
                    if past:
                        mm = eng.matmul(out, pick[:, g, :], suffix[:, bass.ds(n, 1), :].rearrange("h o t -> h (o t)"),
                                        start=False, stop=True)
                    else:
                        eng.matmul(out, pick[:, g, :], negc[:, :], start=False, stop=False)
                        mm = eng.matmul(out, spread[:, :], keep["causal"][0:NEW, 0:NEW], start=False, stop=True)
                if past:
                    mm.then_inc(*kpe.done("s"))
                else:
                    mm.then_inc(final_pe, 1)

            turn(0, 0, 0)
            with eng.Fori(0, CT // 2 - 1) as j:
                for s in (0, 1):
                    turn(2 * j + s + 1, 1 - s, j + s)
                    keys(2 * j + s, s)
            turn(CT - 1, 1, CT // 2 - 1)
            keys(CT - 2, 0)
            keys(CT - 1, 1)
            eng.wait_ge(*kact.after("s", CT - 1))
            keys(CT, 0, past=False)

            eng.matmul(bank[5][0:NEW, :], zeros[0:NEW, :], v[0:NEW, CT, :], start=True, stop=False)
            eng.wait_ge(v_loaded, 16)

            def turn_p(n, s, w=P):
                if not (isinstance(n, int) and n < 2):
                    eng.wait_ge(*vact.after("T", n - 2))
                eng.wait_ge(*vdve.after("p1", n))
                for g in (0, 1):
                    mm = eng.transpose(turned_p[s][0:w, g * P:(g + 1) * P], pn[:, s, g, 0:w], ident)
                mm.then_inc(*vtpe.done("T"))

            def values(n, s, stop, w=P):
                tile = CT - 1 - n if isinstance(n, int) else eng.snap(n * -1 + (CT - 1))
                eng.wait_ge(*vact.after("T", n))
                for h in range(HEADS):
                    g, i = divmod(h, HG)
                    r = v[0:w, CT, h * DH:(h + 1) * DH] if w < P else v[:, bass.ds(tile, 1), h * DH:(h + 1) * DH]\
                        .rearrange("p o c -> p (o c)")
                    mm = eng.matmul(bank[5][0:NEW, h * DH:(h + 1) * DH], pT[0:w, s, g, i * NEW:(i + 1) * NEW], r,
                                    start=False, stop=stop and h == HEADS - 1)
                mm.then_inc(*vpe.done("o"))

            turn_p(0, 0)
            with eng.Fori(0, CT // 2 - 1) as j:
                for s in (0, 1):
                    turn_p(2 * j + s + 1, 1 - s)
                    values(2 * j + s, s, False)
            turn_p(CT - 1, 1)
            values(CT - 2, 0, False)
            turn_p(CT, 0, NEW)
            values(CT - 1, 1, False)
            values(CT, 0, True, NEW)

        @block.scalar
        def _(eng):
            tact.begin(eng)
            kact.begin(eng)
            vact.begin(eng)

            def turned_keys(n, s):
                eng.wait_ge(*tpe.after("T", n))
                eng.wait_ge(*kpe.after("s", n - 2))
                eng.copy(kT[:, s, :], turned[s][:, :]).then_inc(*tact.done("T"))

            def keys(n, s):
                eng.wait_ge(*kpe.after("s", n))
                eng.copy(logit[:, :, bass.ds(n * P, P)], bank[4][:, 0:2 * P].rearrange("p (g t) -> p g t", g=2))\
                   .then_inc(*kact.done("s"))

            turned_keys(0, 0)
            with eng.Fori(0, CT // 2 - 1) as j:
                for s in (0, 1):
                    turned_keys(2 * j + s + 1, 1 - s)
                    keys(2 * j + s, s)
            turned_keys(CT - 1, 1)
            keys(CT - 2, 0)
            keys(CT - 1, 1)
            eng.wait_ge(final_pe, CT // 4 + 1)
            eng.copy(logit[:, :, PAST:KEYS], bank[4][:, 0:2 * P].rearrange("p (g t) -> p g t", g=2)[:, :, 0:NEW])\
               .then_inc(exped, 1)
            for g in (0, 1):
                eng.wait_ge(soft, g + 1)
                eng.activation(logit[:, g, :], logit[:, g, :], ACT.Exp, bias=nmax[:, g:g + 1],
                               accum_out=total[:, g:g + 1]).then_inc(exped, 1)

            def values(n, s, w=P):
                eng.wait_ge(*vtpe.after("T", n))
                eng.wait_ge(*vpe.after("o", n - 2))
                eng.copy(pT[0:w, s, :, :], turned_p[s][0:w, 0:2 * P].rearrange("p (g t) -> p g t", g=2))\
                   .then_inc(*vact.done("T"))

            with eng.Fori(0, CT // 2) as j:
                for s in (0, 1):
                    values(2 * j + s, s)
            values(CT, 0, NEW)

        @block.vector
        def _(eng):
            vdve.begin(eng)
            for c in range(CT // 4):
                eng.wait_ge(final_pe, c + 1)
                eng.tensor_copy(suffix[:, 4 * c:4 * c + 4, :],
                                bank[c % 2][0:HEADS, :].rearrange("h (n t) -> h n t", n=4)).then_inc(tails, 1)
            eng.tensor_copy(totals[:, :], bank[2][0:HEADS, 0:CT]).then_inc(tails, 1)
            eng.wait_ge(tails, CT // 4 + 1)
            eng.wait_ge(made, 4)
            eng.tensor_tensor_scan(out=cum[:, 1:CT + 1], data0=keep["ones"][0:HEADS, 0:CT], data1=totals[:, :],
                                   initial=0.0, op0=ALU.mult, op1=ALU.add).then_inc(tails, 1)
            eng.wait_ge(tails, CT // 4 + 2)
            eng.tensor_tensor(suffix[:, :, :], suffix[:, :, :], cum[:, 0:CT].unsqueeze(2).broadcast_to([HEADS, CT, P]),
                              ALU.add)
            eng.wait_ge(small_loaded, 80)
            for h in range(HEADS):
                a, e = divmod(h, 2)
                rows, i = slice(e * DH, (e + 1) * DH), h % HG
                ins = eng.tensor_copy(qbd[rows, a, i * NEW:(i + 1) * NEW], q[rows, a, :])
            ins.then_inc(ready, 1)
            eng.wait_ge(exped, 1)
            for g in (0, 1):
                eng.tensor_reduce(nmax[:, g:g + 1], logit[:, g, :], AX_X, ALU.max, negate=True).then_inc(soft, 1)
            eng.wait_ge(exped, 3)
            eng.reciprocal(inv[:, :], total[:, :]).then_inc(soft, 1)
            eng.wait_ge(soft, 3)

            def values(n, s, w=P):
                eng.wait_ge(*vtpe.after("T", n - 2))
                for g in (0, 1):
                    eng.tensor_scalar(pn[:, s, g, 0:w], logit[:, g, bass.ds(n * P, w)], inv[:, g:g + 1], None, ALU.mult)\
                       .then_inc(*vdve.done(f"p{g}"))

            with eng.Fori(0, CT // 2) as j:
                for s in (0, 1):
                    values(2 * j + s, s)
            values(CT, 0, NEW)
            eng.wait_ge(*vpe.after("o", CT))
            eng.tensor_copy(keep["fy"][0:NEW, NT, :], bank[5][0:NEW, :])
def normalise(eng, dve, held, act_after, z, stats, mv, std, t):
    for half in (0, 1):
        ins = eng.bn_stats(stats[:, half, :], z[:, half * 512:(half + 1) * 512])
    ins.then_inc(*dve.done("stats"))
    eng.wait_ge(*dve.after("stats", t))
    hold(eng, held)
    eng.bn_aggr(mv[:, 0:2], stats[:, :, :].rearrange("p a b -> p (a b)")).then_inc(*dve.done("mv"))
    eng.wait_ge(*dve.after("mv", t))
    eng.tensor_scalar(mv[:, 2:3], mv[:, 1:2], 1.0, LN_EPS, ALU.mult, ALU.add).then_inc(*dve.done("eps"))
    eng.wait_ge(*act_after)
    eng.reciprocal(mv[:, 3:4], std).then_inc(*dve.done("rstd"))
    eng.wait_ge(*dve.after("rstd", t))
    eng.tensor_scalar(z, z, mv[:, 0:1], mv[:, 3:4], ALU.subtract, ALU.mult).then_inc(*dve.done("norm"))


def mix(nc, io, keep):
    with ExitStack() as ctx:
        def sb(name, shape, dt=F32):
            return ctx.enter_context(nc.sbuf_tensor(name, shape, dt))

        def sem(name):
            return ctx.enter_context(nc.semaphore(name))

        FT = ctx.enter_context(nc.psum_tensor("m_FT", [P, 512], F32))
        M = [[ctx.enter_context(nc.psum_tensor(f"m_M{s}{b}", [P, 512], F32)) for b in range(2)] for s in range(2)]
        HT = [ctx.enter_context(nc.psum_tensor(f"m_HT{b}", [P, 512], F32)) for b in range(2)]
        SC = ctx.enter_context(nc.psum_tensor("m_SC", [P, 512], F32))
        w = keep["w_out"]
        rw = sb("m_rw", [P, KD, EXPERTS])
        gain, offset = sb("m_gain", [P, D]), sb("m_offset", [P, D])
        x = sb("m_x", [P, 2, D])
        ry = sb("m_ry", [P, 2, PAIRS, P])
        og = sb("m_og", [P, 2, DG])
        f = sb("m_f", [P, DG])
        fT = sb("m_fT", [P, PAIRS, P])
        z = sb("m_z", [P, D])
        stats, mv, std = sb("m_stats", [P, 2, 6]), sb("m_mv", [P, 4]), sb("m_std", [P, 1])
        h = sb("m_h", [P, 2, D])
        hT = sb("m_hT", [P, KD, P])

        weights_loaded = sem("m_weights_loaded")
        loaded = [sem(f"m_loaded{s}") for s in (0, 1)]
        stored = [sem(f"m_stored{s}") for s in (0, 1)]
        rest_zeroed, rows_padded = sem("m_rest_zeroed"), sem("m_rows_padded")
        held = sem("m_held")
        mpe = Steps(sem("m_product_pe_steps"), ["fT", "m"])
        mact = Steps(sem("m_product_act_steps"), ["fT"])
        mdve = Steps(sem("m_product_dve_steps"), ["f"])
        pe = Steps(sem("m_pe_steps"), ["hT0", "hT1", "score"])
        act = Steps(sem("m_act_steps"), ["std", "hT0", "hT1", "score"])
        dve = Steps(sem("m_dve_steps"), ["z0", "z1", "stats", "mv", "eps", "rstd", "norm", "gain", "out"])
        block = ctx.enter_context(nc.Block())

        def ahead_over_tiles(eng, product, tile):
            product(0, 0, 0)
            with eng.Fori(0, NT // 2) as j:
                for slot in (0, 1):
                    product(2 * j + slot + 1, 1 - slot, j + slot)
                    tile(2 * j + slot, slot, j)
            tile(NT, 0, NT // 2)

        @block.sync
        def _(sp):
            begin_stores(sp, stored)

            def loads(t, slot, x_src, rows=P):
                sp.dma_start(ry[:, slot, :, :], io["ryT"][:, :, bass.ds(t * P, P)].rearrange("a p t -> p a t"))\
                  .then_inc(loaded[slot], 16)
                sp.dma_start(og[:, slot, :], io["og"][bass.ds(t * P, P), :]).then_inc(loaded[slot], 16)
                sp.dma_start(x[0:rows, slot, :], x_src).then_inc(loaded[slot], 16)

            def store(t, slot):
                sp.wait_ge(*dve.after("out", t))
                sp.dma_start(io["h"][bass.ds(t * P, P), :], h[:, slot, :]).then_inc(stored[slot], 16)

            loads(0, 0, io["x_prompt"][0, 0:P, :])
            loads(1, 1, io["x_prompt"][0, P:2 * P, :])
            with nc.allow_non_contiguous_dma(reason="small rows for all partitions"):
                sp.dma_start(rw[:, :, :], io["router_w"].rearrange("(c p) n -> p c n", p=P)).then_inc(weights_loaded, 16)
                sp.dma_start(gain[:, :], io["ln1_g"].broadcast_to([P, D])).then_inc(weights_loaded, 16)
                sp.dma_start(offset[:, :], io["ln1_b"].broadcast_to([P, D])).then_inc(weights_loaded, 16)
            with sp.Fori(0, NT // 2 - 1) as j:
                for slot in (0, 1):
                    t = 2 * j + slot
                    sp.wait_ge(*dve.after("z1", t))
                    loads(t + 2, slot, io["x_prompt"][0, bass.ds((t + 2) * P, P), :])
                    store(t, slot)
            sp.wait_ge(rows_padded, 1)
            loads(NT, 0, io["x_sample"][0], NEW)
            store(NT - 2, 0)
            store(NT - 1, 1)
            store(NT, 0)
            sp.wait_ge(stored[0], 16 * (NT // 2 + 2))
            sp.wait_ge(stored[1], 16 * (NT // 2 + 1))

        @block.gpsimd
        def _(eng):
            eng.memset(keep["fy"][NEW:2 * NEW, NT, :], 0.0).then_inc(rest_zeroed, 1)
            eng.memset(keep["fy"][DH:P, NT, :], 0.0).then_inc(rest_zeroed, 1)
            eng.wait_ge(rest_zeroed, 2)
            eng.wait_ge(*dve.after("z1", NT - 2))
            eng.memset(x[:, 0, :], 0.0).then_inc(rows_padded, 1)

        @block.tensor
        def _(eng):
            mpe.begin(eng)
            pe.begin(eng)
            ident = keep["ident"][:, :]

            def product(t, slot, turn):
                eng.wait_ge(*mdve.after("f", t))
                eng.wait_ge(*mact.after("fT", t - 1))
                for a in range(PAIRS):
                    mm = eng.transpose(FT[:, a * P:(a + 1) * P], f[:, a * P:(a + 1) * P], ident)
                mm.then_inc(*mpe.done("fT"))
                if not (isinstance(t, int) and t == 0):
                    eng.wait_ge(*dve.after("z1", t - 2))
                for c in range(PAIRS):
                    for half in (0, 1):
                        eng.matmul(M[slot][half][:, :], ry[:, slot, c, :], w[:, c, half * 512:(half + 1) * 512],
                                   start=(c == 0), stop=False)
                eng.wait_ge(*mact.after("fT", t))
                for c in range(PAIRS):
                    for half in (0, 1):
                        mm = eng.matmul(M[slot][half][:, :], fT[:, c, :],
                                        w[:, PAIRS + c, half * 512:(half + 1) * 512], start=False, stop=(c == PAIRS - 1))
                mm.then_inc(*mpe.done("m"))

            def tile(t, slot, j):
                eng.wait_ge(*dve.after("out", t))
                for half in (0, 1):
                    eng.wait_ge(*act.after(f"hT{half}", t - 1))
                    for k in range(4):
                        c = 4 * half + k
                        mm = eng.transpose(HT[half][:, k * P:(k + 1) * P], h[:, slot, c * P:(c + 1) * P], ident)
                    mm.then_inc(*pe.done(f"hT{half}"))
                eng.wait_ge(*act.after("hT1", t))
                eng.wait_ge(*act.after("score", t - 1))
                for c in range(KD):
                    mm = eng.matmul(SC[:, 0:EXPERTS], hT[:, c, :], rw[:, c, :], start=(c == 0), stop=(c == KD - 1))
                mm.then_inc(*pe.done("score"))

            eng.wait_ge(keep["w_out_loaded"], 16)
            eng.wait_ge(weights_loaded, 48)
            ahead_over_tiles(eng, product, tile)

        @block.scalar
        def _(eng):
            mact.begin(eng)
            act.begin(eng)

            def product(t, slot, turn):
                eng.wait_ge(*mpe.after("fT", t))
                eng.wait_ge(*mpe.after("m", t - 1))
                eng.copy(fT[:, :, :], FT[:, :].rearrange("p (a t) -> p a t", a=PAIRS)).then_inc(*mact.done("fT"))

            def tile(t, slot, j):
                eng.wait_ge(*dve.after("eps", t))
                eng.activation(std[:, :], mv[:, 2:3], ACT.Sqrt).then_inc(*act.done("std"))
                for half in (0, 1):
                    eng.wait_ge(*pe.after(f"hT{half}", t))
                    eng.wait_ge(*pe.after("score", t - 1))
                    eng.copy(hT[:, 4 * half:4 * half + 4, :], HT[half][:, :].rearrange("p (a t) -> p a t", a=4))\
                       .then_inc(*act.done(f"hT{half}"))
                eng.wait_ge(*pe.after("score", t))
                eng.copy(keep["logits"][:, bass.ds(t, 1), :], SC[:, 0:EXPERTS].unsqueeze(1)).then_inc(*act.done("score"))

            ahead_over_tiles(eng, product, tile)

        @block.vector
        def _(eng):
            mdve.begin(eng)
            dve.begin(eng)
            eng.wait_ge(rest_zeroed, 2)

            def product(t, slot, turn):
                eng.wait_ge(loaded[slot], 48 * (turn + 1))
                eng.wait_ge(*mpe.after("fT", t - 1))
                eng.tensor_tensor(f[:, :].unsqueeze(1), keep["fy"][:, bass.ds(t, 1), :], og[:, slot, :].unsqueeze(1),
                                  ALU.mult).then_inc(*mdve.done("f"))

            def tile(t, slot, j):
                eng.wait_ge(*mpe.after("m", t))
                eng.wait_ge(*dve.after("out", t - 1))
                for half in (0, 1):
                    c = slice(half * 512, (half + 1) * 512)
                    eng.scalar_tensor_tensor(out=z[:, c], in0=x[:, slot, c], scalar=ALPHA, in1=M[slot][half][:, :],
                                             op0=ALU.mult, op1=ALU.add).then_inc(*dve.done(f"z{half}"))
                eng.wait_ge(*dve.after("z1", t))
                eng.wait_ge(stored[slot], 16 * (j + 1))
                eng.wait_ge(*pe.after("hT1", t - 1))
                normalise(eng, dve, held, act.after("std", t), z[:, :], stats, mv, std[:, :], t)
                eng.wait_ge(*dve.after("norm", t))
                eng.tensor_tensor(z[:, :], z[:, :], gain[:, :], ALU.mult).then_inc(*dve.done("gain"))
                eng.wait_ge(*dve.after("gain", t))
                eng.tensor_tensor(h[:, slot, :], z[:, :], offset[:, :], ALU.add).then_inc(*dve.done("out"))

            eng.wait_ge(weights_loaded, 48)
            ahead_over_tiles(eng, product, tile)


def route(nc, io, keep):
    with ExitStack() as ctx:
        def sb(name, shape, dt=F32):
            return ctx.enter_context(nc.sbuf_tensor(name, shape, dt))

        def sem(name):
            return ctx.enter_context(nc.semaphore(name))

        before = [ctx.enter_context(nc.psum_tensor(f"t_before{s}", [P, 512], F32)) for s in (0, 1)]
        total = [ctx.enter_context(nc.psum_tensor(f"t_total{s}", [P, 512], F32)) for s in (0, 1)]
        rb = sb("t_rb", [P, EXPERTS])
        score, sel, selm, gm, both, rank, base = (sb("t_" + n, [P, TILES, EXPERTS]) for n in (
            "score", "sel", "selm", "gm", "both", "rank", "base"))
        top = sb("t_top", [P, TILES, GROUPS, 8])
        gs, gbest, ebest = (sb("t_" + n, [P, TILES, 8]) for n in ("gs", "gbest", "ebest"))
        gidx, eidx = sb("t_gidx", [P, TILES, 8], U32), sb("t_eidx", [P, TILES, 8], U32)
        gid, gsum, ginv = (sb("t_" + n, [P, TILES]) for n in ("gid", "gsum", "ginv"))
        pick = sb("t_pick", [P, TILES, 2, EXPERTS])
        prod = sb("t_prod", [P, TILES, 2, EXPERTS])
        graw = sb("t_graw", [P, TILES, 2])
        bias_loaded, scored, padded, ranked = sem("t_bias_loaded"), sem("t_scored"), sem("t_padded"), sem("t_ranked")
        steps = sem("t_steps")
        chosen = sem("t_chosen")
        counted = sem("t_counted")
        picked = sem("t_picked")
        block = ctx.enter_context(nc.Block())

        @block.sync
        def _(sp):
            with nc.allow_non_contiguous_dma(reason="one row for all partitions"):
                sp.dma_start(rb[:, :], io["router_b"].unsqueeze(0).broadcast_to([P, EXPERTS])).then_inc(bias_loaded, 16)

        @block.gpsimd
        def _(eng):
            eng.memset(gs[:, :, :], FAR).then_inc(padded, 1)

        @block.scalar
        def _(eng):
            eng.activation(score[:, :, :], keep["logits"][:, :, :], ACT.Sigmoid).then_inc(scored, 1)

        @block.tensor
        def _(eng):
            eng.wait_ge(picked, 1)
            cols = NT * EXPERTS
            for s, (rows, tiles) in enumerate(((P, slice(0, NT)), (NEW, slice(NT, TILES)))):
                n = (tiles.stop - tiles.start) * EXPERTS
                rhs = both[0:rows, tiles, :].rearrange("p t e -> p (t e)")
                eng.matmul(before[s][:, 0:n], keep["before"][0:rows, :], rhs, start=True, stop=True)
                eng.matmul(total[s][:, 0:n], keep["ones"][0:rows, :], rhs, start=True, stop=True).then_inc(ranked, 1)

        @block.vector
        def _(eng):
            n = [0]

            def at(ins):
                n[0] += 1
                ins.then_inc(steps, 1)
                eng.wait_ge(steps, n[0])

            def over(ap, rest):
                return ap.unsqueeze(2).broadcast_to([P, TILES, rest])

            def row(ap):
                return ap.unsqueeze(1).broadcast_to([P, TILES, EXPERTS])

            def maxima(done, values, best, index):
                for t in range(TILES):
                    eng.max(out=best[:, t, :], in_=values[:, t, :]).then_inc(chosen, 1)
                eng.wait_ge(chosen, done + TILES)
                for t in range(TILES):
                    eng.max_index(out=index[:, t, :], in_max=best[:, t, :], in_values=values[:, t, :])\
                       .then_inc(chosen, 1)
                eng.wait_ge(chosen, done + 2 * TILES)

            eng.wait_ge(scored, 1)
            eng.wait_ge(bias_loaded, 16)
            at(eng.tensor_tensor(sel[:, :, :], score[:, :, :], row(rb[:, :]), ALU.add))
            for t in range(TILES):
                for g in range(GROUPS):
                    ins = eng.max(out=top[:, t, g, :], in_=sel[:, t, g * PER_GROUP:(g + 1) * PER_GROUP])
                ins.then_inc(chosen, 1)
            eng.wait_ge(chosen, TILES)
            eng.wait_ge(padded, 1)
            at(eng.tensor_tensor(gs[:, :, 0:GROUPS].unsqueeze(3), top[:, :, :, 0:1], top[:, :, :, 1:2], ALU.add))
            maxima(TILES, gs, gbest, gidx)
            at(eng.tensor_copy(gid[:, :], gidx[:, :, 0:1].rearrange("p t o -> p (t o)")))
            at(eng.tensor_tensor(gm[:, :, :], row(keep["group_of"][:, :]), over(gid[:, :], EXPERTS), ALU.is_equal))
            at(eng.tensor_scalar(selm[:, :, :], gm[:, :, :], -FAR, FAR, ALU.mult, ALU.add))
            at(eng.tensor_tensor(gm[:, :, :], gm[:, :, :], sel[:, :, :], ALU.mult))
            at(eng.tensor_tensor(selm[:, :, :], selm[:, :, :], gm[:, :, :], ALU.add))
            maxima(3 * TILES, selm, ebest, eidx)
            at(eng.tensor_copy(keep["expert"][:, :, :], eidx[:, :, 0:2]))
            for i in (0, 1):
                at(eng.tensor_tensor(pick[:, :, i, :], row(keep["expert_id"][:, :]),
                                     keep["expert"][:, :, i:i + 1].broadcast_to([P, TILES, EXPERTS]), ALU.is_equal))
            eng.tensor_tensor(both[:, :, :], pick[:, :, 0, :], pick[:, :, 1, :], ALU.add).then_inc(picked, 1)
            for i in (0, 1):
                at(eng.tensor_tensor(prod[:, :, i, :], pick[:, :, i, :], score[:, :, :], ALU.mult))
            at(eng.tensor_reduce(graw[:, :, :], prod[:, :, :, :], AX_X, ALU.add))
            at(eng.tensor_tensor(gsum[:, :].unsqueeze(2), graw[:, :, 0:1], graw[:, :, 1:2], ALU.add))
            at(eng.reciprocal(ginv[:, :], gsum[:, :]))
            at(eng.tensor_tensor(keep["gate"][:, :, :], graw[:, :, :], over(ginv[:, :], 2), ALU.mult))
            eng.wait_ge(ranked, 2)
            eng.memset(base[:, 0, :], 0.0).then_inc(counted, 1)
            for t in range(NT):
                eng.wait_ge(counted, t + 1)
                eng.tensor_tensor(base[:, t + 1, :], base[:, t, :], total[0][:, t * EXPERTS:(t + 1) * EXPERTS],
                                  ALU.add).then_inc(counted, 1)
            eng.wait_ge(counted, TILES)
            at(eng.tensor_tensor(keep["counts"][:, :], base[:, NT, :], total[1][:, 0:EXPERTS], ALU.add))
            at(eng.tensor_tensor(rank[:, 0:NT, :].rearrange("p t e -> p (t e)"), before[0][:, :],
                                 base[:, 0:NT, :].rearrange("p t e -> p (t e)"), ALU.add))
            at(eng.tensor_tensor(rank[:, NT, :], before[1][:, 0:EXPERTS], base[:, NT, :], ALU.add))
            for i in (0, 1):
                at(eng.tensor_tensor(prod[:, :, i, :], pick[:, :, i, :], rank[:, :, :], ALU.mult))
            at(eng.tensor_reduce(keep["rank"][:, :, :], prod[:, :, :, :], AX_X, ALU.add))


def dispatch(nc, io, keep):
    with ExitStack() as ctx:
        def sb(name, shape, dt=F32):
            return ctx.enter_context(nc.sbuf_tensor(name, shape, dt))

        def sem(name):
            return ctx.enter_context(nc.semaphore(name))

        frames = ctx.enter_context(nc.psum_tensor("d_frames", [P, 512], F32))
        ci = sb("d_ci", [P, EXPERTS], I32)
        nb = sb("d_nb", [P, EXPERTS])
        end, first = sb("d_end", [P, EXPERTS]), sb("d_first", [P, EXPERTS])
        N2 = 2 * TILES
        eq = sb("d_eq", [P, N2, EXPERTS])
        base = sb("d_base", [P, N2])
        part = sb("d_part", [P, 2, N2], I32)
        partf = sb("d_partf", [P, 2, N2])
        cmp = sb("d_cmp", [1, BLOCKS, EXPERTS])
        be, bf, fresh = (sb("d_" + n, [1, BLOCKS]) for n in ("be", "bf", "fresh"))
        count_i, count = sb("d_count_i", [P, P], I32), sb("d_count", [P, P])
        frame_i, frame = sb("d_frame_i", [P, N2], I32), sb("d_frame", [P, N2])
        in_block = sb("d_in_block", [P, N2, BLOCKS])
        in_row = sb("d_in_row", [P, N2, P])
        numbered, steps, marked, placed = sem("d_numbered"), sem("d_steps"), sem("d_marked"), sem("d_placed")
        block = ctx.enter_context(nc.Block())

        @block.vector
        def _(eng):
            n = [0]

            def at(ins):
                n[0] += 1
                ins.then_inc(steps, 1)
                eng.wait_ge(steps, n[0])

            at(eng.tensor_scalar(ci[:, :], keep["counts"][:, :], float(P - 1), None, ALU.add))
            at(eng.tensor_scalar(ci[:, :], ci[:, :], 7, None, ALU.arith_shift_right))
            at(eng.tensor_copy(nb[:, :], ci[:, :]))
            at(eng.tensor_tensor_scan(out=end[:, :], data0=keep["ones"][:, 0:EXPERTS], data1=nb[:, :], initial=0.0,
                                      op0=ALU.mult, op1=ALU.add))
            at(eng.tensor_tensor(first[:, :], end[:, :], nb[:, :], ALU.subtract))
            at(eng.tensor_tensor(eq[:, :, :], keep["expert_id"][:, :].unsqueeze(1).broadcast_to([P, N2, EXPERTS]),
                                 keep["expert"][:, :, :].rearrange("p n i -> p (n i)").unsqueeze(2)
                                 .broadcast_to([P, N2, EXPERTS]), ALU.is_equal))
            at(eng.tensor_tensor(eq[:, :, :], eq[:, :, :], first[:, :].unsqueeze(1).broadcast_to([P, N2, EXPERTS]),
                                 ALU.mult))
            at(eng.tensor_reduce(base[:, :], eq[:, :, :], AX_X, ALU.add))
            row = keep["row"][:, :, :].rearrange("p n i -> p (n i)")
            at(eng.scalar_tensor_tensor(out=row, in0=base[:, :], scalar=float(P),
                                        in1=keep["rank"][:, :, :].rearrange("p n i -> p (n i)"),
                                        op0=ALU.mult, op1=ALU.add))
            at(eng.tensor_scalar(part[:, 0, :], row, 7, None, ALU.arith_shift_right))
            at(eng.tensor_scalar(part[:, 1, :], row, P - 1, None, ALU.bitwise_and))
            at(eng.tensor_copy(partf[:, :, :], part[:, :, :]))
            eng.wait_ge(numbered, 2)
            at(eng.tensor_copy(count[:, :], count_i[:, :]))
            at(eng.tensor_copy(frame[:, :], frame_i[:, :]))
            at(eng.tensor_tensor(in_row[:, :, :], count[:, :].unsqueeze(1).broadcast_to([P, N2, P]),
                                 partf[:, 1, :].unsqueeze(2).broadcast_to([P, N2, P]), ALU.is_equal))
            at(eng.tensor_tensor(in_block[:, :, :], count[:, 0:BLOCKS].unsqueeze(1).broadcast_to([P, N2, BLOCKS]),
                                 partf[:, 0, :].unsqueeze(2).broadcast_to([P, N2, BLOCKS]), ALU.is_equal))
            eng.tensor_tensor(in_block[:, :, :], in_block[:, :, :], frame[:, :].unsqueeze(2)
                              .broadcast_to([P, N2, BLOCKS]), ALU.mult).then_inc(marked, 1)
            at(eng.tensor_tensor(cmp[:, :, :], end[0:1, :].unsqueeze(1).broadcast_to([1, BLOCKS, EXPERTS]),
                                 count[0:1, 0:BLOCKS].unsqueeze(2).broadcast_to([1, BLOCKS, EXPERTS]), ALU.is_le))
            at(eng.tensor_reduce(be[:, :], cmp[:, :, :], AX_X, ALU.add))
            at(eng.tensor_scalar(be[:, :], be[:, :], float(EXPERTS - 1), None, ALU.min))
            at(eng.tensor_copy(keep["block_expert"][:, :], be[:, :]))
            at(eng.memset(fresh[:, 0:1], 1.0))
            at(eng.tensor_tensor(fresh[:, 1:BLOCKS], be[:, 1:BLOCKS], be[:, 0:BLOCKS - 1], ALU.not_equal))
            at(eng.tensor_copy(keep["block_fresh"][:, :], fresh[:, :]))
            at(eng.tensor_tensor_scan(out=bf[:, :], data0=keep["ones"][0:1, 0:BLOCKS], data1=fresh[:, :], initial=0.0,
                                      op0=ALU.mult, op1=ALU.add))
            at(eng.tensor_copy(keep["block_place"][:, :], bf[:, :]))
            at(eng.tensor_scalar(keep["block_place"][:, :], keep["block_place"][:, :], 1, None, ALU.bitwise_and))
            eng.wait_ge(placed, 1)
            at(eng.tensor_copy(keep["frame_of"][:, :], frames[:, 0:BLOCKS]))

        @block.tensor
        def _(eng):
            eng.wait_ge(marked, 1)
            for n in range(N2):
                rows = P if n < 2 * NT else NEW
                mm = eng.matmul(frames[:, 0:BLOCKS], in_row[0:rows, n, :], in_block[0:rows, n, :],
                                start=(n == 0), stop=(n == N2 - 1))
            mm.then_inc(placed, 1)

        @block.gpsimd
        def _(eng):
            eng.iota(count_i[:, :], pattern=[[1, P]], base=0, channel_multiplier=0).then_inc(numbered, 1)
            eng.wait_ge(numbered, 1)
            eng.iota(frame_i[:, :], pattern=[[P, TILES], [0, 2]], base=0, channel_multiplier=1).then_inc(numbered, 1)


def experts(nc, io, keep):
    with ExitStack() as ctx:
        def sb(name, shape, dt=F32):
            return ctx.enter_context(nc.sbuf_tensor(name, shape, dt))

        def sem(name):
            return ctx.enter_context(nc.semaphore(name))

        KE = DE // P
        XT = [ctx.enter_context(nc.psum_tensor(f"e_XT{b}", [P, 512], F32)) for b in range(2)]
        H1 = ctx.enter_context(nc.psum_tensor("e_H1", [P, 512], F32))
        H3 = ctx.enter_context(nc.psum_tensor("e_H3", [P, 512], F32))
        GT = ctx.enter_context(nc.psum_tensor("e_GT", [P, 512], F32))
        Y = [ctx.enter_context(nc.psum_tensor(f"e_Y{b}", [P, 512], F32)) for b in range(2)]
        w1, w3 = sb("e_w1", [P, 2, KD, DE]), sb("e_w3", [P, 2, KD, DE])
        w2 = sb("e_w2", [P, 2, KE, D])
        idx = sb("e_idx", [P, 2], I32)
        x = sb("e_x", [P, 2, D])
        xT = sb("e_xT", [P, 2, KD, P])
        a = sb("e_a", [P, DE])
        g = sb("e_g", [P, DE])
        gT = sb("e_gT", [P, KE, P])
        y = sb("e_y", [P, 2, D])

        w1_loaded = [sem(f"e_w1_loaded{s}") for s in (0, 1)]
        w3_loaded = [sem(f"e_w3_loaded{s}") for s in (0, 1)]
        w2_loaded = [sem(f"e_w2_loaded{s}") for s in (0, 1)]
        pool = Steps(sem("e_pool_steps"), ["idx"])
        x_loaded = [sem(f"e_x_loaded{s}") for s in (0, 1)]
        stored = [sem(f"e_stored{s}") for s in (0, 1)]
        held, sp_held = sem("e_pool_held"), sem("e_sp_held")
        xpe = Steps(sem("e_x_pe_steps"), ["xT0", "xT1"], ahead=2)
        xact = Steps(sem("e_x_act_steps"), ["xT0"])
        xdve = Steps(sem("e_x_dve_steps"), ["xT1"])
        pe = Steps(sem("e_pe_steps"), ["h1", "h3", "gT", "y0", "y1"], ahead=2)
        act = Steps(sem("e_act_steps"), ["a", "y0"])
        dve = Steps(sem("e_dve_steps"), ["g", "gT", "y1"])
        block = ctx.enter_context(nc.Block())
        PAIRED = BLOCKS // 2
        assert BLOCKS % 2 == 0

        def over_blocks(eng, body):
            with eng.Fori(0, PAIRED) as j:
                for s in (0, 1):
                    body(2 * j + s, s, j)

        def over_blocks_ahead(eng, body):
            with eng.Fori(0, PAIRED - 1) as j:
                for s in (0, 1):
                    body(2 * j + s, s, j)
            body(BLOCKS - 2, 0, PAIRED - 1)
            body(BLOCKS - 1, 1, PAIRED - 1, following=False)

        @block.sync
        def _(sp):
            def body(b, s, j):
                e = sp.value_load(keep["block_expert"][0:1, bass.ds(b, 1)], min_val=0, max_val=EXPERTS - 1)
                place = sp.value_load(keep["block_place"][0:1, bass.ds(b, 1)], min_val=0, max_val=1)
                fresh = sp.value_load(keep["block_fresh"][0:1, bass.ds(b, 1)], min_val=0, max_val=1)
                sp.wait_ge(*pe.after("h3", b - 2))
                hold(sp, sp_held)
                for w, name, loaded in ((w1, "moe_w1", w1_loaded), (w3, "moe_w3", w3_loaded)):
                    sp.dma_start(w[:, bass.ds(place, 1), :, :],
                                 io[name][0, bass.ds(e, 1)].rearrange("o (p k) n -> p o k n", k=KD), cond=fresh)\
                      .then_inc(loaded[s], 16)
                sp.wait_ge(*pe.after("y1", b - 2))
                hold(sp, sp_held)
                sp.dma_start(w2[:, bass.ds(place, 1), :, :],
                             io["moe_w2"][0, bass.ds(e, 1)].rearrange("o (p k) n -> p o k n", k=KE), cond=fresh)\
                  .then_inc(w2_loaded[s], 16)

            over_blocks(sp, body)

        @block.gpsimd
        def _(eng):
            pool.begin(eng)

            def body(b, s, j):
                eng.wait_ge(*xpe.after("xT1", b - 2))
                hold(eng, held)
                eng.tensor_copy(idx[:, s:s + 1], keep["frame_of"][:, bass.ds(b, 1)]).then_inc(*pool.done("idx"))
                eng.wait_ge(*pool.after("idx", b))
                hold(eng, held)
                eng.indirect_dma_start(out=x[:, s, :], out_offset=None, in_=io["h"][:, :],
                                       in_offset=bass.IndirectOffsetOnAxis(ap=idx[:, s:s + 1], axis=0),
                                       bounds_check=ROWS - 1, oob_is_err=False).then_inc(x_loaded[s], 16)

            over_blocks(eng, body)

        @block.tensor
        def _(eng):
            xpe.begin(eng)
            pe.begin(eng)
            ident = keep["ident"][:, :]

            def turn_x(b, s, j):
                eng.wait_ge(x_loaded[s], 16 * (j + 1))
                for half in (0, 1):
                    eng.wait_ge(*(xdve.after("xT1", b - 1) if half else xact.after("xT0", b - 1)))
                    for k in range(4):
                        mm = eng.transpose(XT[half][:, k * P:(k + 1) * P], x[:, s, 4 * half + k:D:KD], ident)
                    mm.then_inc(*xpe.done(f"xT{half}"))

            def body(b, s, j, following=True):
                place = eng.value_load(keep["block_place"][0:1, bass.ds(b, 1)], min_val=0, max_val=1)
                eng.wait_ge(*xact.after("xT0", b))
                eng.wait_ge(*xdve.after("xT1", b))
                for name, w, loaded, out, free in (("h1", w1, w1_loaded, H1, act.after("a", b - 1)),
                                                   ("h3", w3, w3_loaded, H3, dve.after("g", b - 1))):
                    eng.wait_ge(loaded[s], 16 * (j + 1))
                    eng.wait_ge(*free)
                    for k in range(KD):
                        mm = eng.matmul(out[:, :], xT[:, s, k, :], w[:, bass.ds(place, 1), k, :], start=(k == 0), stop=(k == KD - 1))
                    mm.then_inc(*pe.done(name))
                if following:
                    turn_x(b + 1, 1 - s, j + s)
                eng.wait_ge(*dve.after("g", b))
                eng.wait_ge(*dve.after("gT", b - 1))
                for k in range(KE):
                    mm = eng.transpose(GT[:, k * P:(k + 1) * P], g[:, k:DE:KE], ident)
                mm.then_inc(*pe.done("gT"))
                eng.wait_ge(w2_loaded[s], 16 * (j + 1))
                eng.wait_ge(*dve.after("gT", b))
                for half in (0, 1):
                    eng.wait_ge(*(dve.after("y1", b - 1) if half else act.after("y0", b - 1)))
                    for k in range(KE):
                        mm = eng.matmul(Y[half][:, :], gT[:, k, :], w2[:, bass.ds(place, 1), k, half * 512:(half + 1) * 512],
                                        start=(k == 0), stop=(k == KE - 1))
                    mm.then_inc(*pe.done(f"y{half}"))

            turn_x(0, 0, 0)
            over_blocks_ahead(eng, body)

        @block.scalar
        def _(eng):
            act.begin(eng)
            xact.begin(eng)
            begin_stores(eng, stored)

            def copy_x(b, s):
                eng.wait_ge(*xpe.after("xT0", b))
                eng.wait_ge(*pe.after("h3", b - 1))
                eng.copy(xT[:, s, 0:4, :], XT[0][:, :].rearrange("p (k t) -> p k t", k=4)).then_inc(*xact.done("xT0"))

            def body(b, s, j, following=True):
                eng.wait_ge(*pe.after("h1", b))
                eng.wait_ge(*dve.after("g", b - 1))
                eng.activation(a[:, :], H1[:, :], ACT.Silu).then_inc(*act.done("a"))
                if following:
                    copy_x(b + 1, 1 - s)
                eng.wait_ge(*pe.after("y0", b))
                eng.wait_ge(stored[s], 16 * (j + 1))
                eng.copy(y[:, s, 0:512], Y[0][:, :]).then_inc(*act.done("y0"))
                eng.wait_ge(*act.after("y0", b))
                eng.wait_ge(*dve.after("y1", b))
                eng.dma_start(io["ypad"][bass.ds(b * P, P), :], y[:, s, :]).then_inc(stored[s], 16)

            copy_x(0, 0)
            over_blocks_ahead(eng, body)
            eng.wait_ge(stored[0], 16 * (PAIRED + 1))
            eng.wait_ge(stored[1], 16 * (PAIRED + 1))

        @block.vector
        def _(eng):
            dve.begin(eng)
            xdve.begin(eng)

            def copy_x(b, s):
                eng.wait_ge(*xpe.after("xT1", b))
                eng.wait_ge(*pe.after("h3", b - 1))
                eng.tensor_copy(xT[:, s, 4:8, :], XT[1][:, :].rearrange("p (k t) -> p k t", k=4))\
                   .then_inc(*xdve.done("xT1"))

            def body(b, s, j, following=True):
                eng.wait_ge(*act.after("a", b))
                eng.wait_ge(*pe.after("h3", b))
                eng.wait_ge(*pe.after("gT", b - 1))
                eng.tensor_tensor(g[:, :], a[:, :], H3[:, :], ALU.mult).then_inc(*dve.done("g"))
                if following:
                    copy_x(b + 1, 1 - s)
                eng.wait_ge(*pe.after("gT", b))
                eng.wait_ge(*pe.after("y1", b - 1))
                eng.tensor_copy(gT[:, :, :], GT[:, :].rearrange("p (k t) -> p k t", k=KE)).then_inc(*dve.done("gT"))
                eng.wait_ge(*pe.after("y1", b))
                eng.wait_ge(stored[s], 16 * (j + 1))
                eng.tensor_copy(y[:, s, 512:D], Y[1][:, :]).then_inc(*dve.done("y1"))

            copy_x(0, 0)
            over_blocks_ahead(eng, body)


def combine(nc, io, keep):
    with ExitStack() as ctx:
        def sb(name, shape, dt=F32):
            return ctx.enter_context(nc.sbuf_tensor(name, shape, dt))

        def sem(name):
            return ctx.enter_context(nc.semaphore(name))

        gain, offset = sb("z_gain", [P, D]), sb("z_offset", [P, D])
        h = sb("z_h", [P, 2, D])
        idx = sb("z_idx", [P, 2, 2], I32)
        y = sb("z_y", [P, 2, 2, D])
        z = sb("z_z", [P, 2, D])
        stats, mv, std = sb("z_stats", [P, 2, 6]), sb("z_mv", [P, 4]), sb("z_std", [P, 1])
        out = sb("z_out", [P, 2, D])
        weights_loaded = sem("z_weights_loaded")
        h_loaded = [sem(f"z_h_loaded{s}") for s in (0, 1)]
        y_loaded = [sem(f"z_y_loaded{s}") for s in (0, 1)]
        stored = [sem(f"z_stored{s}") for s in (0, 1)]
        held, pool_held = sem("z_held"), sem("z_pool_held")
        index = Steps(sem("z_index_steps"), ["idx"])
        pool = Steps(sem("z_pool_steps"), ["out"], ahead=2)
        act = Steps(sem("z_act_steps"), ["y0", "std"])
        dve = Steps(sem("z_dve_steps"), ["y1", "z", "stats", "mv", "eps", "rstd", "norm", "gain"], ahead=2)
        block = ctx.enter_context(nc.Block())

        @block.sync
        def _(sp):
            begin_stores(sp, stored)
            sp.dma_start(gain[:, :], io["ln2_g"].broadcast_to([P, D])).then_inc(weights_loaded, 16)
            sp.dma_start(offset[:, :], io["ln2_b"].broadcast_to([P, D])).then_inc(weights_loaded, 16)

            def load(t, s):
                sp.dma_start(h[:, s, :], io["h"][bass.ds(t * P, P), :]).then_inc(h_loaded[s], 16)

            def store(t, s, dst, rows=P):
                sp.wait_ge(*pool.after("out", t))
                sp.dma_start(dst, out[0:rows, s, :]).then_inc(stored[s], 16)

            load(0, 0)
            load(1, 1)
            with sp.Fori(0, NT // 2 - 1) as j:
                for s in (0, 1):
                    t = 2 * j + s
                    store(t, s, io["y_prompt"][0, bass.ds(t * P, P), :])
                    load(t + 2, s)
            store(NT - 2, 0, io["y_prompt"][0, (NT - 2) * P:(NT - 1) * P, :])
            load(NT, 0)
            store(NT - 1, 1, io["y_prompt"][0, (NT - 1) * P:NT * P, :])
            store(NT, 0, io["y_sample"][0], NEW)
            sp.wait_ge(stored[0], 16 * (NT // 2 + 2))
            sp.wait_ge(stored[1], 16 * (NT // 2 + 1))

        @block.gpsimd
        def _(eng):
            index.begin(eng)
            pool.begin(eng)

            def gather(t, s):
                rows = NEW if isinstance(t, int) and t == NT else P
                if not (isinstance(t, int) and t < 2):
                    eng.wait_ge(*dve.after("y1", t - 2))
                    hold(eng, pool_held)
                eng.tensor_copy(idx[:, s, :].unsqueeze(1), keep["row"][:, bass.ds(t, 1), :]).then_inc(*index.done("idx"))
                eng.wait_ge(*index.after("idx", t))
                hold(eng, pool_held)
                for i in (0, 1):
                    eng.indirect_dma_start(out=y[0:rows, s, i, :], out_offset=None, in_=io["ypad"][:, :],
                                           in_offset=bass.IndirectOffsetOnAxis(ap=idx[0:rows, s, i:i + 1], axis=0),
                                           bounds_check=BLOCKS * P - 1, oob_is_err=False).then_inc(y_loaded[s], 16)

            def finish(t, s, j):
                eng.wait_ge(*dve.after("gain", t))
                eng.wait_ge(stored[s], 16 * (j + 1))
                eng.tensor_tensor(out[:, s, :], z[:, s, :], offset[:, :], ALU.add).then_inc(*pool.done("out"))

            eng.wait_ge(weights_loaded, 32)
            gather(0, 0)
            gather(1, 1)
            with eng.Fori(0, NT // 2 - 1) as j:
                for s in (0, 1):
                    t = 2 * j + s
                    gather(t + 2, s)
                    finish(t, s, j)
            gather(NT, 0)
            for t in (NT - 2, NT - 1, NT):
                finish(t, t % 2, t // 2)

        @block.scalar
        def _(eng):
            act.begin(eng)

            def tile(t, s, j):
                eng.wait_ge(y_loaded[s], 32 * (j + 1))
                eng.wait_ge(*pool.after("out", t - 2))
                g0 = keep["gate"][:, bass.ds(t, 1), 0:1].rearrange("p o i -> p (o i)")
                eng.activation(z[:, s, :], y[:, s, 0, :], ACT.Identity, scale=g0).then_inc(*act.done("y0"))
                eng.wait_ge(*dve.after("eps", t))
                eng.activation(std[:, :], mv[:, 2:3], ACT.Sqrt).then_inc(*act.done("std"))

            over_tiles(eng, tile)

        @block.vector
        def _(eng):
            dve.begin(eng)
            eng.wait_ge(weights_loaded, 32)
            eng.wait_ge(weights_loaded, 32)

            def tile(t, s, j):
                g1 = keep["gate"][:, bass.ds(t, 1), 1:2].rearrange("p o i -> p (o i)")
                eng.wait_ge(y_loaded[s], 32 * (j + 1))
                eng.wait_ge(*act.after("y0", t))
                eng.scalar_tensor_tensor(out=z[:, s, :], in0=y[:, s, 1, :], scalar=g1, in1=z[:, s, :], op0=ALU.mult,
                                         op1=ALU.add).then_inc(*dve.done("y1"))
                eng.wait_ge(h_loaded[s], 16 * (j + 1))
                eng.wait_ge(*dve.after("y1", t))
                eng.scalar_tensor_tensor(out=z[:, s, :], in0=h[:, s, :], scalar=ALPHA, in1=z[:, s, :], op0=ALU.mult,
                                         op1=ALU.add).then_inc(*dve.done("z"))
                eng.wait_ge(*dve.after("z", t))
                normalise(eng, dve, held, act.after("std", t), z[:, s, :], stats, mv, std[:, :], t)
                eng.wait_ge(*dve.after("norm", t))
                eng.tensor_tensor(z[:, s, :], z[:, s, :], gain[:, :], ALU.mult).then_inc(*dve.done("gain"))

            over_tiles(eng, tile)


def build(nc, io):
    with ExitStack() as ctx:
        keep = constants(nc, ctx)
        for name in ("w_rwkv", "w_out"):
            keep[name + "_loaded"] = ctx.enter_context(nc.semaphore(name + "_loaded"))
        with ExitStack() as inner:
            keep["w_rwkv"] = inner.enter_context(nc.sbuf_tensor("w_rwkv", [P, KD, RCOLS], F32))
            fox_projection(nc, io, keep)
            rwkv(nc, io, keep)
        with ExitStack() as inner:
            keep["w_out"] = inner.enter_context(nc.sbuf_tensor("w_out_sb", [P, KD, D], F32))
            keep["fy"] = inner.enter_context(nc.sbuf_tensor("fy", [P, TILES, DG], F32))
            fox_prompt(nc, io, keep)
            fox_sample(nc, io, keep)
            mix(nc, io, keep)
        route(nc, io, keep)
        dispatch(nc, io, keep)
        experts(nc, io, keep)
        combine(nc, io, keep)


_INS = ['x_prompt', 'x_sample', 'cache_fox_k', 'cache_fox_v', 'cache_fox_logf', 'state_rwkv', 'state_rwkv_shift',
        'w_in', 'rwkv_mu', 'rwkv_w0', 'rwkv_w2', 'rwkv_a0', 'rwkv_a2', 'rwkv_g2', 'rwkv_k_k', 'rwkv_k_a', 'rwkv_r_k',
        'rwkv_lnx_w', 'rwkv_lnx_b', 'fox_b_f', 'fox_q_g', 'fox_k_g', 'w_out', 'ln1_g', 'ln1_b', 'ln2_g', 'ln2_b',
        'router_w', 'router_b', 'moe_w1', 'moe_w3', 'moe_w2']
_OUTS = [('y_prompt', (1, SEQ, D), (1, SEQ, D)), ('y_sample', (1, NEW, D), (1, NEW, D)),
         ('p_k', (SEQ, DG), (1, 1, SEQ, HEADS, DH)), ('p_v', (SEQ, DG), (1, 1, SEQ, HEADS, DH)),
         ('p_lf', (SEQ, HEADS), (1, 1, SEQ, HEADS)), ('p_rwkv', (HEADS, DH, DH), (1, 1, HEADS, DH, DH)),
         ('p_shift', (1, RCOLS), (1, 1, 1, RCOLS)),
         ('s_k', (NEW, DG), (1, 1, NEW, HEADS, DH)), ('s_v', (NEW, DG), (1, 1, NEW, HEADS, DH)),
         ('s_lf', (NEW, HEADS), (1, 1, NEW, HEADS)), ('s_rwkv', (HEADS, DH, DH), (1, 1, HEADS, DH, DH)),
         ('s_shift', (1, RCOLS), (1, 1, 1, RCOLS))]
_SCRATCH = [('qT', (PAIRS, P, ROWS), F32), ('kT', (PAIRS, P, ROWS), F32), ('cT', (HEADS, ROWS), F32),
            ('ryT', (PAIRS, P, ROWS), F32), ('og', (ROWS, DG), F32), ('h', (ROWS, D), F32),
            ('ypad', (BLOCKS * P, D), F32)]


def kernel(**inputs):
    import numpy as np
    import concourse.bacc as bacc
    from concourse.bass_utils import run_bass_kernel_spmd

    nc = bacc.Bacc("TRN2", target_bir_lowering=False, num_devices=1)
    arrays, io = {}, {}
    for name in _INS:
        a = np.ascontiguousarray(inputs[name])
        arrays[f"in_{name}"] = a
        io[name] = nc.dram_tensor(f"in_{name}", a.shape, mybir.dt.from_np(a.dtype), kind="ExternalInput").ap()
    for name, shape, _ in _OUTS:
        io[name] = nc.dram_tensor(f"out_{name}", shape, F32, kind="ExternalOutput").ap()
    for name, shape, dt in _SCRATCH:
        io[name] = nc.dram_tensor(f"scratch_{name}", shape, dt, kind="Internal").ap()
    build(nc, io)
    r = run_bass_kernel_spmd(nc, [arrays], core_ids=[0])
    return tuple(r.results[0][f"out_{name}"].reshape(shape) for name, _, shape in _OUTS)
```
